# Optimizing a Trainium2 kernel written in Bass

```python
import jax, jax.numpy as jnp
from jax import lax
import numpy as np
import math

D_MODEL = 1024
BATCH = 1
SEQ = 512
DEPTH = 1

CONV_CH = D_MODEL
CONV_WIDTH = 31
HEAD_DIM = 64
N_Q_HEADS = 16
N_KV_HEADS = 2
GROUP = N_Q_HEADS // N_KV_HEADS
ATTN_W = N_Q_HEADS * HEAD_DIM
KV_W = N_KV_HEADS * HEAD_DIM
WINDOW = 128
BLOCK = 128
ROPE_THETA = 10000.0
PEER_HEADS = 8
N_KEYS = 128
N_EXPERTS = N_KEYS * N_KEYS
PEER_DKEY = 256
PEER_DHALF = PEER_DKEY // 2
PEER_TOPK = 16
PEER_CHUNK = 128
IN_COLS = 2 * CONV_CH + ATTN_W + 2 * KV_W + 2 * D_MODEL
EPS = 1e-6
NEG = -1e30


def rmsnorm(x, g):
    xf = x.astype(jnp.float32)
    y = xf * lax.rsqrt(jnp.mean(xf * xf, axis=-1, keepdims=True) + EPS)
    return (y * g.astype(jnp.float32)).astype(x.dtype)

def layernorm(x, g, b):
    xf = x.astype(jnp.float32)
    mu = jnp.mean(xf, axis=-1, keepdims=True)
    xc = xf - mu
    y = xc * lax.rsqrt(jnp.mean(xc * xc, axis=-1, keepdims=True) + EPS)
    return (y * g.astype(jnp.float32) + b.astype(jnp.float32)).astype(x.dtype)

def rope(t, positions):
    half = HEAD_DIM // 2
    inv = ROPE_THETA ** (-(jnp.arange(half, dtype=jnp.float32) * 2.0 / HEAD_DIM))
    ang = positions.astype(jnp.float32)[..., None] * inv
    cos = jnp.cos(ang)[:, :, None, :]
    sin = jnp.sin(ang)[:, :, None, :]
    tf = t.astype(jnp.float32)
    t1, t2 = tf[..., :half], tf[..., half:]
    out = jnp.concatenate([t1 * cos - t2 * sin, t2 * cos + t1 * sin], axis=-1)
    return out.astype(t.dtype)

def conformer_conv(val, gate, conv_w, conv_b, ln_g, ln_b, w_conv_out):
    u = val * jax.nn.sigmoid(gate)
    up = jnp.pad(u, ((0, 0), (CONV_WIDTH - 1, 0), (0, 0)))
    y = lax.conv_general_dilated(
        up, conv_w[:, None, :], window_strides=(1,), padding="VALID",
        dimension_numbers=("NWC", "WIO", "NWC"), feature_group_count=CONV_CH) + conv_b
    y = jax.nn.silu(layernorm(y, ln_g, ln_b))
    return y @ w_conv_out

def swa_sink_attention(q, k, v, sinks):
    B, S = q.shape[0], q.shape[1]
    nb = S // BLOCK
    qb = q.reshape(B, nb, BLOCK, N_KV_HEADS, GROUP, HEAD_DIM)

    def band(t):
        tp = jnp.pad(t, ((0, 0), (BLOCK, 0), (0, 0), (0, 0)))
        tb = tp.reshape(B, nb + 1, BLOCK, N_KV_HEADS, HEAD_DIM)
        return jnp.concatenate([tb[:, :-1], tb[:, 1:]], axis=2)

    kb, vb = band(k), band(v)
    s = jnp.einsum("bnqhgd,bnkhd->bnhgqk", qb, kb,
                   preferred_element_type=jnp.float32) * (HEAD_DIM ** -0.5)
    qi = jnp.arange(BLOCK)[:, None]
    kj = jnp.arange(2 * BLOCK)[None, :]
    rel = qi + BLOCK - kj
    in_window = (rel >= 0) & (rel < WINDOW)
    not_pad = (kj >= BLOCK)[None] | (jnp.arange(nb)[:, None, None] > 0)
    mask = in_window[None] & not_pad
    s = jnp.where(mask[None, :, None, None], s, NEG)
    sk = sinks.astype(jnp.float32).reshape(N_KV_HEADS, GROUP)[:, :, None, None]
    m = jnp.maximum(jnp.max(s, axis=-1, keepdims=True), sk)
    e = jnp.exp(s - m)
    p = e / (jnp.sum(e, axis=-1, keepdims=True) + jnp.exp(sk - m))
    o = jnp.einsum("bnhgqk,bnkhd->bnqhgd", p.astype(v.dtype), vb)
    return o.reshape(B, S, ATTN_W)

def peer(h, w_pq, sub_keys, u_emb, v_emb):
    B, S, D = h.shape
    q = (h @ w_pq).reshape(B, S, PEER_HEADS, 2, PEER_DHALF)
    sc = jnp.einsum("bshcd,hcnd->bshcn", q, sub_keys,
                    preferred_element_type=jnp.float32)
    s_top, i_top = lax.top_k(sc, PEER_TOPK)
    cand = s_top[..., 0, :, None] + s_top[..., 1, None, :]
    cand_idx = i_top[..., 0, :, None] * N_KEYS + i_top[..., 1, None, :]
    cand = cand.reshape(B, S, PEER_HEADS, PEER_TOPK * PEER_TOPK)
    cand_idx = cand_idx.reshape(B, S, PEER_HEADS, PEER_TOPK * PEER_TOPK)
    best, pos = lax.top_k(cand, PEER_TOPK)
    expert_idx = jnp.take_along_axis(cand_idx, pos, axis=-1)
    gate = jax.nn.softmax(best, axis=-1).astype(h.dtype)

    n_chunks = (B * S) // PEER_CHUNK
    hc = h.reshape(n_chunks, PEER_CHUNK, D)
    ic = expert_idx.reshape(n_chunks, PEER_CHUNK, PEER_HEADS * PEER_TOPK)
    gc = gate.reshape(n_chunks, PEER_CHUNK, PEER_HEADS * PEER_TOPK)

    def chunk(args):
        hx, idx, g = args
        a = jax.nn.gelu(jnp.einsum("ced,cd->ce", u_emb[idx], hx), approximate=False)
        return jnp.einsum("ce,ced->cd", g * a, v_emb[idx])

    out = lax.map(chunk, (hc, ic, gc))
    return out.reshape(B, S, D)

def first_inputs(seed: int = 0) -> dict:
    key = jax.random.key(seed)
    ks = jax.random.split(key, 20)
    f32 = jnp.float32
    nrm = lambda k, shape, scale: jax.random.normal(k, shape, f32) * scale
    L = DEPTH
    return {
        "x": nrm(ks[0], (BATCH, SEQ, D_MODEL), 1.0),
        "positions": jnp.broadcast_to(jnp.arange(SEQ, dtype=jnp.int32)[None, :], (BATCH, SEQ)),
        "norm1_g": 1.0 + nrm(ks[1], (L, D_MODEL), 0.02),
        "w_in": nrm(ks[2], (L, D_MODEL, IN_COLS), D_MODEL ** -0.5),
        "b_in": nrm(ks[3], (L, IN_COLS), 0.01),
        "conv_w": nrm(ks[4], (L, CONV_WIDTH, CONV_CH), CONV_WIDTH ** -0.5),
        "conv_b": nrm(ks[5], (L, CONV_CH), 0.01),
        "conv_ln_g": 1.0 + nrm(ks[6], (L, CONV_CH), 0.02),
        "conv_ln_b": nrm(ks[7], (L, CONV_CH), 0.01),
        "w_conv_out": nrm(ks[8], (L, CONV_CH, D_MODEL), CONV_CH ** -0.5),
        "attn_sinks": nrm(ks[9], (L, N_Q_HEADS), 0.5),
        "w_attn_o": nrm(ks[10], (L, ATTN_W, D_MODEL), ATTN_W ** -0.5),
        "w_out": nrm(ks[11], (L, D_MODEL, D_MODEL), D_MODEL ** -0.5),
        "norm2_g": 1.0 + nrm(ks[12], (L, D_MODEL), 0.02),
        "w_peer_q": nrm(ks[13], (L, D_MODEL, PEER_HEADS * PEER_DKEY), D_MODEL ** -0.5),
        "peer_sub_keys": nrm(ks[14], (L, PEER_HEADS, 2, N_KEYS, PEER_DHALF), PEER_DHALF ** -0.5),
        "peer_u": nrm(ks[15], (L, N_EXPERTS, D_MODEL), D_MODEL ** -0.5),
        "peer_v": nrm(ks[16], (L, N_EXPERTS, D_MODEL), (PEER_HEADS * PEER_TOPK) ** -0.5),
        "final_g": 1.0 + nrm(ks[17], (D_MODEL,), 0.02),
    }

def first_block(x, positions, norm1_g, w_in, b_in, conv_w, conv_b, conv_ln_g, conv_ln_b,
              w_conv_out, attn_sinks, w_attn_o, w_out, norm2_g, w_peer_q, peer_sub_keys,
              peer_u, peer_v, final_g):
    B, S, _ = x.shape
    c0 = CONV_CH
    c1 = c0 + CONV_CH
    c2 = c1 + ATTN_W
    c3 = c2 + KV_W
    c4 = c3 + KV_W
    c5 = c4 + D_MODEL
    for l in range(DEPTH):
        h = rmsnorm(x, norm1_g[l])
        z = h @ w_in[l] + b_in[l]
        glu_val, glu_gate, q, k, v, g_conv, g_attn = jnp.split(z, [c0, c1, c2, c3, c4, c5], axis=-1)

        conv_out = conformer_conv(glu_val, glu_gate, conv_w[l], conv_b[l],
                                  conv_ln_g[l], conv_ln_b[l], w_conv_out[l])

        q = rope(q.reshape(B, S, N_Q_HEADS, HEAD_DIM), positions)
        k = rope(k.reshape(B, S, N_KV_HEADS, HEAD_DIM), positions)
        v = v.reshape(B, S, N_KV_HEADS, HEAD_DIM)
        attn_out = swa_sink_attention(q, k, v, attn_sinks[l]) @ w_attn_o[l]

        merged = jax.nn.sigmoid(g_conv) * conv_out + jax.nn.sigmoid(g_attn) * attn_out
        x = x + merged @ w_out[l]

        h2 = rmsnorm(x, norm2_g[l])
        x = x + peer(h2, w_peer_q[l], peer_sub_keys[l], peer_u[l], peer_v[l])
    return rmsnorm(x, final_g)


PLE_DIM = 256
D_FF = 2816
GLA_HEADS = 4
GLA_DK = 128
GLA_DV = 256
GLA_LOWRANK = 16
GLA_TAU = 16.0
GLA_CHUNK = 64
DSA_HEADS = 8
DSA_LATENT = 128
IDX_HEADS = 8
IDX_DIM = 64
TOPK_MAX = 256
Q_BLOCK = 128
REL_BUCKETS = 32
REL_MAX_DIST = 128

IN_SIZES = (
    GLA_HEADS * GLA_DK,
    GLA_HEADS * GLA_DK,
    GLA_HEADS * GLA_DV,
    GLA_HEADS * GLA_DV,
    GLA_LOWRANK,
    DSA_HEADS * DSA_LATENT,
    DSA_LATENT,
    IDX_HEADS * IDX_DIM,
    IDX_DIM,
    IDX_HEADS,
    2 * D_MODEL,
)
D_IN = sum(IN_SIZES)


def rms_norm(x, g):
    xf = x.astype(jnp.float32)
    y = xf * lax.rsqrt(jnp.mean(xf * xf, axis=-1, keepdims=True) + EPS)
    return (y * g.astype(jnp.float32)).astype(x.dtype)

def swiglu(x, w_in, w_out):
    gate, up = jnp.split(x @ w_in, 2, axis=-1)
    return (jax.nn.silu(gate) * up) @ w_out

def t5_bucket(dist):
    max_exact = REL_BUCKETS // 2
    d = jnp.maximum(dist, 0)
    ratio = jnp.maximum(d, 1).astype(jnp.float32) / max_exact
    large = max_exact + (jnp.log(ratio) / math.log(REL_MAX_DIST / max_exact)
                         * (REL_BUCKETS - max_exact)).astype(jnp.int32)
    large = jnp.minimum(large, REL_BUCKETS - 1)
    return jnp.where(d < max_exact, d, large)

def gla_chunked(q, k, v, log_a):
    B, H, S, dk = q.shape
    dv = v.shape[-1]
    C = GLA_CHUNK
    N = S // C

    def to_chunks(t):
        return jnp.moveaxis(t.reshape(B, H, N, C, t.shape[-1]), 2, 0)

    causal = jnp.tril(jnp.ones((C, C), dtype=bool))[:, :, None]

    def step(state, inp):
        qi, ki, vi, gi = inp
        b = jnp.cumsum(gi.astype(jnp.float32), axis=2)
        o_inter = jnp.einsum('bhtd,bhde->bhte', qi * jnp.exp(b), state)
        diff = b[:, :, :, None, :] - b[:, :, None, :, :]
        decay = jnp.exp(jnp.where(causal, diff, -jnp.inf))
        scores = jnp.einsum('bhtd,bhsd,bhtsd->bhts', qi, ki, decay)
        o_intra = jnp.einsum('bhts,bhse->bhte', scores, vi)
        b_last = b[:, :, -1:, :]
        k_dec = ki * jnp.exp(b_last - b)
        new_state = (jnp.exp(b_last[:, :, 0, :])[..., None] * state
                     + jnp.einsum('bhsd,bhse->bhde', k_dec, vi))
        return new_state, o_inter + o_intra

    state0 = jnp.zeros((B, H, dk, dv), jnp.float32)
    _, out = lax.scan(step, state0, (to_chunks(q), to_chunks(k), to_chunks(v), to_chunks(log_a)))
    return jnp.moveaxis(out, 0, 2).reshape(B, H, S, dv)

def dsa_attention(q, c_kv, q_idx, k_idx, w_idx, rel_bias):
    B, S, H, dc = q.shape
    top_k = min(TOPK_MAX, S // 4)
    nb = S // Q_BLOCK
    key_pos = jnp.arange(S, dtype=jnp.int32)
    bidx = jnp.arange(B)[:, None, None]

    def blocks(t):
        return jnp.moveaxis(t.reshape(B, nb, Q_BLOCK, *t.shape[2:]), 1, 0)

    def one_block(args):
        blk, qb, qib, wb = args
        q_pos = blk * Q_BLOCK + jnp.arange(Q_BLOCK, dtype=jnp.int32)
        dots = jnp.einsum('bthd,bsd->bths', qib, k_idx).astype(jnp.float32) * (IDX_DIM ** -0.5)
        w = wb.astype(jnp.float32) * (IDX_HEADS ** -0.5)
        score = jnp.einsum('bths,bth->bts', jax.nn.relu(dots), w)
        causal = key_pos[None, :] <= q_pos[:, None]
        score = jnp.where(causal[None], score, -jnp.inf)
        _, sel = lax.top_k(score, top_k)
        valid = sel <= q_pos[None, :, None]
        kv_sel = c_kv[bidx, sel]
        bias = rel_bias[t5_bucket(q_pos[None, :, None] - sel)]
        logits = (jnp.einsum('bthc,btkc->bthk', qb, kv_sel).astype(jnp.float32) * (dc ** -0.5)
                  + jnp.moveaxis(bias, -1, 2).astype(jnp.float32))
        logits = jnp.where(valid[:, :, None, :], logits, -jnp.inf)
        probs = jax.nn.softmax(logits, axis=-1)
        return jnp.einsum('bthk,btkc->bthc', probs.astype(kv_sel.dtype), kv_sel)

    out = lax.map(one_block, (jnp.arange(nb, dtype=jnp.int32), blocks(q), blocks(q_idx), blocks(w_idx)))
    return jnp.moveaxis(out, 0, 1).reshape(B, S, H, dc)

def hybrid_mixer(u, w_in, alpha_w, alpha_b, gla_norm_g, gla_w_out, ckv_g, dsa_w_out, rel_bias, w_out):
    B, S, _ = u.shape
    split_pts = np.cumsum(IN_SIZES)[:-1].tolist()
    (gq, gk, gv, gr, ga, dq, dkv, iq, ik, iw, gates) = jnp.split(u @ w_in, split_pts, axis=-1)

    def heads(t, n):
        return t.reshape(B, S, n, -1).transpose(0, 2, 1, 3)

    log_a = jax.nn.log_sigmoid((ga @ alpha_w + alpha_b).astype(jnp.float32)) / GLA_TAU
    o = gla_chunked(heads(gq, GLA_HEADS) * (GLA_DK ** -0.5), heads(gk, GLA_HEADS),
                    heads(gv, GLA_HEADS), heads(log_a, GLA_HEADS))
    o = rms_norm(o, gla_norm_g.reshape(GLA_HEADS, 1, GLA_DV)).astype(u.dtype)
    o = o.transpose(0, 2, 1, 3).reshape(B, S, GLA_HEADS * GLA_DV) * jax.nn.silu(gr)
    y_gla = o @ gla_w_out

    c_kv = rms_norm(dkv, ckv_g)
    od = dsa_attention(dq.reshape(B, S, DSA_HEADS, DSA_LATENT), c_kv,
                       iq.reshape(B, S, IDX_HEADS, IDX_DIM), ik, iw, rel_bias)
    y_dsa = od.reshape(B, S, DSA_HEADS * DSA_LATENT) @ dsa_w_out

    g_gla, g_dsa = jnp.split(jax.nn.sigmoid(gates), 2, axis=-1)
    return (g_gla * y_gla + g_dsa * y_dsa) @ w_out

def second_inputs(seed: int = 0) -> dict:
    key = jax.random.key(seed)
    ks = jax.random.split(key, 24)
    L, D, F = DEPTH, D_MODEL, D_FF

    def dense(k, shape, fan_in):
        return jax.random.normal(k, shape, jnp.float32) * (fan_in ** -0.5)

    def gain(k, shape):
        return 1.0 + 0.05 * jax.random.normal(k, shape, jnp.float32)

    return {
        "x": jax.random.normal(ks[0], (BATCH, SEQ, D), jnp.float32),
        "p": jax.random.normal(ks[1], (DEPTH, BATCH, SEQ, PLE_DIM), jnp.float32),
        "ffn1_norm": gain(ks[2], (L, D)),
        "ffn1_w_in": dense(ks[3], (L, D, 2 * F), D),
        "ffn1_w_out": dense(ks[4], (L, F, D), F),
        "mix_norm": gain(ks[5], (L, D)),
        "mix_w_in": dense(ks[6], (L, D, D_IN), D),
        "gla_alpha_w": dense(ks[7], (L, GLA_LOWRANK, GLA_HEADS * GLA_DK), GLA_LOWRANK),
        "gla_alpha_b": 0.1 * jax.random.normal(ks[8], (L, GLA_HEADS * GLA_DK), jnp.float32),
        "gla_out_norm": gain(ks[9], (L, GLA_HEADS * GLA_DV)),
        "gla_w_out": dense(ks[10], (L, GLA_HEADS * GLA_DV, D), GLA_HEADS * GLA_DV),
        "ckv_norm": gain(ks[11], (L, DSA_LATENT)),
        "dsa_w_out": dense(ks[12], (L, DSA_HEADS * DSA_LATENT, D), DSA_HEADS * DSA_LATENT),
        "rel_bias": 0.5 * jax.random.normal(ks[13], (REL_BUCKETS, DSA_HEADS), jnp.float32),
        "mix_w_out": dense(ks[14], (L, D, D), D),
        "ffn2_norm": gain(ks[15], (L, D)),
        "ffn2_w_in": dense(ks[16], (L, D, 2 * F), D),
        "ffn2_w_out": dense(ks[17], (L, F, D), F),
        "ple_norm": gain(ks[18], (L, D)),
        "ple_w_gate": dense(ks[19], (L, D, D), D),
        "ple_w_proj": dense(ks[20], (L, PLE_DIM, D), PLE_DIM),
        "final_norm": gain(ks[21], (D,)),
    }

def second_block(x, p, ffn1_norm, ffn1_w_in, ffn1_w_out, mix_norm, mix_w_in, gla_alpha_w, gla_alpha_b,
              gla_out_norm, gla_w_out, ckv_norm, dsa_w_out, rel_bias, mix_w_out, ffn2_norm, ffn2_w_in,
              ffn2_w_out, ple_norm, ple_w_gate, ple_w_proj, final_norm):
    h = x
    for i in range(DEPTH):
        h = h + 0.5 * swiglu(rms_norm(h, ffn1_norm[i]), ffn1_w_in[i], ffn1_w_out[i])
        h = h + hybrid_mixer(rms_norm(h, mix_norm[i]), mix_w_in[i], gla_alpha_w[i], gla_alpha_b[i],
                             gla_out_norm[i], gla_w_out[i], ckv_norm[i], dsa_w_out[i], rel_bias,
                             mix_w_out[i])
        h = h + 0.5 * swiglu(rms_norm(h, ffn2_norm[i]), ffn2_w_in[i], ffn2_w_out[i])
        hn = rms_norm(h, ple_norm[i])
        h = h + jax.nn.sigmoid(hn @ ple_w_gate[i]) * (p[i] @ ple_w_proj[i])
    return rms_norm(h, final_norm)


def setup_inputs(seed=0):
    out = dict(first_inputs(seed))
    for name, value in second_inputs(seed + 1).items():
        if name != "x":
            out[name + "_2"] = value
    return out


def reference(
    x, positions, norm1_g, w_in, b_in, conv_w, conv_b, conv_ln_g, conv_ln_b, w_conv_out,
    attn_sinks, w_attn_o, w_out, norm2_g, w_peer_q, peer_sub_keys, peer_u, peer_v, final_g, p_2,
    ffn1_norm_2, ffn1_w_in_2, ffn1_w_out_2, mix_norm_2, mix_w_in_2, gla_alpha_w_2,
    gla_alpha_b_2, gla_out_norm_2, gla_w_out_2, ckv_norm_2, dsa_w_out_2, rel_bias_2,
    mix_w_out_2, ffn2_norm_2, ffn2_w_in_2, ffn2_w_out_2, ple_norm_2, ple_w_gate_2, ple_w_proj_2,
    final_norm_2,
):
    x = first_block(
        x, positions, norm1_g, w_in, b_in, conv_w, conv_b, conv_ln_g, conv_ln_b, w_conv_out,
        attn_sinks, w_attn_o, w_out, norm2_g, w_peer_q, peer_sub_keys, peer_u, peer_v, final_g,
    )
    return second_block(
        x, p_2, ffn1_norm_2, ffn1_w_in_2, ffn1_w_out_2, mix_norm_2, mix_w_in_2, gla_alpha_w_2,
        gla_alpha_b_2, gla_out_norm_2, gla_w_out_2, ckv_norm_2, dsa_w_out_2, rel_bias_2,
        mix_w_out_2, ffn2_norm_2, ffn2_w_in_2, ffn2_w_out_2, ple_norm_2, ple_w_gate_2,
        ple_w_proj_2, final_norm_2,
    )


_drawn_inputs = setup_inputs


def setup_inputs(seed=0):
    import zlib

    import numpy as np

    out = dict(_drawn_inputs(seed))
    spreads = {}
    factors = {'norm1_g': 4.358,
     'b_in': 5.183,
     'conv_b': 5.337,
     'conv_ln_g': 4.688,
     'conv_ln_b': 8.0,
     'attn_sinks': 8.0,
     'norm2_g': 5.932,
     'gla_alpha_b_2': 4.569,
     'gla_out_norm_2': 3.973,
     'ckv_norm_2': 6.699,
     'ffn2_norm_2': 3.331,
     'ple_norm_2': 6.674}
    for name, (base, spread) in spreads.items():
        noise = np.random.default_rng([zlib.crc32(name.encode()), seed]).standard_normal(out[name].shape)
        drawn = base * np.exp(spread * noise) if base else spread * noise
        out[name] = __import__('jax').numpy.asarray(drawn.astype(out[name].dtype))
    for name, factor in factors.items():
        out[name] = (out[name] * factor).astype(out[name].dtype)
    return out
```

```python
from contextlib import ExitStack

import numpy as np
import concourse.bass as bass
from concourse import mybir

F32 = mybir.dt.float32
BF16 = mybir.dt.bfloat16
I32 = mybir.dt.int32
U32 = mybir.dt.uint32
ALU = mybir.AluOpType
ACT = mybir.ActivationFunctionType
AX = mybir.AxisListType

P = 128
S = 512
D = 1024
KT = D // P
NB = S // P
TAPS = 31
HEADS, HD = 16, 64
PH, NKEY, TOPK = 8, 128, 16
NQ = 4
JQ = NKEY // NQ
FT = 2816 // P
GH, GDV = 4, 256
DH = 8
SEL = 128
EPS = 1e-6
NEG = -1e30
TAKEN = -3e38
RING = 4
TWO_PI = 6.283185307179586
MAGIC = 12582912.0

STREAM = [
    ("glu", 16), ("q", 8), ("kv", 3), ("gates", 16), ("attn_o", 8), ("conv_out", 8), ("w_out", 8),
    ("peer_q_u0", 48), ("u1", 32), ("v0", 32), ("u2", 32), ("v1", 32), ("u3", 32),
    ("v2", 32), ("v3", 32),
    ("f1_in", 44), ("f1_out", 22),
    ("misc", 1), ("ik", 1), ("iq", 4), ("dkv", 1), ("gqk", 8), ("gv", 8), ("wide2", 32),
    ("gla_out", 8), ("dsa_out", 8), ("mix_out", 8),
    ("f2_in", 44), ("f2_out", 22), ("ple_proj", 2), ("ple_gate", 8),
]
START = {}
SLOTS = 0
for _name, _k in STREAM:
    START[_name] = SLOTS
    SLOTS += _k

COLS = [
    ("norm1", 8), ("b_glu", 16), ("b_q", 8), ("b_k", 2), ("b_gates", 16), ("conv_w", 8 * TAPS),
    ("conv_b", 8), ("ln_g", 8), ("ln_b", 8), ("norm2", 8), ("final1", 8), ("ffn1_n", 8),
    ("mix_n", 8), ("alpha_b", 4), ("gla_n", 8), ("ckv_n", 1), ("ffn2_n", 8), ("ple_n", 8),
    ("final2", 8), ("inv_freq", 1), ("eps", 1), ("half_pi", 1), ("one", 1), ("zero", 1),
]
COL = {}
_n = 0
for _name, _k in COLS:
    COL[_name] = _n
    _n += _k
NCOLS = _n
SQ = {"ident": 0, "mean": 128, "rot": 256, "iota": 384}
MAXD = 639


class Signal:

    def __init__(self, nc, ctx, name):
        self.sem = ctx.enter_context(nc.semaphore(name))
        self.n = 0
        self.first = 1

    def by_dma(self):
        self.first = 0
        return self

    def plan(self, k):
        base = self.n
        self.n += k
        return base

    def wait(self, e, value):
        e.wait_ge(self.sem, value + self.first)


def build(nc, a, out, stop=99, start=0):
    ctx = ExitStack()
    queues = {"pe": [], "act": [], "dve": [], "pool": [], "sp": []}

    def on(engine):
        def put(f):
            queues[engine].append(f)
            return f
        return put

    def sb(c, name, shape, dt=F32):
        return c.enter_context(nc.sbuf_tensor(name, shape, dt))

    total = {1: START["peer_q_u0"], 2: START["f1_in"], 3: START["misc"], 4: START["f2_in"],
             5: START["ple_proj"]}.get(stop, SLOTS)
    signals = {}

    def sig(name):
        if name not in signals:
            signals[name] = Signal(nc, ctx, "s_" + name)
        return signals[name]

    def tile(T, t):
        if isinstance(t, int):
            return T[:, t, :]
        return T[:, bass.ds(t, 1), :].rearrange("p a s -> p (a s)")

    def col(T, c):
        return T[:, c:c + 1] if isinstance(c, int) else T[:, bass.ds(c, 1)]

    def view(ap, *dims):
        return bass.AP(tensor=ap.tensor, offset=ap.offset, ap=[ap.ap[0], *[list(d) for d in dims]])

    X = sb(ctx, "x_res", [P, KT, S])
    H = sb(ctx, "h_norm", [P, KT, S])
    ring = sb(ctx, "ring", [P, RING, D])
    cst = sb(ctx, "cst", [P, NCOLS])
    sq = sb(ctx, "squares_const", [P, 512])
    norm_sq = sb(ctx, "norm_sq", [P, 2, S])
    norm_r = sb(ctx, "norm_r", [P, S])
    PS = ctx.enter_context(nc.psum_tensor("ps", [P, 8, 512], F32))
    ident = sq[:, SQ["ident"]:SQ["ident"] + P]
    mean = sq[:, SQ["mean"]:SQ["mean"] + P]
    rot = sq[:, SQ["rot"]:SQ["rot"] + P]
    iota = sq[:, SQ["iota"]:SQ["iota"] + P]

    def c_(name, i=0):
        return cst[:, COL[name] + i:COL[name] + i + 1]

    def cd(name, i):
        return col(cst, i + COL[name])

    arrive = [ctx.enter_context(nc.semaphore(f"s_slot{r}")) for r in range(RING)]
    slot_done = sig("slot_done")
    s_const = sig("const").by_dma()
    evac_act = sig("evac_act")
    evac_dve = sig("evac_dve")
    phase = sig("phase")

    on("act")(lambda e: e.sem_inc(evac_act.sem, 4))
    on("dve")(lambda e: e.sem_inc(evac_dve.sem, 4))
    evac_act.n = evac_dve.n = 4
    glu_gate = sig("glu_gate")
    glu_done = sig("glu_done")
    on("dve")(lambda e: e.sem_inc(glu_done.sem, 2))
    glu_done.n = 2
    slot_done.n = 0

    @on("sp")
    def _(e):
        e.dma_start(cst[:, :], a["cols"]).then_inc(s_const.sem, 16)
        e.dma_start(X[:, :, :], a["xT"].rearrange("(k p) s -> p k s", p=P)).then_inc(s_const.sem, 16)
        e.dma_start(sq[:, :], a["squares"]).then_inc(s_const.sem, 16)
        for r in range(RING):
            e.dma_start(ring[:, r, :], a["stream"][r]).then_inc(arrive[r], 16)
        with e.Fori(1, total // RING) as i:
            for r in range(RING):
                slot_done.wait(e, (i - 1) * RING + r + 1)
                e.dma_start(ring[:, r, :], a["stream"][i * RING + r]).then_inc(arrive[r], 16)
        for n in range(total // RING * RING, total):
            slot_done.wait(e, n - RING + 1)
            e.dma_start(ring[:, n % RING, :], a["stream"][n]).then_inc(arrive[n % RING], 16)
    CONST_IN = 48

    s_held = sig("held")

    def held(e):
        e.sem_inc(s_held.sem, 1)

    def skip_constants():
        for name in ("pe", "act", "dve", "pool"):
            on(name)(lambda e: s_const.wait(e, CONST_IN))

    def barrier():
        phase.plan(4)
        want = phase.n
        for name in ("pe", "act", "dve", "pool"):
            def f(e):
                e.drain().then_inc(phase.sem, 1)
                phase.wait(e, want)
            on(name)(f)

    def use_slot(e, n0, i, per, r):
        n = n0 + r
        e.wait_ge(arrive[n % RING], i * (16 * per // RING) + 16 * (n // RING + 1))
        return ring[:, n % RING, :]

    def tiles_of(slot):
        return slot.rearrange("p (k c) -> p k c", k=KT)

    def pe_gemm(name, n, rhs, first_wait=None, free=evac_act, banks=(0, 1, 2, 3)):
        n0 = START[name]
        fbase = free.n
        others = [(s, s.n) for s in (evac_act, evac_dve, glu_done)]

        def one(e, i, r):
            w = tiles_of(use_slot(e, n0, i, 4, r))
            free.wait(e, i * 4 + (fbase + r - 3))
            for k in range(KT):
                if first_wait and isinstance(i, int) and i == 0 and r == 0:
                    first_wait[0].wait(e, first_wait[1] + k + 1)
                m = e.matmul(PS[:, banks[r], :], w[:, k, :], rhs(k), start=k == 0, stop=k == KT - 1)
            m.then_inc(slot_done.sem, 1)

        @on("pe")
        def _(e):
            for s, v in others:
                s.wait(e, v)
            for r in range(min(4, n)):
                one(e, 0, r)
            if n >= 8:
                with e.Fori(1, n // 4) as i:
                    for r in range(4):
                        one(e, i, r)
        return n0

    def evacuate(engine, name, n, op, done, before=None, banks=(0, 1, 2, 3)):
        n0 = START[name]
        done.plan(n)

        @on(engine)
        def _(e):
            if before:
                before(e)

            def one(i, r):
                slot_done.wait(e, i * 4 + (n0 + r + 1))
                op(e, i * 4 + r, PS[:, banks[r], :]).then_inc(done.sem, 1)
            if n < 8:
                for r in range(n):
                    one(0, r)
            else:
                with e.Fori(0, n // 4) as i:
                    for r in range(4):
                        one(i, r)

    s_sq, s_sqmm, s_root, s_h = sig("norm_sq"), sig("norm_mm"), sig("norm_root"), sig("norm_h")
    s_inv = sig("norm_inv")

    def rms_norm(gain, dst=H, bank=7, ready=None):
        b_sq, b_mm, b_root, b_h, b_inv = (s_sq.plan(KT), s_sqmm.plan(KT), s_root.plan(1),
                                          s_h.plan(KT), s_inv.plan(1))

        @on("act")
        def _(e):
            for k in range(KT):
                if ready:
                    ready[0].wait(e, ready[1] + k + 1)
                if k >= 2:
                    s_sqmm.wait(e, b_mm + k - 1)
                elif b_mm:
                    s_sqmm.wait(e, b_mm)
                e.activation(norm_sq[:, k % 2, :], X[:, k, :], ACT.Square).then_inc(s_sq.sem, 1)
            s_sqmm.wait(e, b_mm + KT)
            if b_h:
                s_h.wait(e, b_h)
            e.activation(norm_r[:, :], PS[:, bank, :], ACT.Sqrt, bias=c_("eps")).then_inc(s_root.sem, 1)

        @on("pe")
        def _(e):
            for k in range(KT):
                s_sq.wait(e, b_sq + k + 1)
                e.matmul(PS[:, bank, :], mean, norm_sq[:, k % 2, :], start=k == 0,
                         stop=k == KT - 1).then_inc(s_sqmm.sem, 1)

        @on("dve")
        def _(e):
            s_root.wait(e, b_root + 1)
            e.reciprocal(norm_r[:, :], norm_r[:, :]).then_inc(s_inv.sem, 1)
            s_inv.wait(e, b_inv + 1)
            for k in range(KT):
                e.scalar_tensor_tensor(out=dst[:, k, :], in0=X[:, k, :], scalar=c_(gain, k),
                                       in1=norm_r[:, :], op0=ALU.mult, op1=ALU.mult).then_inc(s_h.sem, 1)
        return b_h

    def finish(last=None):
        s_out = sig("out").by_dma()
        want = s_h.n if last is None else last

        @on("sp")
        def _(e):
            if last is None:
                s_h.wait(e, want)
                src = H
            else:
                phase.wait(e, want)
                src = X
            e.dma_start(out.rearrange("(k p) s -> p k s", p=P), src[:, :, :]).then_inc(s_out.sem, 16)
            s_out.wait(e, 16)
        go = ctx.enter_context(nc.semaphore("s_go"))
        seeded = [x.sem for x in signals.values() if x.first]
        queues["pool"].insert(0, lambda e: [e.sem_inc(x, 1) for x in seeded + [go]])
        for name in ("pe", "act", "dve"):
            queues[name].insert(0, lambda e: e.wait_ge(go, 1))
        with nc.Block() as block:
            for name, deco in (("sp", block.sync), ("pe", block.tensor), ("act", block.scalar),
                               ("dve", block.vector), ("pool", block.gpsimd)):
                def program(e, name=name):
                    for f in queues[name]:
                        f(e)
                deco(program)
        ctx.close()


    def glu(name, pairs, tmp, act, func, value, first_wait):
        n0 = START[name]
        others = [(s, s.n) for s in (evac_act, evac_dve, glu_done)]
        b_gate, b_done = glu_gate.plan(pairs), glu_done.plan(pairs)

        def loop(e, one):
            for r in range(2):
                one(e, 0, r)
            with e.Fori(1, pairs // 2) as i:
                for r in range(2):
                    one(e, i, r)

        @on("pe")
        def _(e):
            for s, v in others:
                s.wait(e, v)

            def one(e, i, r):
                for j in range(2):
                    w = tiles_of(use_slot(e, n0, i, 4, 2 * r + j))
                    glu_done.wait(e, i * 2 + (b_done + r - 1))
                    for k in range(KT):
                        if isinstance(i, int) and r == 0 and j == 0:
                            first_wait[0].wait(e, first_wait[1] + k + 1)
                        m = e.matmul(PS[:, 2 * r + j, :], w[:, k, :], H[:, k, :], start=k == 0,
                                     stop=k == KT - 1)
                    m.then_inc(slot_done.sem, 1)
            loop(e, one)

        @on("act")
        def _(e):
            def one(e, i, r):
                slot_done.wait(e, i * 4 + (n0 + 2 * r + 1))
                glu_done.wait(e, i * 2 + (b_done + r - 1))
                act(e, i * 2 + r, tmp[:, r, :], PS[:, 2 * r, :], func).then_inc(glu_gate.sem, 1)
            loop(e, one)

        @on("dve")
        def _(e):
            def one(e, i, r):
                slot_done.wait(e, i * 4 + (n0 + 2 * r + 2))
                glu_gate.wait(e, i * 2 + (b_gate + r + 1))
                value(e, i * 2 + r, PS[:, 2 * r + 1, :], tmp[:, r, :]).then_inc(glu_done.sem, 1)
            loop(e, one)

    def evac_add(name, n, scale=1.0):
        def op(e, t, bank):
            return e.scalar_tensor_tensor(out=tile(X, t), in0=bank, scalar=scale, in1=tile(X, t),
                                          op0=ALU.mult, op1=ALU.add)
        evacuate("dve", name, n, op, evac_dve)

    def mixer1():
        m = ExitStack()
        U = sb(m, "conv_in", [P, KT, TAPS - 1 + S])
        Y = sb(m, "conv_out", [P, KT, S])
        Q = sb(m, "q_raw", [P, KT, S])
        O = sb(m, "attn_T", [P, KT, S])
        G = sb(m, "gates", [P, 2 * KT, S])
        kz = sb(m, "k_padded", [P, 4, P + S])
        V = sb(m, "v_tokens", [P, NB + 1, P])
        cos, sin = sb(m, "cos", [P, S]), sb(m, "sin", [P, S])
        M = sb(m, "band_mask", [P, NB, 2 * P])
        qr = sb(m, "q_roped", [P, 2, S])
        Sb = sb(m, "scores", [P, 2, NB, 2 * P])
        pT = sb(m, "probs_T", [P, 2, 2 * NB, P])
        ra, rb = sb(m, "rope_a", [P, S]), sb(m, "rope_b", [P, S])
        osb = sb(m, "o_tokens", [P, NB, P])
        sinks = sb(m, "sinks", [P, HEADS])
        bv = sb(m, "b_v", [P, P])
        st = sb(m, "stats", [P, 2, 6, NB])
        tmp2 = Sb[:, :, 0:2, :].rearrange("p a b c -> p a (b c)")

        s_in = sig("m1_in").by_dma()

        @on("act")
        def _(e):
            e.dma_start(rb[:, :].bitcast(I32), a["positions"].partition_broadcast(P)).then_inc(s_in.sem, 16)
            e.dma_start(M[:, :, :], a["band_mask"]).then_inc(s_in.sem, 16)
            e.dma_start(sinks[:, :], a["sinks"].partition_broadcast(P)).then_inc(s_in.sem, 16)
            e.dma_start(bv[:, :], a["b_v"].partition_broadcast(P)).then_inc(s_in.sem, 16)
            s_const.wait(e, CONST_IN)

        s_zero = sig("m1_zero")

        @on("pool")
        def _(e):
            e.memset(U[:, :, 0:TAPS - 1], 0.0)
            e.memset(kz[:, :, :], 0.0)
            e.memset(V[:, 0, :], 0.0).then_inc(s_zero.sem, 1)

        on("pe")(lambda e: s_const.wait(e, CONST_IN))
        on("dve")(lambda e: s_const.wait(e, CONST_IN))
        b_h = rms_norm("norm1")

        s_ang, s_trig = sig("m1_angles"), sig("m1_trig")

        @on("dve")
        def _(e):
            s_in.wait(e, 64)
            e.tensor_scalar(ra[:, :], rb[:, :].bitcast(I32), c_("inv_freq"), None, ALU.mult)
            for shift, dst in ((0.0, sin), (0.25, cos)):
                e.drain()
                e.tensor_scalar(dst[:, :], ra[:, :], 1.0 / TWO_PI, shift, ALU.mult, ALU.add)
                e.drain()
                e.tensor_scalar(dst[:, :], dst[:, :], MAGIC, None, ALU.add)
                e.drain()
                e.tensor_scalar(qr[:, 0, :], dst[:, :], MAGIC, None, ALU.subtract)
                e.drain()
                e.scalar_tensor_tensor(out=dst[:, :], in0=qr[:, 0, :], scalar=-6.28125,
                                       in1=ra[:, :], op0=ALU.mult, op1=ALU.add)
                for part in (-1.9350051879882812e-3, -3.01991598195675e-7):
                    e.drain()
                    e.scalar_tensor_tensor(out=dst[:, :], in0=qr[:, 0, :], scalar=part,
                                           in1=dst[:, :], op0=ALU.mult, op1=ALU.add)
                if shift:
                    e.drain()
                    e.tensor_scalar(dst[:, :], dst[:, :], TWO_PI / 4, None, ALU.add)
                e.drain()
                e.tensor_scalar(dst[:, :], dst[:, :], 3.1415925, -3.1415925, ALU.min, ALU.max)\
                    .then_inc(s_ang.sem, 1)

        @on("act")
        def _(e):
            for n, dst in enumerate((sin, cos)):
                s_ang.wait(e, n + 1)
                e.activation(dst[:, :], dst[:, :], ACT.Sin).then_inc(s_trig.sem, 1)

        on("dve")(lambda e: s_zero.wait(e, 1))
        glu("glu", KT, tmp2,
            lambda e, p, t, bank, f: e.activation(t, bank, f, bias=cd("b_glu", p * 2)),
            ACT.Sigmoid,
            lambda e, p, bank, t: e.scalar_tensor_tensor(
                out=(U[:, p, TAPS - 1:] if isinstance(p, int) else
                     U[:, bass.ds(p, 1), TAPS - 1:].rearrange("p a s -> p (a s)")),
                in0=bank, scalar=cd("b_glu", p * 2 + 1), in1=t, op0=ALU.add, op1=ALU.mult),
            (s_h, b_h))

        pe_gemm("q", KT, lambda k: H[:, k, :])
        evacuate("act", "q", KT,
                 lambda e, t, bank: e.activation(tile(Q, t), bank, ACT.Identity, bias=cd("b_q", t)),
                 evac_act)
        q_in = evac_act.n

        n_kv = START["kv"]
        e_act, e_dve = evac_act.n, evac_dve.n
        evac_act.plan(2)
        evac_dve.plan(1)
        s_kr, s_kc, s_kz, s_v = sig("k_rot"), sig("k_cos"), sig("k_done"), sig("v_done")

        @on("pe")
        def _(e):
            evac_act.wait(e, e_act)
            for j in range(2):
                w = tiles_of(use_slot(e, n_kv, 0, 4, j))
                for k in range(KT):
                    mm = e.matmul(PS[:, j, :], w[:, k, :], H[:, k, :], start=k == 0, stop=k == KT - 1)
                mm.then_inc(slot_done.sem, 1)
            w = tiles_of(use_slot(e, n_kv, 0, 4, 2))
            for n in range(NB):
                for k in range(KT):
                    mm = e.matmul(PS[:, 2, n * P:(n + 1) * P], H[:, k, n * P:(n + 1) * P],
                                  w[:, k, :], start=k == 0, stop=k == KT - 1)
            mm.then_inc(slot_done.sem, 1)
            for j in range(2):
                evac_act.wait(e, e_act + j + 1)
                e.matmul(PS[:, 4 + j, :], rot, O[:, j, :], start=True, stop=True).then_inc(s_kr.sem, 1)

        @on("act")
        def _(e):
            for j in range(2):
                slot_done.wait(e, n_kv + j + 1)
                e.activation(O[:, j, :], PS[:, j, :], ACT.Identity, bias=c_("b_k", j))\
                    .then_inc(evac_act.sem, 1)

        @on("pool")
        def _(e):
            s_trig.wait(e, 2)
            for j in range(2):
                evac_act.wait(e, e_act + j + 1)
                e.tensor_tensor(qr[:, j, :], O[:, j, :], cos[:, :], ALU.mult).then_inc(s_kc.sem, 1)

        @on("dve")
        def _(e):
            slot_done.wait(e, n_kv + 3)
            e.tensor_tensor(V[:, 1:, :], PS[:, 2, :].rearrange("p (n c) -> p n c", n=NB),
                            view(bv[:, :], [0, NB], [1, P]), ALU.add).then_inc(evac_dve.sem, 1)
            s_trig.wait(e, 2)
            for j in range(2):
                e.drain()
                s_kr.wait(e, j + 1)
                s_kc.wait(e, j + 1)
                e.tensor_tensor(rb[:, :], PS[:, 4 + j, :], sin[:, :], ALU.mult)
                e.drain()
                for half in range(2):
                    h = slice(64 * half, 64 * half + 64)
                    e.tensor_tensor(kz[h, 2 * j + half, P:], qr[h, j, :], rb[h, :], ALU.add)\
                        .then_inc(s_kz.sem, 1)
            for c in range(KT):
                e.tensor_scalar(Y[:, c, :], U[:, c, 0:S], c_("conv_w", c), c_("conv_b", c),
                                ALU.mult, ALU.add)

        def tap(e, w):
            e.drain()
            for c in range(KT):
                e.scalar_tensor_tensor(out=Y[:, c, :], in0=U[:, c, bass.ds(w, S)],
                                       scalar=cd("conv_w", w * KT + c), in1=Y[:, c, :],
                                       op0=ALU.mult, op1=ALU.add)

        n_g = START["gates"]
        g_base = evac_act.plan(16)
        (s_arot, s_aqc, s_qr, s_sc, s_sm, s_ex, s_tr, s_pt, s_pv, s_on, s_ot, s_oe) = [
            sig("at_" + x) for x in ("rot", "qcos", "qr", "scores", "max", "exp", "trans", "probsT",
                                     "pv", "norm", "oT", "o_out")]

        def tiles_loop(e, one):
            with e.Fori(0, 2) as g:
                with e.Fori(0, 2) as i:
                    for b in range(2):
                        one(g, g * 4 + i * 2 + b, g * 2 + i, b)

        @on("pe")
        def _(e):
            evac_act.wait(e, q_in + 2)
            evac_dve.wait(e, e_dve + 1)
            s_kz.wait(e, 4)

            def gemm(it, b, j, t):
                w = tiles_of(use_slot(e, n_g, it, 4, 2 * b + j))
                evac_act.wait(e, t * 2 + (g_base + j))
                for k in range(KT):
                    mm = e.matmul(PS[:, 7, :], w[:, k, :], H[:, k, :], start=k == 0, stop=k == KT - 1)
                mm.then_inc(slot_done.sem, 1)

            def one(g, t, it, b):
                s_on.wait(e, t * 2)
                e.matmul(PS[:, 6, :], rot, tile(Q, t), start=True, stop=True).then_inc(s_arot.sem, 1)
                gemm(it, b, 0, t)
                s_qr.wait(e, t + 1)
                for h in range(2):
                    (s_oe if h else s_pt).wait(e, t if h else t * 2)
                    for n in range(NB):
                        mm = e.matmul(PS[:, 2 * h + n // 2, (n % 2) * 256:(n % 2) * 256 + 256],
                                      qr[:, b, n * P:(n + 1) * P],
                                      kz[:, bass.ds(g * 2 + h, 1), n * P:(n + 2) * P]
                                      .rearrange("p a s -> p (a s)"), start=True, stop=True)
                    mm.then_inc(s_sc.sem, 1)
                gemm(it, b, 1, t)
                for h in range(2):
                    s_ex.wait(e, t * 2 + (h + 1))
                    for c in range(2 * NB):
                        bank = (0 if h else 4) + c // 4
                        mm = e.transpose(PS[:, bank, (c % 4) * P:(c % 4 + 1) * P],
                                         Sb[:, h, c // 2, (c % 2) * P:(c % 2 + 1) * P], ident)
                    mm.then_inc(s_tr.sem, 1)
                for h in range(2):
                    s_pt.wait(e, t * 2 + (h + 1))
                    for n in range(NB):
                        for c in range(2):
                            mm = e.matmul(PS[:, 3 if h else 6, n * HD:(n + 1) * HD],
                                          pT[:, h, 2 * n + c, :],
                                          V[:, n + c, bass.ds(g * HD, HD)], start=c == 0, stop=c == 1)
                    mm.then_inc(s_pv.sem, 1)
                s_on.wait(e, t * 2 + 2)
                for n in range(NB):
                    mm = e.transpose(PS[:, 2, n * P:(n + 1) * P], osb[:, n, :], ident)
                mm.then_inc(s_ot.sem, 1)
            tiles_loop(e, one)

        @on("pool")
        def _(e):
            s_kz.wait(e, 4)

            def one(g, t, it, b):
                s_qr.wait(e, t)
                e.tensor_tensor(ra[:, :], tile(Q, t), cos[:, :], ALU.mult).then_inc(s_aqc.sem, 1)
            tiles_loop(e, one)

        @on("dve")
        def _(e):
            def one(g, t, it, b):
                e.drain()
                s_arot.wait(e, t + 1)
                e.tensor_tensor(rb[:, :], PS[:, 6, :], sin[:, :], ALU.mult)
                e.drain()
                s_aqc.wait(e, t + 1)
                e.tensor_tensor(qr[:, b, :], ra[:, :], rb[:, :], ALU.add).then_inc(s_qr.sem, 1)
                for h in range(2):
                    s_sc.wait(e, t * 2 + (h + 1))
                    mx, nm, ds = st[:, h, 0, :], st[:, h, 1, :], st[:, h, 2, :]
                    e.scalar_tensor_tensor(
                        out=Sb[:, h, :, :].rearrange("p n k -> p (n k)"),
                        in0=PS[:, 2 * h:2 * h + 2, :].rearrange("p a b -> p (a b)"),
                        scalar=HD ** -0.5, in1=M[:, :, :].rearrange("p n k -> p (n k)"),
                        op0=ALU.mult, op1=ALU.add)
                    e.drain()
                    e.tensor_reduce(mx, Sb[:, h, :, :], AX.X, ALU.max)
                    e.drain()
                    e.tensor_scalar(nm, mx, col(sinks, t * 2 + h), -1.0, ALU.max, ALU.mult)
                    e.drain()
                    e.tensor_scalar(ds, nm, col(sinks, t * 2 + h), None, ALU.add).then_inc(s_sm.sem, 1)
                for h in range(2):
                    tap(e, t * 2 + (h + 1))
                    s_ex.wait(e, t * 2 + (h + 1))
                    e.tensor_tensor(st[:, h, 5, :], st[:, h, 3, :], st[:, h, 4, :], ALU.add)
                    e.drain()
                    e.reciprocal(st[:, h, 5, :], st[:, h, 5, :])
                    e.drain()
                    s_pv.wait(e, t * 2 + (h + 1))
                    if h == 0:
                        s_ot.wait(e, t)
                    e.tensor_tensor(osb[:, :, h * HD:(h + 1) * HD],
                                    PS[:, 3 if h else 6, 0:NB * HD]
                                    .rearrange("p (n c) -> p n c", n=NB),
                                    view(st[:, h, 5, :], [1, NB], [0, HD]), ALU.mult)\
                        .then_inc(s_on.sem, 1)
            tiles_loop(e, one)
            with e.Fori(2 * KT + 1, TAPS) as w:
                tap(e, w)

        @on("act")
        def _(e):
            def gate(t, j):
                slot_done.wait(e, t * 2 + (n_g + j + 1))
                e.activation(tile(G, t * 2 + j), PS[:, 7, :], ACT.Identity, bias=cd("b_gates", t * 2 + j))\
                    .then_inc(evac_act.sem, 1)

            def one(g, t, it, b):
                gate(t, 0)
                for h in range(2):
                    s_sm.wait(e, t * 2 + (h + 1))
                    for n in range(NB):
                        e.activation(Sb[:, h, n, :], Sb[:, h, n, :], ACT.Exp,
                                     bias=st[:, h, 1, n:n + 1], accum_out=st[:, h, 3, n:n + 1])
                    e.activation(st[:, h, 4, :], st[:, h, 2, :], ACT.Exp).then_inc(s_ex.sem, 1)
                gate(t, 1)
                for h in range(2):
                    s_tr.wait(e, t * 2 + (h + 1))
                    s_pv.wait(e, t * 2)
                    bank = 0 if h else 4
                    e.activation(pT[:, h, :, :].rearrange("p c k -> p (c k)"),
                                 PS[:, bank:bank + 2, :].rearrange("p a b -> p (a b)"), ACT.Copy)\
                        .then_inc(s_pt.sem, 1)
                s_ot.wait(e, t + 1)
                e.activation(tile(O, t), PS[:, 2, :], ACT.Copy).then_inc(s_oe.sem, 1)
            tiles_loop(e, one)

        s_ao, s_sg = sig("m1_attn_gated"), sig("m1_sigmoid")

        @on("act")
        def _(e):
            e.drain()
            with e.Fori(0, 2 * KT) as i:
                e.activation(tile(G, i), tile(G, i), ACT.Sigmoid).then_inc(s_sg.sem, 1)
        on("pe")(lambda e: s_oe.wait(e, KT))
        pe_gemm("attn_o", KT, lambda k: O[:, k, :])
        ao = evac_act.n
        evacuate("act", "attn_o", KT,
                 lambda e, t, bank: e.activation(tile(H, t), bank, ACT.Copy), evac_act)

        @on("pool")
        def _(e):
            s_sg.wait(e, 2 * KT)
            with e.Fori(0, KT) as i:
                evac_act.wait(e, i + (ao + 1))
                e.tensor_tensor(tile(H, i), tile(H, i), tile(G, i + KT), ALU.mult).then_inc(s_ao.sem, 1)

        s_y, s_mu, s_xc, s_lsq, s_lmm, s_lr, s_ln, s_silu = [
            sig("ln_" + x) for x in ("in", "mean", "centred", "square", "var", "root", "scaled", "silu")]

        @on("dve")
        def _(e):
            e.drain().then_inc(s_y.sem, 1)
            s_mu.wait(e, 1)
            for c in range(KT):
                e.tensor_tensor(Y[:, c, :], Y[:, c, :], PS[:, 5, :], ALU.subtract).then_inc(s_xc.sem, 1)
            s_lr.wait(e, 1)
            e.reciprocal(ra[:, :], ra[:, :])
            e.drain()
            for c in range(KT):
                e.scalar_tensor_tensor(out=Y[:, c, :], in0=Y[:, c, :], scalar=c_("ln_g", c),
                                       in1=ra[:, :], op0=ALU.mult, op1=ALU.mult).then_inc(s_ln.sem, 1)

        @on("pe")
        def _(e):
            s_y.wait(e, 1)
            for c in range(KT):
                mm = e.matmul(PS[:, 5, :], mean, Y[:, c, :], start=c == 0, stop=c == KT - 1)
            mm.then_inc(s_mu.sem, 1)
            for c in range(KT):
                s_lsq.wait(e, c + 1)
                e.matmul(PS[:, 6, :], mean, norm_sq[:, c % 2, :], start=c == 0, stop=c == KT - 1)\
                    .then_inc(s_lmm.sem, 1)

        @on("act")
        def _(e):
            for c in range(KT):
                s_xc.wait(e, c + 1)
                if c >= 2:
                    s_lmm.wait(e, c - 1)
                e.activation(norm_sq[:, c % 2, :], Y[:, c, :], ACT.Square).then_inc(s_lsq.sem, 1)
            s_lmm.wait(e, KT)
            e.activation(ra[:, :], PS[:, 6, :], ACT.Sqrt, bias=c_("eps")).then_inc(s_lr.sem, 1)
            for c in range(KT):
                s_ln.wait(e, c + 1)
                e.activation(Y[:, c, :], Y[:, c, :], ACT.Silu, bias=c_("ln_b", c)).then_inc(s_silu.sem, 1)

        pe_gemm("conv_out", KT, lambda k: Y[:, k, :], (s_silu, 0), free=evac_dve)
        merged = evac_dve.n

        def merge(e, t, bank):
            e.tensor_tensor(tile(G, t), bank, tile(G, t), ALU.mult)
            e.drain()
            s_ao.wait(e, t + 1)
            return e.tensor_tensor(tile(Q, t), tile(G, t), tile(H, t), ALU.add)
        evacuate("dve", "conv_out", KT, merge, evac_dve)
        pe_gemm("w_out", KT, lambda k: Q[:, k, :], (evac_dve, merged), free=evac_dve)
        evac_add("w_out", KT)
        barrier()
        m.close()

    def peer():
        m = ExitStack()
        A0 = sb(m, "experts_0", [P, JQ, S])
        TT = sb(m, "picks_T", [P, 2, S])
        gate_row = norm_r
        gp = sb(m, "gate_parts", [P, 3, S], BF16)
        iota_b = sb(m, "iota_bf16", [P, P], BF16)
        hot_i = sb(m, "key1_one_hot", [P, 2, 16, P], BF16)
        hot_e = sb(m, "key2_one_hot", [P, 16, JQ], BF16)
        hot_j = sb(m, "gate_at_key2", [P, 2, 3, 16, JQ], BF16)
        sc = ExitStack()
        keysT = sb(sc, "sub_keys_T", [P, 2 * PH, NKEY])
        qh = sb(sc, "peer_q", [P, 2, S])
        raw = sb(sc, "peer_scores", [P, 8, NKEY])
        work = sb(sc, "scores_left", [P, 8, NKEY])
        cand = sb(sc, "sums", [P, NB, TOPK * TOPK])
        cand2 = sb(sc, "sums_left", [P, NB, TOPK * TOPK])
        eq_a, eq_b = sb(sc, "row_hot", [P, NB * TOPK, TOPK]), sb(sc, "col_hot", [P, NB * TOPK, TOPK])
        T = sb(sc, "picks", [P, 3, NB, PH * TOPK])
        top = sb(sc, "top", [P, 8, TOPK])
        idx, idxf = sb(sc, "top_index", [P, 8, TOPK], U32), sb(sc, "top_index_f", [P, 8, TOPK])
        best = sb(sc, "best", [P, NB, TOPK])
        pos = sb(sc, "best_pos", [P, NB, TOPK], U32)
        pa, pb = sb(sc, "pos_row", [P, NB, TOPK], U32), sb(sc, "pos_col", [P, NB, TOPK], U32)
        gsum = sb(sc, "gate_sum", [P, NB * PH])

        s_keys = sig("peer_keys").by_dma()
        s_qe, s_psc, s_top, s_u = [sig("peer_" + x) for x in ("q_out", "scores", "top", "u_out")]
        on("act")(lambda e: e.dma_start(keysT[:, :, :], a["keysT"]).then_inc(s_keys.sem, 16))
        b_h = rms_norm("norm2")
        nq = START["peer_q_u0"]

        def heads_loop(e, one):
            with e.Fori(0, PH // 2) as i:
                for b in range(2):
                    one(i, i * 2 + b, b)

        on("pe")(lambda e: (s_keys.wait(e, 16), s_h.wait(e, b_h + KT)))

        @on("pe")
        def _(e):
            def product(bank, w):
                for k in range(KT):
                    mm = e.matmul(PS[:, bank, :], w[:, k, :], H[:, k, :], start=k == 0, stop=k == KT - 1)
                mm.then_inc(slot_done.sem, 1)

            def one(i, h, b):
                def scores(c):
                    s_qe.wait(e, h * 2 + (c + 1))
                    s_top.wait(e, h)
                    for n in range(NB):
                        mm = e.matmul(PS[:, 2 + c, n * P:(n + 1) * P], qh[:, c, n * P:(n + 1) * P],
                                      tile(keysT, h * 2 + c), start=True, stop=True)
                    mm.then_inc(s_psc.sem, 1)

                for c in range(2):
                    w = tiles_of(use_slot(e, nq, i, 12, 6 * b + c))
                    s_qe.wait(e, h * 2)
                    product(c, w)
                for r in range(4):
                    if r in (0, 1):
                        scores(r)
                    w = tiles_of(use_slot(e, nq, i, 12, 6 * b + 2 + r))
                    s_u.wait(e, h * 4)
                    product(4 + r, w)
            heads_loop(e, one)

        @on("act")
        def _(e):
            def one(i, h, b):
                for c in range(2):
                    slot_done.wait(e, i * 12 + (nq + 6 * b + c + 1))
                    s_psc.wait(e, h * 2)
                    e.activation(qh[:, c, :], PS[:, c, :], ACT.Copy).then_inc(s_qe.sem, 1)
                for r in range(4):
                    slot_done.wait(e, i * 12 + (nq + 6 * b + 3 + r))
                    e.activation(tile(A0, h * 4 + r), PS[:, 4 + r, :], ACT.Gelu).then_inc(s_u.sem, 1)
            heads_loop(e, one)
        s_u.plan(JQ)

        @on("dve")
        def _(e):
            def top16(values, left, vals, index, n):
                for c in range(n):
                    e.max(vals[:, c, 0:8], values(c))
                e.drain()
                for c in range(n):
                    e.max_index(index[:, c, 0:8], vals[:, c, 0:8], values(c))
                    e.match_replace(left[:, c, :], vals[:, c, 0:8], values(c), TAKEN)
                e.drain()
                for c in range(n):
                    e.max(vals[:, c, 8:16], left[:, c, :])
                e.drain()
                for c in range(n):
                    e.max_index(index[:, c, 8:16], vals[:, c, 8:16], left[:, c, :])
                e.drain()

            def one(i, h, b):
                e.drain()
                s_psc.wait(e, h * 2 + 2)
                e.tensor_copy(raw[:, :, :].rearrange("p c n -> p (c n)"),
                              PS[:, 2:4, :].rearrange("p a b -> p (a b)")).then_inc(s_top.sem, 1)
                e.drain()
                top16(lambda c: raw[:, c, :], work, top, idx, 8)
                e.tensor_copy(idxf[:, :, :], idx[:, :, :])
                e.tensor_tensor(cand[:, :, :].rearrange("p n (r c) -> p n r c", r=TOPK),
                                view(top[:, 0, :], [TOPK, NB], [1, TOPK], [0, TOPK]),
                                view(top[:, NB, :], [TOPK, NB], [0, TOPK], [1, TOPK]), ALU.add)
                e.drain()
                top16(lambda c: cand[:, c, :], cand2, best, pos, NB)
                e.tensor_scalar(pa[:, :, :], pos[:, :, :], 4, None, ALU.logical_shift_right)
                e.tensor_scalar(pb[:, :, :], pos[:, :, :], 15, None, ALU.bitwise_and)
                e.tensor_copy(T[:, 2, :, bass.ds(h * TOPK, TOPK)], best[:, :, :])
                e.drain()
                for p_, eq in ((pa, eq_a), (pb, eq_b)):
                    e.tensor_tensor(eq[:, :, :], view(p_[:, 0, :], [1, NB * TOPK], [0, TOPK]),
                                    view(iota, [0, NB * TOPK], [1, TOPK]), ALU.is_equal)
                e.drain()
                for c, eq in enumerate((eq_a, eq_b)):
                    v = eq[:, :, :].rearrange("p (n k) r -> p n k r", n=NB)
                    e.tensor_tensor(v, v, view(idxf[:, c * NB, :], [TOPK, NB], [0, TOPK], [1, TOPK]),
                                    ALU.mult)
                e.drain()
                for c, eq in enumerate((eq_a, eq_b)):
                    e.tensor_reduce(T[:, c, :, bass.ds(h * TOPK, TOPK)],
                                    eq[:, :, :].rearrange("p (n k) r -> p n k r", n=NB), AX.X, ALU.add)
            heads_loop(e, one)

        s_gx, s_ge, s_tab, s_tt, s_tabT = [sig("gate_" + x) for x in
                                           ("shifted", "exp", "table", "turned", "table_T")]
        g2 = T[:, 2, :, :].rearrange("p n (h k) -> p (n h) k", k=TOPK)

        @on("dve")
        def _(e):
            e.drain()
            e.tensor_copy(gsum[:, :], view(T[:, 2, 0, 0:1], [TOPK, NB * PH]))
            e.drain()
            e.tensor_tensor(g2, g2, view(gsum[:, :], [1, NB * PH], [0, TOPK]), ALU.subtract)\
                .then_inc(s_gx.sem, 1)
            s_ge.wait(e, 1)
            e.tensor_reduce(gsum[:, :], g2, AX.X, ALU.add)
            e.drain()
            e.reciprocal(gsum[:, :], gsum[:, :])
            e.drain()
            e.tensor_tensor(g2, g2, view(gsum[:, :], [1, NB * PH], [0, TOPK]), ALU.mult)\
                .then_inc(s_tab.sem, 1)
            for v in range(3):
                s_tt.wait(e, v + 1)
                e.tensor_copy(TT[:, v, :] if v < 2 else gate_row[:, :], PS[:, v, :]).then_inc(s_tabT.sem, 1)
            e.tensor_copy(iota_b[:, :], iota)
            for v in range(3):
                e.drain()
                e.tensor_copy(gp[:, v, :], gate_row[:, :])
                e.drain()
                if v < 2:
                    e.tensor_tensor(gate_row[:, :], gate_row[:, :], gp[:, v, :], ALU.subtract)

        @on("act")
        def _(e):
            s_gx.wait(e, 1)
            v = T[:, 2, :, :]
            e.activation(v, v, ACT.Exp).then_inc(s_ge.sem, 1)

        @on("pe")
        def _(e):
            s_tab.wait(e, 1)
            s_qe.wait(e, 2 * PH)
            for v in range(3):
                for n in range(NB):
                    mm = e.transpose(PS[:, v, n * P:(n + 1) * P], T[:, v, n, :], ident)
                mm.then_inc(s_tt.sem, 1)
        on("act")(lambda e: s_tt.wait(e, 3))
        sc.close()
        A1 = sb(m, "experts_1", [P, JQ, S])
        A = [A0, A1]

        s_hot, s_wm, s_g, s_ve = [sig("w_" + x) for x in ("one_hot", "product", "gated", "v_out")]
        on("pe")(lambda e: e.sem_inc(s_wm.sem, 4))
        on("dve")(lambda e: e.sem_inc(s_g.sem, 2))
        s_wm.n, s_g.n = 4, 2
        u_ready, g_ready = {0: s_u.n}, {}

        def u_slot(e, q, base, i, r):
            w = tiles_of(use_slot(e, START[f"u{q}"], i, 4, r))
            s_u.wait(e, i * 4 + (base + r - 1))
            for k in range(KT):
                mm = e.matmul(PS[:, 4 + r % 2, :], w[:, k, :], H[:, k, :], start=k == 0,
                              stop=k == KT - 1)
            mm.then_inc(slot_done.sem, 1)

        def v_slot(e, q, base, dh, i, r, first, last):
            n0 = START[f"v{q}"]
            n = n0 + r
            e.wait_ge(arrive[n % RING], dh * 64 + i * 16 + 16 * (n // RING + 1))
            w = ring[:, n % RING, :].rearrange("p (j c) -> p j c", j=2)
            for j in range(2):
                for d in range(4):
                    if first and r == 0 and j == 0:
                        s_ve.wait(e, dh * 4 + base)
                    mm = e.matmul(PS[:, d, :], w[:, j, d * P:(d + 1) * P],
                                  tile(A[q % 2], i * 8 + (2 * r + j)),
                                  start=first and r == 0 and j == 0, stop=last and r == 3 and j == 1)
            mm.then_inc(slot_done.sem, 1)

        def w_group(e, bw, bg, g, r):
            s_g.wait(e, g + (bg - 1))
            for u in range(16):
                if u % 4 == 0:
                    s_hot.wait(e, g * 4 + (bw + u // 4 + 1))
                for v in range(3):
                    mm = e.matmul(PS[:, 6 + r % 2, u * JQ:(u + 1) * JQ], hot_i[:, r % 2, u, :],
                                  hot_j[:, r % 2, v, u, :], start=v == 0, stop=v == 2)
                if u % 4 == 3:
                    mm.then_inc(s_wm.sem, 1)

        def hot_and_gate(e, q, bw, bwm, g, r):
            s0 = g * 16
            tj = TT[:, 1, bass.ds(s0, 16)].unsqueeze(2).broadcast_to([P, 16, JQ])
            e.tensor_tensor(hot_e[:, :, :], tj,
                            view(iota[:, q * JQ:(q + 1) * JQ], [0, 16], [1, JQ]), ALU.is_equal)
            e.drain()
            s_wm.wait(e, g * 4 + (bwm - 4))
            for v in range(3):
                e.tensor_tensor(hot_j[:, r % 2, v, :, :], hot_e[:, :, :],
                                gp[:, v, bass.ds(s0, 16)].unsqueeze(2).broadcast_to([P, 16, JQ]),
                                ALU.mult)
            for u in range(16):
                ins = e.tensor_scalar(hot_i[:, r % 2, u, :], iota_b[:, :],
                                      TT[:, 0, bass.ds(s0 + u, 1)], None, ALU.is_equal)
                if u % 4 == 3:
                    ins.then_inc(s_hot.sem, 1)
            s_wm.wait(e, g * 4 + (bwm + 4))
            At = A[q % 2][:, :, bass.ds(s0, 16)]
            e.tensor_tensor(At, PS[:, 6 + r % 2, :].rearrange("p (s j) -> p j s", j=JQ), At,
                            ALU.mult).then_inc(s_g.sem, 1)

        def window(kind, q, wq):
            bu, bv = s_u.n, s_ve.n
            if wq is not None:
                bw, bwm, bg = s_hot.plan(128), s_wm.plan(128), s_g.plan(32)
                g_ready[wq] = s_g.n
            if kind == "u":
                s_u.plan(JQ)
                u_ready[q] = s_u.n

                @on("pe")
                def _(e):
                    with e.Fori(0, JQ // 4) as i:
                        for r in range(4):
                            u_slot(e, q, bu, i, r)
                            if wq is not None:
                                w_group(e, bw, bg, i * 4 + r, r)

                @on("act")
                def _(e):
                    with e.Fori(0, JQ // 4) as i:
                        for r in range(4):
                            slot_done.wait(e, i * 4 + (START[f"u{q}"] + r + 1))
                            e.activation(tile(A[q % 2], i * 4 + r), PS[:, 4 + r % 2, :], ACT.Gelu)\
                                .then_inc(s_u.sem, 1)
                if wq is not None:
                    @on("dve")
                    def _(e):
                        s_u.wait(e, u_ready[wq])
                        with e.Fori(0, 8) as i:
                            for r in range(4):
                                hot_and_gate(e, wq, bw, bwm, i * 4 + r, r)
            else:
                s_ve.plan(8)

                @on("pe")
                def _(e):
                    s_g.wait(e, g_ready[q])
                    with e.Fori(0, 2) as dh:
                        def body(i, first, last):
                            for r in range(4):
                                v_slot(e, q, bv, dh, i, r, first, last)
                                if wq is not None:
                                    w_group(e, bw, bg, dh * 16 + i * 4 + r, r)
                        body(0, True, False)
                        with e.Fori(1, 3) as i:
                            body(i, False, False)
                        body(3, False, True)

                @on("dve")
                def _(e):
                    if wq is not None:
                        s_u.wait(e, u_ready[wq])
                    with e.Fori(0, 2) as dh:
                        if wq is not None:
                            with e.Fori(0, 4) as i:
                                for r in range(4):
                                    hot_and_gate(e, wq, bw, bwm, dh * 16 + i * 4 + r, r)
                        slot_done.wait(e, dh * 16 + (START[f"v{q}"] + 16))
                        for d in range(4):
                            e.tensor_tensor(tile(X, dh * 4 + d), PS[:, d, :], tile(X, dh * 4 + d),
                                            ALU.add).then_inc(s_ve.sem, 1)
                    e.drain()

        on("pe")(lambda e: s_tabT.wait(e, 3))
        for kind, q, wq in (("u", 1, 0), ("v", 0, 1), ("u", 2, None), ("v", 1, 2), ("u", 3, None),
                            ("v", 2, 3), ("v", 3, None)):
            window(kind, q, wq)
        rms_norm("final1", dst=X, ready=(s_ve, s_ve.n - KT))
        barrier()
        m.close()

    def ffn(n):
        m = ExitStack()
        F = sb(m, f"ffn{n}_hidden", [P, FT, S])
        tmp = sb(m, f"ffn{n}_gate", [P, 2, S])
        b_h = rms_norm(f"ffn{n}_n")
        first = glu_done.n
        glu(f"f{n}_in", FT, tmp, lambda e, p, t, bank, f: e.activation(t, bank, f), ACT.Silu,
            lambda e, p, bank, t: e.tensor_tensor(tile(F, p), bank, t, ALU.mult), (s_h, b_h))
        nd = START[f"f{n}_out"]

        @on("pe")
        def _(e):
            def slot(i, r, first_, last):
                glu_done.wait(e, i * 4 + (first + r + 1))
                w = tiles_of(use_slot(e, nd, i, 4, r))
                for d in range(KT):
                    if first_ and d < 4:
                        glu_done.wait(e, first + FT)
                    mm = e.matmul(PS[:, d, :], w[:, d, :], tile(F, i * 4 + r), start=first_, stop=last)
                mm.then_inc(slot_done.sem, 1)
            for r in range(4):
                slot(0, r, r == 0, False)
            with e.Fori(1, FT // 4) as i:
                for r in range(4):
                    slot(i, r, False, False)
            for r in range(FT % 4):
                slot(FT // 4, r, False, r == FT % 4 - 1)
        done = evac_dve.plan(KT)

        @on("dve")
        def _(e):
            slot_done.wait(e, nd + FT)
            for d in range(KT):
                e.scalar_tensor_tensor(out=X[:, d, :], in0=PS[:, d, :], scalar=0.5, in1=X[:, d, :],
                                       op0=ALU.mult, op1=ALU.add).then_inc(evac_dve.sem, 1)
        barrier()
        m.close()
        return done

    def mixer2():
        m = ExitStack()
        qk = sb(m, "gla_qk", [P, 2 * GH, S])
        v = sb(m, "gla_v", [P, NB, GH * GDV])
        wide = sb(m, "wide2", [P, 32, S])
        ckvT, ckv = sb(m, "ckv_T", [P, S]), sb(m, "ckv", [P, NB, P])
        sel = sb(m, "selection", [P, NB, S], mybir.dt.bfloat16)
        gl = ExitStack()
        la = sb(gl, "log_decay", [P, GH, S])
        lmask = sb(gl, "level_mask", [P, 8, P])
        iqT, ikT = wide[:, 0:4, :], wide[:, 4, :]
        gaT, alw = wide[0:16, 5, :], wide[0:16, 6, :]
        score = wide[:, 8:12, :]
        rel = wide[:, 12:14, :]
        ex = wide[:, 16:20, :]
        iw = sb(gl, "index_w", [P, NB, 8])
        i8 = sb(gl, "index_top", [P, 3, 8])
        tri = sb(gl, "causal", [P, P])

        s_in, s_hd = sig("m2_in").by_dma(), sig("m2_evac")
        b_in = s_in.plan(64)

        @on("act")
        def _(e):
            e.dma_start(alw, a["alpha_w"]).then_inc(s_in.sem, 16)
            e.dma_start(lmask[:, :, :], a["level_mask"]).then_inc(s_in.sem, 16)
            e.dma_start(tri[:, :], a["causal"]).then_inc(s_in.sem, 16)
        b_h = rms_norm("mix_n")
        nh = START["misc"]
        s_root2, s_csq, s_cmm, s_cn, s_ct, s_ce = [sig("ckv_" + x) for x in
                                                   ("root", "square", "mean", "normed", "turned", "tokens")]
        s_al, s_ax, s_dot, s_rel, s_acc = [sig("ix_" + x) for x in
                                           ("alpha", "log", "dots", "relu", "sum")]
        on("dve")(lambda e: e.sem_inc(s_acc.sem, 2))
        s_acc.n = 2
        combos = [(n, h) for n in range(1, NB) for h in range(8)]
        old = [(s, s.n) for s in (evac_act, evac_dve, glu_done)]

        @on("pe")
        def _(e):
            s_h.wait(e, b_h + KT)
            for s, x in old:
                s.wait(e, x)
            w = tiles_of(use_slot(e, nh, 0, 4, 0))
            for k in range(KT):
                e.matmul(PS[0:16, 0, :], w[:, k, 0:16], H[:, k, :], start=k == 0, stop=k == KT - 1)
            for n in range(NB):
                for k in range(KT):
                    mm = e.matmul(PS[:, 1, n * 8:(n + 1) * 8], H[:, k, n * P:(n + 1) * P],
                                  w[:, k, 16:24], start=k == 0, stop=k == KT - 1)
            mm.then_inc(slot_done.sem, 1)
            for j in range(6):
                w = tiles_of(use_slot(e, nh, 0, 4, j + 1))
                for k in range(KT):
                    mm = e.matmul(PS[:, 2 + j, :], w[:, k, :], H[:, k, :], start=k == 0, stop=k == KT - 1)
                mm.then_inc(slot_done.sem, 1)
            s_in.wait(e, 48)
            s_hd.wait(e, 2)
            for h in range(GH):
                if h >= 2:
                    s_hd.wait(e, h + 1)
                e.matmul(PS[:, h, :], alw[:, h * P:(h + 1) * P], gaT, start=True, stop=True)\
                    .then_inc(s_al.sem, 1)
            s_csq.wait(e, 1)
            e.matmul(PS[:, 7, :], mean, norm_sq[:, 0, :], start=True, stop=True).then_inc(s_cmm.sem, 1)
            for x, (n, h) in enumerate(combos):
                rows = slice(64 * (h % 2), 64 * (h % 2) + 64)
                s_rel.wait(e, max(x - 1, 0))
                e.matmul(PS[:, 4 + x % 2, 0:(n + 1) * P], iqT[rows, h // 2, n * P:(n + 1) * P],
                         ikT[rows, 0:(n + 1) * P], start=True, stop=True).then_inc(s_dot.sem, 1)
            s_cn.wait(e, 1)
            for n in range(NB):
                mm = e.transpose(PS[:, 6, n * P:(n + 1) * P], ckvT[:, n * P:(n + 1) * P], ident)
            mm.then_inc(s_ct.sem, 1)

        @on("act")
        def _(e):
            slot_done.wait(e, nh + 1)
            e.activation(gaT, PS[0:16, 0, :], ACT.Copy).then_inc(s_hd.sem, 1)
            e.activation(iw[:, :, :].rearrange("p n h -> p (n h)"), PS[:, 1, 0:32], ACT.Copy,
                         scale=8 ** -0.5).then_inc(s_hd.sem, 1)
            for j, dst in enumerate([ikT] + [iqT[:, t, :] for t in range(4)] + [ckvT[:, :]]):
                slot_done.wait(e, nh + j + 2)
                e.activation(dst, PS[:, 2 + j, :], ACT.Copy).then_inc(s_hd.sem, 1)
            s_hd.wait(e, 8)
            e.activation(norm_sq[:, 0, :], ckvT[:, :], ACT.Square).then_inc(s_csq.sem, 1)
            s_cmm.wait(e, 1)
            e.activation(norm_r[:, :], PS[:, 7, :], ACT.Sqrt, scale=float(KT), bias=c_("eps"))\
                .then_inc(s_root2.sem, 1)
            for h in range(GH):
                s_al.wait(e, h + 1)
                e.activation(la[:, h, :], PS[:, h, :], ACT.Identity, bias=c_("alpha_b", h))
            e.drain()
            flat, exf = la[:, :, :], ex
            e.activation(exf, flat, ACT.Abs)
            e.drain()
            e.activation(exf, exf, ACT.Exp, scale=-1.0)
            e.drain()
            e.activation(exf, exf, ACT.Ln, bias=c_("one")).then_inc(s_ax.sem, 1)
            for x, (n, h) in enumerate(combos):
                s_dot.wait(e, x + 1)
                s_acc.wait(e, x + 1)
                e.activation(rel[:, x % 2, 0:(n + 1) * P], PS[:, 4 + x % 2, 0:(n + 1) * P], ACT.Relu,
                             scale=0.125).then_inc(s_rel.sem, 1)
            s_ct.wait(e, 1)
            e.activation(ckv[:, :, :].rearrange("p n c -> p (n c)"), PS[:, 6, :], ACT.Copy)\
                .then_inc(s_ce.sem, 1)

        s_la = sig("m2_decay")

        @on("dve")
        def _(e):
            s_root2.wait(e, 1)
            e.reciprocal(norm_r[:, :], norm_r[:, :])
            e.drain()
            e.scalar_tensor_tensor(out=ckvT[:, :], in0=ckvT[:, :], scalar=c_("ckv_n"),
                                   in1=norm_r[:, :], op0=ALU.mult, op1=ALU.mult).then_inc(s_cn.sem, 1)
            s_ax.wait(e, 1)
            la2, ex2 = (x.rearrange("p h s -> p (h s)") for x in (la[:, :, :], ex))
            e.scalar_tensor_tensor(out=la2, in0=la2, scalar=0.0, in1=ex2, op0=ALU.min,
                                   op1=ALU.subtract)
            e.drain()
            e.tensor_scalar(la2, la2, 1.0 / 16, None, ALU.mult).then_inc(s_la.sem, 1)
            s_hd.wait(e, 8)
            for x, (n, h) in enumerate(combos):
                e.drain()
                s_rel.wait(e, x + 1)
                sc_, r_ = score[:, n, 0:(n + 1) * P], rel[:, x % 2, 0:(n + 1) * P]
                if h == 0:
                    e.tensor_scalar(sc_, r_, iw[:, n, 0:1], None, ALU.mult).then_inc(s_acc.sem, 1)
                else:
                    e.scalar_tensor_tensor(out=sc_, in0=r_, scalar=iw[:, n, h:h + 1], in1=sc_,
                                           op0=ALU.mult, op1=ALU.add).then_inc(s_acc.sem, 1)
            e.drain()
            s_in.wait(e, 48)
            for n in range(1, NB):
                d = score[:, n, n * P:(n + 1) * P]
                e.tensor_tensor(d, d, tri[:, :], ALU.add)
            with e.Fori(0, SEL // 8):
                e.drain()
                for n in range(1, NB):
                    e.max(i8[:, n - 1, :], score[:, n, 0:(n + 1) * P])
                e.drain()
                for n in range(1, NB):
                    w = score[:, n, 0:(n + 1) * P]
                    e.match_replace(w, i8[:, n - 1, :], w, TAKEN)
            e.drain()
            e.tensor_copy(sel[:, 0, 0:P], tri[:, :])
            for n in range(1, NB):
                e.tensor_scalar(sel[:, n, 0:(n + 1) * P], score[:, n, 0:(n + 1) * P], TAKEN / 2, NEG,
                                ALU.is_gt, ALU.mult)
            e.drain()

        s_ax_n = 1
        on("pe")(lambda e: s_ax.wait(e, s_ax_n))
        pe_gemm("gqk", 2 * GH, lambda k: H[:, k, :])
        n_qk = START["gqk"]
        qk_base = evac_act.plan(2 * GH)

        @on("act")
        def _(e):
            with e.Fori(0, 2) as i:
                for r in range(4):
                    slot_done.wait(e, i * 4 + (n_qk + r + 1))
                    e.activation(tile(qk, i * 4 + r), PS[:, r, :], ACT.Copy,
                                 scale=1.0 if r % 2 else P ** -0.5).then_inc(evac_act.sem, 1)
        nv = START["gv"]
        v_base = evac_act.plan(8)
        s_ce_n = 1

        @on("pe")
        def _(e):
            evac_act.wait(e, v_base)
            s_ce.wait(e, s_ce_n)
            for c in range(2):
                for kp in range(4):
                    w = use_slot(e, nv, 0, 4, 4 * c + kp).rearrange("p (k c) -> p k c", k=2)
                    for k in range(2):
                        for n in range(NB):
                            mm = e.matmul(PS[:, 4 * c + n, :], H[:, 2 * kp + k, n * P:(n + 1) * P],
                                          w[:, k, :], start=kp == 0 and k == 0, stop=kp == 3 and k == 1)
                    mm.then_inc(slot_done.sem, 1)

        @on("act")
        def _(e):
            for c in range(2):
                slot_done.wait(e, nv + 4 * c + 4)
                for n in range(NB):
                    e.activation(v[:, n, c * 512:(c + 1) * 512], PS[:, 4 * c + n, :], ACT.Copy)\
                        .then_inc(evac_act.sem, 1)

        b = sb(gl, "log_decay_sum", [P, S])
        dd = sb(gl, "decay_diff", [P, 2, S])
        E = sb(gl, "decay", [P, 2, S])
        ql, kl = sb(gl, "q_level", [P, 2, S]), sb(gl, "k_level", [P, 2, S])
        acc = sb(gl, "gla_scores_T", [P, S])
        qe = sb(gl, "q_decayed", [P, S])
        kdT = sb(gl, "k_decayed", [P, NB, P])
        St = sb(gl, "state", [P, 3, GDV])
        ot = sb(gl, "gla_o", [P, NB, GDV])
        gs = sb(gl, "gla_stats", [P, 3, NB])
        names = ("b", "diff", "exp", "q", "k", "scores", "picked", "el", "kd", "kdT", "kd_out", "kv",
                 "state", "o", "square", "root", "o_norm", "oT", "o_out")
        (s_b, s_d, s_e, s_q, s_k, s_s, s_p, s_el, s_kd, s_kt, s_ko, s_kv, s_st, s_o, s_os, s_or,
         s_on, s_ot, s_oo) = [sig("gla_" + x) for x in names]
        nw = START["wide2"]
        w_base = evac_act.plan(32)
        LV = 7

        @on("pe")
        def _(e):
            evac_act.wait(e, v_base + 8)

            def gemm(h, r):
                w = tiles_of(use_slot(e, nw, h, 8, r))
                evac_act.wait(e, h * 8 + (w_base + r - 1))
                for k in range(KT):
                    mm = e.matmul(PS[:, 6 + r % 2, :], w[:, k, :], H[:, k, :], start=k == 0,
                                  stop=k == KT - 1)
                mm.then_inc(slot_done.sem, 1)

            with e.Fori(0, GH) as h:
                for l in range(LV + 1):
                    if l < LV:
                        gemm(h, l)
                    s_q.wait(e, h * (LV + 1) + (l + 1))
                    s_k.wait(e, h * (LV + 1) + (l + 1))
                    if l >= 2:
                        s_p.wait(e, h * (LV + 1) + (l - 1))
                    elif True:
                        s_p.wait(e, h * (LV + 1))
                    for n in range(NB):
                        t = slice(n * P, (n + 1) * P)
                        mm = e.matmul(PS[:, l % 2, t], kl[:, l % 2, t], ql[:, l % 2, t],
                                      start=True, stop=True)
                    mm.then_inc(s_s.sem, 1)
                s_kd.wait(e, h + 1)
                for n in range(NB):
                    mm = e.transpose(PS[:, 4, n * P:(n + 1) * P], dd[:, 1, n * P:(n + 1) * P], ident)
                mm.then_inc(s_kt.sem, 1)
                gemm(h, 7)
                s_ko.wait(e, h + 1)
                for n in range(NB - 1):
                    mm = e.matmul(PS[:, 2 + n // 2, (n % 2) * GDV:(n % 2 + 1) * GDV], kdT[:, n, :],
                                  v[:, n, bass.ds(h * GDV, GDV)], start=True, stop=True)
                mm.then_inc(s_kv.sem, 1)
                s_st.wait(e, h + 1)
                for n in range(NB):
                    o_ = PS[:, 4 + n // 2, (n % 2) * GDV:(n % 2 + 1) * GDV]
                    mm = e.matmul(o_, acc[:, n * P:(n + 1) * P], v[:, n, bass.ds(h * GDV, GDV)],
                                  start=True, stop=n == 0)
                    if n:
                        mm = e.matmul(o_, qe[:, n * P:(n + 1) * P], St[:, n - 1, :], start=False,
                                      stop=True)
                mm.then_inc(s_o.sem, 1)
                s_on.wait(e, h + 1)
                for j in range(2):
                    for n in range(NB):
                        mm = e.transpose(PS[:, 2 + j, n * P:(n + 1) * P],
                                         ot[:, n, j * P:(j + 1) * P], ident)
                mm.then_inc(s_ot.sem, 1)

        @on("dve")
        def _(e):
            s_la.wait(e, 1)
            with e.Fori(0, GH) as h:
                e.drain()
                for n in range(NB):
                    t = slice(n * P, (n + 1) * P)
                    e.tensor_tensor_scan(dd[:, 0, t], view(c_("one"), [0, P]), la[:, bass.ds(h, 1), t]
                                         .rearrange("p a s -> p (a s)"), 0.0, ALU.mult, ALU.add)
                e.drain()
                e.tensor_copy(b[:, :], dd[:, 0, :]).then_inc(s_b.sem, 1)
                e.memset(acc[:, :], 0.0)
                e.drain()

                def diff(l):
                    half = 64 >> l
                    nb = S // (2 * half)
                    e.tensor_tensor(view(dd[:, l % 2, :], [2 * half, nb], [1, 2 * half]),
                                    view(b[:, :], [2 * half, nb], [1, 2 * half]),
                                    view(b[:, half - 1:half], [2 * half, nb], [0, 2 * half]),
                                    ALU.subtract).then_inc(s_d.sem, 1)

                def pick(l):
                    e.drain()
                    s_s.wait(e, h * (LV + 1) + (l + 1))
                    held(e)
                    e.copy_predicated(acc[:, :].rearrange("p (n t) -> p n t", n=NB),
                                      view(lmask[:, l, :].bitcast(I32), [0, NB], [1, P]),
                                      PS[:, l % 2, :].rearrange("p (n t) -> p n t", n=NB))\
                        .then_inc(s_p.sem, 1)
                diff(0)
                for l in range(LV):
                    if l + 1 < LV:
                        diff(l + 1)
                    s_e.wait(e, h * LV + (l + 1))
                    e.tensor_tensor(ql[:, l % 2, :], tile(qk, h * 2), E[:, l % 2, :], ALU.mult)\
                        .then_inc(s_q.sem, 1)
                    if l:
                        pick(l - 1)
                e.drain()
                e.tensor_copy(ql[:, LV % 2, :], tile(qk, h * 2)).then_inc(s_q.sem, 1)
                e.tensor_tensor(dd[:, 0, :].rearrange("p (n t) -> p n t", n=NB),
                                view(b[:, P - 1:P], [P, NB], [0, P]),
                                b[:, :].rearrange("p (n t) -> p n t", n=NB), ALU.subtract)\
                    .then_inc(s_d.sem, 1)
                pick(LV - 1)
                s_el.wait(e, h + 1)
                e.tensor_tensor(qe[:, :], tile(qk, h * 2), E[:, 0, :], ALU.mult)
                e.tensor_tensor(dd[:, 1, :], tile(qk, h * 2 + 1), E[:, 1, :], ALU.mult)\
                    .then_inc(s_kd.sem, 1)
                e.drain()
                pick(LV)
                s_kv.wait(e, h + 1)
                e.tensor_copy(St[:, 0, :], PS[:, 2, 0:GDV])
                for n in range(1, NB - 1):
                    e.drain()
                    ins = e.scalar_tensor_tensor(
                        out=St[:, n, :], in0=St[:, n - 1, :], scalar=gs[:, 0, n:n + 1],
                        in1=PS[:, 2 + n // 2, (n % 2) * GDV:(n % 2 + 1) * GDV],
                        op0=ALU.mult, op1=ALU.add)
                ins.then_inc(s_st.sem, 1)
                s_or.wait(e, h + 1)
                e.reciprocal(gs[:, 2, :], gs[:, 2, :])
                e.drain()
                for n in range(NB):
                    ins = e.tensor_scalar(ot[:, n, :], PS[:, 4 + n // 2, (n % 2) * GDV:(n % 2 + 1) * GDV],
                                          gs[:, 2, n:n + 1], None, ALU.mult)
                ins.then_inc(s_on.sem, 1)
                s_ot.wait(e, h + 1)
                for j in range(2):
                    e.tensor_scalar(tile(qk, h * 2 + j), PS[:, 2 + j, :], cd("gla_n", h * 2 + j), None,
                                    ALU.mult).then_inc(s_oo.sem, 1)

        @on("pool")
        def _(e):
            with e.Fori(0, GH) as h:
                for l in range(LV):
                    s_e.wait(e, h * LV + (l + 1))
                    if l >= 2:
                        s_s.wait(e, h * (LV + 1) + (l - 1))
                    held(e)
                    e.tensor_tensor(kl[:, l % 2, :], tile(qk, h * 2 + 1), E[:, l % 2, :], ALU.mult)\
                        .then_inc(s_k.sem, 1)
                s_s.wait(e, h * (LV + 1) + LV - 1)
                held(e)
                e.tensor_copy(kl[:, LV % 2, :], tile(qk, h * 2 + 1)).then_inc(s_k.sem, 1)

        @on("act")
        def _(e):
            def gate(h, r):
                slot_done.wait(e, h * 8 + (nw + r + 1))
                e.activation(tile(wide, h * 8 + r), PS[:, 6 + r % 2, :], ACT.Copy)\
                    .then_inc(evac_act.sem, 1)

            with e.Fori(0, GH) as h:
                for l in range(LV):
                    s_d.wait(e, h * (LV + 1) + (l + 1))
                    if l >= 2:
                        s_q.wait(e, h * (LV + 1) + (l - 1))
                        s_k.wait(e, h * (LV + 1) + (l - 1))
                    e.activation(E[:, l % 2, :], dd[:, l % 2, :], ACT.Abs)
                    e.drain()
                    e.activation(E[:, l % 2, :], E[:, l % 2, :], ACT.Exp, scale=-1.0)\
                        .then_inc(s_e.sem, 1)
                    gate(h, l)
                s_d.wait(e, h * (LV + 1) + (LV + 1))
                s_q.wait(e, h * (LV + 1) + LV)
                s_k.wait(e, h * (LV + 1) + LV)
                e.activation(E[:, 0, :], b[:, :], ACT.Exp)
                e.activation(E[:, 1, :], dd[:, 0, :], ACT.Exp)
                e.activation(gs[:, 0, :], view(b[:, P - 1:P], [P, NB]), ACT.Exp).then_inc(s_el.sem, 1)
                s_kt.wait(e, h + 1)
                e.activation(kdT[:, :, :].rearrange("p n k -> p (n k)"), PS[:, 4, :], ACT.Copy)\
                    .then_inc(s_ko.sem, 1)
                gate(h, 7)
                s_o.wait(e, h + 1)
                for n in range(NB):
                    e.activation(ot[:, n, :], PS[:, 4 + n // 2, (n % 2) * GDV:(n % 2 + 1) * GDV],
                                 ACT.Square, accum_out=gs[:, 1, n:n + 1])
                e.drain()
                e.activation(gs[:, 2, :], gs[:, 1, :], ACT.Sqrt, scale=1.0 / GDV, bias=c_("eps"))\
                    .then_inc(s_or.sem, 1)
        barrier()
        gl.close()

        ds_ = ExitStack()
        OFF = [P, 0, 2 * P, 0]
        LB = [1, 2, 1, 0]
        LO = [0, P, 3 * P, 6 * P, 10 * P]
        OFF = [0, 0, P, 0]
        bias = sb(ds_, "bias_by_distance", [P, DH, S])
        hot = sb(ds_, "bucket_one_hot", [32, 640])
        rb_ = sb(ds_, "rel_bias", [32, DH])
        rows_ = sb(ds_, "bias_rows", [DH, 640])
        qs = sb(ds_, "dq_static", [P, S])
        BS = sb(ds_, "bias_and_selection", [P, 10 * P])
        L = sb(ds_, "dsa_logits", [P, 10 * P])
        pT = sb(ds_, "dsa_probs_T", [P, 10, P])
        dst_ = sb(ds_, "dsa_stats", [P, 3, NB])
        staged = [x[:, j * S:(j + 1) * S] for x in (BS, L) for j in range(2)]
        staged += [pT[:, 4 * j:4 * j + 4, :].rearrange("p c k -> p (c k)") for j in range(2)]
        staged += [norm_sq[:, j, :] for j in range(2)]
        scratch = nc.dram_tensor("bias_rows_dram", (DH, 640), F32, kind="Internal").ap()
        s_rmm, s_row = sig("bias_product"), sig("bias_rows")
        s_rin, s_rdr, s_bias = [sig("bias_" + x).by_dma() for x in ("in", "dram", "tiles")]
        s_turn = sig("bias_turned")
        s_silu, s_og, s_sg = [sig("m2_" + x) for x in ("silu", "o_gated", "sigmoid")]
        (d_qs, d_bs, d_lg, d_l, d_nm, d_ex, d_nrm, d_tr, d_pt, d_pv, d_o) = [sig("dsa_" + x) for x in (
            "q", "bias", "logits", "summed", "max", "exp", "probs", "trans", "probsT", "pv", "out")]
        ng = START["gla_out"]
        y_base = evac_dve.plan(KT)

        @on("act")
        def _(e):
            e.dma_start(hot[:, :], a["buckets"]).then_inc(s_rin.sem, 16)
            e.dma_start(rb_[:, :], a["rel_bias"]).then_inc(s_rin.sem, 16)
            with e.Fori(0, KT) as i:
                e.activation(tile(wide, i + 16), tile(wide, i + 16), ACT.Silu).then_inc(s_silu.sem, 1)
            s_rmm.wait(e, 1)
            for j in range(2):
                e.activation(rows_[:, j * 320:(j + 1) * 320], PS[0:DH, 4 + j, 0:320], ACT.Copy)\
                    .then_inc(s_row.sem, 1)
            s_row.wait(e, 2)
            e.dma_start(scratch, rows_[:, :]).then_inc(s_rdr.sem, 16)
            s_rdr.wait(e, 16)
            for h in range(DH):
                e.dma_start(staged[h], bass.AP(tensor=scratch.tensor, offset=h * 640,
                                               ap=[[1, P], [1, S]])).then_inc(s_bias.sem, 16)
            with e.Fori(0, 2 * KT) as i:
                e.activation(tile(wide, i), tile(wide, i), ACT.Sigmoid).then_inc(s_sg.sem, 1)
            with e.Fori(0, 2) as i:
                for r in range(4):
                    h = i * 4 + r
                    d_nm.wait(e, h + 1)
                    for n in range(NB):
                        seg = L[:, LO[n]:LO[n + 1]]
                        ins = e.activation(seg, seg, ACT.Exp, bias=dst_[:, 0, n:n + 1],
                                           accum_out=dst_[:, 1, n:n + 1])
                    ins.then_inc(d_ex.sem, 1)
                    d_tr.wait(e, h + 1)
                    e.activation(pT[:, :, :].rearrange("p c k -> p (c k)"),
                                 view(PS[:, 4, 0:1], [1, 10 * P]), ACT.Copy).then_inc(d_pt.sem, 1)
                    d_pv.wait(e, h + 1)
                    e.activation(tile(H, h), PS[:, 7, :], ACT.Copy).then_inc(d_o.sem, 1)

        @on("pool")
        def _(e):
            with e.Fori(0, KT) as i:
                s_silu.wait(e, i + 1)
                held(e)
                e.tensor_tensor(tile(qk, i), tile(qk, i), tile(wide, i + 16), ALU.mult)\
                    .then_inc(s_og.sem, 1)
            s_turn.wait(e, DH)
            with e.Fori(0, DH) as h:
                d_lg.wait(e, h)
                held(e)
                e.tensor_copy(qs[:, :], tile(wide, h + 24)).then_inc(d_qs.sem, 1)
                d_l.wait(e, h)
                held(e)
                for n in range(NB):
                    ins = e.tensor_tensor(BS[:, LO[n]:LO[n + 1]],
                                          bias[:, bass.ds(h, 1), 384 - n * P:512]
                                          .rearrange("p a s -> p (a s)"),
                                          sel[:, n, 0:(n + 1) * P], ALU.add)
                ins.then_inc(d_bs.sem, 1)

        @on("pe")
        def _(e):
            s_rin.wait(e, 32)
            for j in range(2):
                mm = e.matmul(PS[0:DH, 4 + j, 0:320], rb_[:, :], hot[:, j * 320:(j + 1) * 320],
                              start=True, stop=True)
            mm.then_inc(s_rmm.sem, 1)
            s_row.wait(e, 2)
            with e.Fori(0, 2) as i:
                for r in range(4):
                    h = i * 4 + r
                    d_qs.wait(e, h + 1)
                    d_l.wait(e, h)
                    for n in range(NB):
                        mm = e.matmul(PS[:, LB[n], OFF[n]:OFF[n] + (n + 1) * P],
                                      qs[:, n * P:(n + 1) * P], ckvT[:, 0:(n + 1) * P],
                                      start=True, stop=True)
                    mm.then_inc(d_lg.sem, 1)
                    w = tiles_of(use_slot(e, ng, i, 4, r))
                    if r == 0:
                        s_og.wait(e, KT)
                    evac_dve.wait(e, h + y_base)
                    for k in range(KT):
                        mm = e.matmul(PS[:, 3, :], w[:, k, :], qk[:, k, :], start=k == 0,
                                      stop=k == KT - 1)
                    mm.then_inc(slot_done.sem, 1)
                    d_nrm.wait(e, h + 1)
                    c = 0
                    for n in range(NB):
                        for kb in range(n + 1):
                            mm = e.transpose(view(PS[:, 4, c * P:c * P + 1], [1, P]) if c < 4 else
                                             PS[:, 4 + c // 4, (c % 4) * P:(c % 4 + 1) * P],
                                             L[:, c * P:(c + 1) * P], ident)
                            c += 1
                    mm.then_inc(d_tr.sem, 1)
                    d_pt.wait(e, h + 1)
                    d_o.wait(e, h)
                    c = 0
                    for n in range(NB):
                        for kb in range(n + 1):
                            mm = e.matmul(PS[:, 7, n * P:(n + 1) * P], ckv[:, kb, :], pT[:, c, :],
                                          start=kb == 0, stop=kb == n)
                            c += 1
                    mm.then_inc(d_pv.sem, 1)

        @on("dve")
        def _(e):
            s_bias.wait(e, 16 * DH)
            for h in range(DH):
                e.tensor_copy(bias[:, h, :], view(staged[h][:, S - 1:S], [-1, S]))\
                    .then_inc(s_turn.sem, 1)
            e.drain()
            with e.Fori(0, 2) as i:
                for r in range(4):
                    h = i * 4 + r
                    d_lg.wait(e, h + 1)
                    d_bs.wait(e, h + 1)
                    d_tr.wait(e, h)
                    for n in range(NB):
                        ins = e.scalar_tensor_tensor(
                            out=L[:, LO[n]:LO[n + 1]], in0=PS[:, LB[n], OFF[n]:OFF[n] + (n + 1) * P],
                            scalar=P ** -0.5, in1=BS[:, LO[n]:LO[n + 1]], op0=ALU.mult, op1=ALU.add)
                    ins.then_inc(d_l.sem, 1)
                    e.drain()
                    for n in range(NB):
                        ins = e.tensor_reduce(dst_[:, 0, n:n + 1], L[:, LO[n]:LO[n + 1]], AX.X,
                                              ALU.max, negate=True)
                    ins.then_inc(d_nm.sem, 1)
                    e.drain()
                    d_ex.wait(e, h + 1)
                    e.reciprocal(dst_[:, 2, :], dst_[:, 1, :])
                    e.drain()
                    for n in range(NB):
                        seg = L[:, LO[n]:LO[n + 1]]
                        ins = e.tensor_scalar(seg, seg, dst_[:, 2, n:n + 1], None, ALU.mult)
                    ins.then_inc(d_nrm.sem, 1)
                    slot_done.wait(e, i * 4 + (ng + r + 1))
                    if r == 0:
                        s_sg.wait(e, 2 * KT)
                    e.tensor_tensor(tile(wide, h), PS[:, 3, :], tile(wide, h), ALU.mult)\
                        .then_inc(evac_dve.sem, 1)

        on("pe")(lambda e: d_o.wait(e, DH))
        pe_gemm("dsa_out", KT, lambda k: H[:, k, :], free=evac_dve)
        merged = evac_dve.n

        def merge(e, t, bank):
            e.tensor_tensor(tile(wide, t + KT), bank, tile(wide, t + KT), ALU.mult)
            e.drain()
            return e.tensor_tensor(tile(wide, t), tile(wide, t + KT), tile(wide, t), ALU.add)
        evacuate("dve", "dsa_out", KT, merge, evac_dve)
        pe_gemm("mix_out", KT, lambda k: wide[:, k, :], (evac_dve, merged), free=evac_dve)
        evac_add("mix_out", KT)
        barrier()
        ds_.close()
        m.close()

    def ple():
        m = ExitStack()
        pT_ = sb(m, "p_T", [P, 2, S])
        pp = sb(m, "p_projected", [P, KT, S])
        gt = sb(m, "ple_gate", [P, KT, S])
        s_pin, s_pp, s_pl = sig("ple_in").by_dma(), sig("ple_proj"), sig("ple_out")
        on("act")(lambda e: e.dma_start(pT_[:, :, :], a["pT"].rearrange("(k p) s -> p k s", p=P))
                  .then_inc(s_pin.sem, 16))
        npj = START["ple_proj"]

        @on("pe")
        def _(e):
            s_pin.wait(e, 16)
            for j in range(2):
                w = use_slot(e, npj, 0, 4, j).rearrange("p (t k c) -> p t k c", t=4, k=2)
                for t in range(4):
                    if j == 1 and t == 3:
                        s_pp.wait(e, 1)
                    for k in range(2):
                        mm = e.matmul(PS[:, (4 * j + t) % 7, :], w[:, t, k, :], pT_[:, k, :],
                                      start=k == 0, stop=k == 1)
                mm.then_inc(slot_done.sem, 1)

        @on("act")
        def _(e):
            for t in range(KT):
                slot_done.wait(e, npj + t // 4 + 1)
                e.activation(pp[:, t, :], PS[:, t % 7, :], ACT.Copy).then_inc(s_pp.sem, 1)
        b_h = rms_norm("ple_n")
        on("pe")(lambda e: s_pp.wait(e, KT))
        pe_gemm("ple_gate", KT, lambda k: H[:, k, :], (s_h, b_h))
        g0 = evac_act.n
        evacuate("act", "ple_gate", KT, lambda e, t, bank: e.activation(tile(gt, t), bank, ACT.Sigmoid),
                 evac_act)
        s_pl.plan(KT)

        @on("dve")
        def _(e):
            e.drain()
            for t in range(KT):
                evac_act.wait(e, g0 + t + 1)
                e.tensor_tensor(gt[:, t, :], gt[:, t, :], pp[:, t, :], ALU.mult)
                e.drain()
                e.tensor_tensor(X[:, t, :], X[:, t, :], gt[:, t, :], ALU.add).then_inc(s_pl.sem, 1)
        rms_norm("final2", ready=(s_pl, 0))
        m.close()

    phases = [mixer1, peer, lambda: ffn(1), mixer2, lambda: ffn(2), ple]
    if start:
        skip_constants()
    for n, f in enumerate(phases):
        if n >= start:
            f()
        if n + 1 == stop:
            return finish(phase.n)
    finish()


def tiles(w, K=KT):
    n = w.shape[1] // P
    return w.reshape(K, P, n, P).transpose(2, 1, 0, 3).reshape(n, P, K * P)


def columns(v):
    return v.reshape(-1, P).T


def stream_parts(i):
    w_in = i["w_in"][0]
    val, gate, q, k, v, gates = (w_in[:, s:e] for s, e in (
        (0, 1024), (1024, 2048), (2048, 3072), (3072, 3200), (3200, 3328), (3328, 5376)))
    yield "glu", np.stack([tiles(gate), tiles(val)], 1).reshape(16, P, D)
    yield "q", tiles(q)
    yield "kv", tiles(np.concatenate([k[:, :64], k[:, :64], k[:, 64:], k[:, 64:], v], 1))
    yield "gates", tiles(gates)
    yield "attn_o", tiles(i["w_attn_o"][0])
    yield "conv_out", tiles(i["w_conv_out"][0])
    yield "w_out", tiles(i["w_out"][0])
    u = i["peer_u"][0].reshape(NKEY, NKEY, KT, P).transpose(1, 3, 2, 0).reshape(NKEY, P, D)
    pq = tiles(i["w_peer_q"][0]).reshape(PH, 2, P, D)
    yield "peer_q_u0", np.concatenate([pq, u[:JQ].reshape(PH, 4, P, D)], 1).reshape(48, P, D)
    v = i["peer_v"][0].reshape(NKEY, NQ, JQ // 2, 2, 2, D // 2).transpose(1, 4, 2, 0, 3, 5)
    for q_ in range(NQ):
        if q_:
            yield f"u{q_}", u[q_ * JQ:(q_ + 1) * JQ]
        yield f"v{q_}", v[q_].reshape(JQ, P, D)


def stream_parts2(i):
    for n in (1, 2):
        w = i[f"ffn{n}_w_in_2"][0]
        yield f"f{n}_in", np.stack([tiles(w[:, :FT * P]), tiles(w[:, FT * P:])], 1).reshape(-1, P, D)
        yield f"f{n}_out", i[f"ffn{n}_w_out_2"][0].reshape(FT, P, D)
    w = i["mix_w_in_2"][0]
    at = np.cumsum([0, 512, 512, 1024, 1024, 16, 1024, 128, 512, 64, 8, 2048])
    gq, gk, gv, gr, ga, dq, dkv, iq, ik, iw, gates = (w[:, s:e] for s, e in zip(at[:-1], at[1:]))
    yield "misc", tiles(np.concatenate([ga, iw, np.zeros((D, P - 24), np.float32)], 1))
    yield "ik", tiles(np.concatenate([ik, ik], 1))
    yield "iq", tiles(iq)
    yield "dkv", tiles(dkv)
    yield "gqk", np.stack([tiles(gq), tiles(gk)], 1).reshape(8, P, D)
    yield "gv", gv.reshape(4, 2, P, 2, 512).transpose(3, 0, 2, 1, 4).reshape(8, P, D)
    yield "wide2", tiles(np.concatenate([gates, gr, dq], 1))
    yield "gla_out", tiles(i["gla_w_out_2"][0])
    yield "dsa_out", tiles(i["dsa_w_out_2"][0])
    yield "mix_out", tiles(i["mix_w_out_2"][0])
    yield "ple_proj", i["ple_w_proj_2"][0].reshape(2, P, 2, 4, P).transpose(2, 1, 3, 0, 4).reshape(2, P, D)
    yield "ple_gate", tiles(i["ple_w_gate_2"][0])


def level_masks():
    s_, t_ = np.arange(P)[:, None], np.arange(P)[None]
    m_ = [(s_ // (2 * h) == t_ // (2 * h)) & (s_ % (2 * h) < h) & (t_ % (2 * h) >= h)
          for h in (64 >> l for l in range(7))]
    return np.stack(m_ + [s_ == t_], 1).astype(np.float32)


def bucket_rows():
    dist = np.maximum(np.arange(640) - (P - 1), 0)
    large = 16 + (np.log(np.maximum(dist, 1) / 16.0) / np.log(8.0) * 16).astype(np.int32)
    bucket = np.where(dist < 16, dist, np.minimum(large, 31))
    return (np.arange(32)[:, None] == bucket[None]).astype(np.float32)


def lay_out(i):
    stream = np.zeros((SLOTS, P, D), np.float32)
    for name, part in [*stream_parts(i), *stream_parts2(i)]:
        stream[START[name]:START[name] + len(part)] = part
    b = i["b_in"][0]
    d = np.arange(P)
    rot = np.zeros((P, P), np.float32)
    for m_ in range(P):
        if m_ % 64 < 32:
            rot[m_ + 32, m_] = -1.0
        else:
            rot[m_ - 32, m_] = 1.0
    squares = np.concatenate([np.eye(P), np.full((P, P), 1.0 / D), rot,
                              np.broadcast_to(d, (P, P))], 1).astype(np.float32)
    inv = (10000.0 ** (-(np.arange(32) * 2.0 / HD))).astype(np.float32)
    one = np.ones((P, 1), np.float32)
    cols = {
        "norm1": columns(i["norm1_g"]),
        "b_glu": np.stack([columns(b[1024:2048]), columns(b[:1024])], 2).reshape(P, 16),
        "b_q": columns(b[2048:3072]),
        "b_k": columns(np.concatenate([b[3072:3136], b[3072:3136], b[3136:3200], b[3136:3200]])),
        "b_gates": columns(b[3328:5376]),
        "conv_w": i["conv_w"][0].reshape(TAPS, KT, P).transpose(2, 0, 1).reshape(P, -1),
        "conv_b": columns(i["conv_b"]), "ln_g": columns(i["conv_ln_g"]),
        "ln_b": columns(i["conv_ln_b"]), "norm2": columns(i["norm2_g"]),
        "final1": columns(i["final_g"]), "ffn1_n": columns(i["ffn1_norm_2"]),
        "mix_n": columns(i["mix_norm_2"]), "alpha_b": columns(i["gla_alpha_b_2"]),
        "gla_n": columns(i["gla_out_norm_2"]), "ckv_n": columns(i["ckv_norm_2"]),
        "ffn2_n": columns(i["ffn2_norm_2"]), "ple_n": columns(i["ple_norm_2"]),
        "final2": columns(i["final_norm_2"]), "inv_freq": inv[d % 32][:, None],
        "eps": EPS * one, "half_pi": np.float32(np.pi / 2) * one, "one": one, "zero": 0 * one,
    }
    q, k = np.arange(P)[:, None], np.arange(2 * P)[None]
    rel = q + P - k
    band = (rel >= 0) & (rel < P)
    band = np.stack([band & ((k >= P) | (n > 0)) for n in range(NB)], 1)
    return {
        "alpha_w": i["gla_alpha_w_2"][0], "level_mask": level_masks(),
        "causal": np.where(np.arange(P)[None] <= np.arange(P)[:, None], 0.0, NEG).astype(np.float32),
        "buckets": bucket_rows(), "rel_bias": i["rel_bias_2"], "pT": i["p_2"][0, 0].T,
        "keysT": i["peer_sub_keys"][0].reshape(2 * PH, NKEY, P).transpose(2, 0, 1),
        "xT": i["x"][0].T, "stream": stream,
        "cols": np.concatenate([cols[n] for n, _ in COLS], 1).astype(np.float32),
        "squares": squares, "band_mask": np.where(band, 0.0, NEG).astype(np.float32),
        "positions": i["positions"][0], "sinks": i["attn_sinks"][0], "b_v": b[3200:3328],
    }


def kernel(**inputs):
    import concourse.bacc as bacc
    from concourse.bass_utils import run_bass_kernel_spmd
    arrays = {k: np.ascontiguousarray(v) for k, v in
              lay_out({k: np.asarray(v) for k, v in inputs.items()}).items()}
    nc = bacc.Bacc("TRN2", target_bir_lowering=False, num_devices=1)
    a = {n: nc.dram_tensor("in_" + n, v.shape, mybir.dt.from_np(v.dtype), kind="ExternalInput").ap()
         for n, v in arrays.items()}
    out = nc.dram_tensor("out", (D, S), F32, kind="ExternalOutput").ap()
    build(nc, a, out)
    r = run_bass_kernel_spmd(nc, [{"in_" + n: v for n, v in arrays.items()}], core_ids=[0])
    return np.ascontiguousarray(r.results[0]["out"].T)[None]
```

```python
from contextlib import ExitStack

import numpy as np
import concourse.bass as bass
from concourse import mybir

F32 = mybir.dt.float32
BF16 = mybir.dt.bfloat16
F32R = mybir.dt.float32r
I32 = mybir.dt.int32
U32 = mybir.dt.uint32
ALU = mybir.AluOpType
ACT = mybir.ActivationFunctionType
AX = mybir.AxisListType

P = 128
S = 512
D = 1024
KT = D // P
NB = S // P
TAPS = 31
HEADS, HD = 16, 64
PH, NKEY, TOPK = 8, 128, 16
NQ = 8
JQ = NKEY // NQ
FT = 2816 // P
GH, GDV = 4, 256
DH = 8
SEL = 128
EPS = 1e-6
NEG = -1e30
TAKEN = -3e38
RING = 4
THREE = ((0, 0), (0, 1), (1, 0))
TWO_PI = 6.283185307179586
MAGIC = 12582912.0

STREAM = [
    ("glu", 16), ("q", 8), ("kv", 3), ("gates", 16), ("attn_o", 8), ("conv_out", 8), ("w_out", 8),
    ("peer_q_u0", 32), ("u1", 16),
    *[(f"{kind}{q_ + 2 * (kind == 'u')}", 16) for q_ in range(6) for kind in "vu"],
    ("v6", 16), ("v7", 16),
    ("f1_in", 44), ("f1_out", 22),
    ("misc", 1), ("ik", 1), ("iq", 4), ("dkv", 1), ("gqk", 8), ("gv", 8), ("wide2", 32),
    ("gla_out", 8), ("dsa_out", 8), ("mix_out", 8),
    ("f2_in", 44), ("f2_out", 22), ("ple_proj", 2), ("ple_gate", 8),
]
START = {}
SLOTS = 0
for _name, _k in STREAM:
    START[_name] = SLOTS
    SLOTS += _k

COLS = [
    ("norm1", 8), ("b_glu", 16), ("b_q", 8), ("b_k", 2), ("b_gates", 16), ("conv_w", 8 * TAPS),
    ("conv_b", 8), ("ln_g", 8), ("ln_b", 8), ("norm2", 8), ("final1", 8), ("ffn1_n", 8),
    ("mix_n", 8), ("alpha_b", 4), ("gla_n", 8), ("ckv_n", 1), ("ffn2_n", 8), ("ple_n", 8),
    ("final2", 8), ("inv_freq", 1), ("eps", 1), ("half_pi", 1), ("one", 1), ("zero", 1),
]
COL = {}
_n = 0
for _name, _k in COLS:
    COL[_name] = _n
    _n += _k
NCOLS = _n
SQ = {"ident": 0, "mean": 128, "rot": 256, "iota": 384}
MAXD = 639


class Signal:

    def __init__(self, nc, ctx, name):
        self.sem = ctx.enter_context(nc.semaphore(name))
        self.n = 0
        self.first = 1

    def by_dma(self):
        self.first = 0
        return self

    def plan(self, k):
        base = self.n
        self.n += k
        return base

    def wait(self, e, value):
        e.wait_ge(self.sem, value + self.first)


def build(nc, a, out, stop=99, start=0):
    ctx = ExitStack()
    queues = {"pe": [], "act": [], "dve": [], "pool": [], "sp": []}

    def on(engine):
        def put(f):
            queues[engine].append(f)
            return f
        return put

    def sb(c, name, shape, dt=F32):
        return c.enter_context(nc.sbuf_tensor(name, shape, dt))

    def two_names(c, plain, rounded, shape):
        with ExitStack() as first:
            one = sb(first, plain, shape)
        return one, sb(c, rounded, shape, F32R)

    total = {1: START["peer_q_u0"], 2: START["f1_in"], 3: START["misc"], 4: START["f2_in"],
             5: START["ple_proj"]}.get(stop, SLOTS)
    signals = {}

    def sig(name):
        if name not in signals:
            signals[name] = Signal(nc, ctx, "s_" + name)
        return signals[name]

    def tile(T, t):
        if isinstance(t, int):
            return T[:, t, :]
        return T[:, bass.ds(t, 1), :].rearrange("p a s -> p (a s)")

    def col(T, c):
        return T[:, c:c + 1] if isinstance(c, int) else T[:, bass.ds(c, 1)]

    def view(ap, *dims):
        return bass.AP(tensor=ap.tensor, offset=ap.offset, ap=[ap.ap[0], *[list(d) for d in dims]])

    X = sb(ctx, "x_res", [P, KT, S])
    H, Hh = two_names(ctx, "h_norm", "h_norm_hi", [P, KT, S])
    ring = sb(ctx, "ring", [P, RING, D])
    cst = sb(ctx, "cst", [P, NCOLS])
    sq = sb(ctx, "squares_const", [P, 512])
    norm_sq = sb(ctx, "norm_sq", [P, 2, S])
    norm_r = sb(ctx, "norm_r", [P, S])
    PS = ctx.enter_context(nc.psum_tensor("ps", [P, 8, 512], F32))
    ident = sq[:, SQ["ident"]:SQ["ident"] + P]
    mean = sq[:, SQ["mean"]:SQ["mean"] + P]
    rot = sq[:, SQ["rot"]:SQ["rot"] + P]
    iota = sq[:, SQ["iota"]:SQ["iota"] + P]

    def c_(name, i=0):
        return cst[:, COL[name] + i:COL[name] + i + 1]

    def cd(name, i):
        return col(cst, i + COL[name])

    arrive = [ctx.enter_context(nc.semaphore(f"s_slot{r}")) for r in range(RING)]
    slot_done = sig("slot_done")
    s_const = sig("const").by_dma()
    evac_act = sig("evac_act")
    evac_dve = sig("evac_dve")
    phase = sig("phase")

    on("act")(lambda e: e.sem_inc(evac_act.sem, 4))
    on("dve")(lambda e: e.sem_inc(evac_dve.sem, 4))
    evac_act.n = evac_dve.n = 4
    glu_gate = sig("glu_gate")
    glu_done = sig("glu_done")
    on("dve")(lambda e: e.sem_inc(glu_done.sem, 2))
    glu_done.n = 2
    slot_done.n = 0

    @on("sp")
    def _(e):
        e.dma_start(cst[:, :], a["cols"]).then_inc(s_const.sem, 16)
        e.dma_start(X[:, :, :], a["xT"].rearrange("(k p) s -> p k s", p=P)).then_inc(s_const.sem, 16)
        e.dma_start(sq[:, :], a["squares"]).then_inc(s_const.sem, 16)
        for r in range(RING):
            e.dma_start(ring[:, r, :], a["stream"][r]).then_inc(arrive[r], 16)
        with e.Fori(1, total // RING) as i:
            for r in range(RING):
                slot_done.wait(e, (i - 1) * RING + r + 1)
                e.dma_start(ring[:, r, :], a["stream"][i * RING + r]).then_inc(arrive[r], 16)
        for n in range(total // RING * RING, total):
            slot_done.wait(e, n - RING + 1)
            e.dma_start(ring[:, n % RING, :], a["stream"][n]).then_inc(arrive[n % RING], 16)
    CONST_IN = 48

    s_held = sig("held")

    def held(e):
        e.sem_inc(s_held.sem, 1)

    def skip_constants():
        for name in ("pe", "act", "dve", "pool"):
            on(name)(lambda e: s_const.wait(e, CONST_IN))

    def barrier():
        phase.plan(4)
        want = phase.n
        for name in ("pe", "act", "dve", "pool"):
            def f(e):
                e.drain().then_inc(phase.sem, 1)
                phase.wait(e, want)
            on(name)(f)

    def use_slot(e, n0, i, per, r):
        n = n0 + r
        e.wait_ge(arrive[n % RING], i * (16 * per // RING) + 16 * (n // RING + 1))
        return ring[:, n % RING, :]

    def tiles_of(slot):
        return slot.rearrange("p (k c) -> p k c", k=KT)

    s_hi, s_lo = sig("slot_hi"), sig("slot_lo")

    class Split:

        def __init__(self, m, name, first, count, buffers=RING):
            self.parts = sb(m, name, [P, buffers, 2, D], F32R)
            self.buffers = buffers
            self.base = s_hi.plan(count) - first
            s_lo.plan(count)

        def hi(self, e, i, per, n):
            b = n % self.buffers
            e.wait_ge(arrive[n % RING], i * (16 * per // RING) + 16 * (n // RING + 1))
            slot_done.wait(e, i * per + (n - self.buffers + 1))
            e.activation(self.parts[:, b, 0, :], ring[:, n % RING, :], ACT.Copy)\
                .then_inc(s_hi.sem, 1)

        def lo(self, e, i, per, n):
            b = n % self.buffers
            s_hi.wait(e, i * per + (n + self.base + 1))
            held(e)
            e.tensor_tensor(self.parts[:, b, 1, :], ring[:, n % RING, :],
                            self.parts[:, b, 0, :].bitcast(F32), ALU.subtract).then_inc(s_lo.sem, 1)

        def use(self, e, i, per, n):
            s_lo.wait(e, i * per + (n + self.base + 1))
            return [tiles_of(self.parts[:, n % self.buffers, v, :]) for v in range(2)]

        def lows(self, first, count):
            @on("pool")
            def _(e):
                self.loop(e, self.lo, first, count)

        def loop(self, e, f, first, count):
            if count >= 8:
                with e.Fori(0, count // 4) as i:
                    for r in range(4):
                        f(e, i, 4, first + r)
                first, count = first + count // 4 * 4, count % 4
            for r in range(count):
                f(e, 0, 4, first + r)

    def product3(e, psum, w, k, x, start, stop):
        for v, (a_, b_) in enumerate(THREE):
            mm = e.matmul(psum, w[a_][:, k, :], x[b_], start=start and v == 0, stop=stop and v == 2)
        return mm

    def pe_gemm(name, n, rhs, first_wait=None, free=evac_act, banks=(0, 1, 2, 3)):
        n0 = START[name]
        fbase = free.n
        others = [(s, s.n) for s in (evac_act, evac_dve, glu_done)]

        def one(e, i, r):
            w = tiles_of(use_slot(e, n0, i, 4, r))
            free.wait(e, i * 4 + (fbase + r - 3))
            for k in range(KT):
                if first_wait and isinstance(i, int) and i == 0 and r == 0:
                    first_wait[0].wait(e, first_wait[1] + k + 1)
                m = e.matmul(PS[:, banks[r], :], w[:, k, :], rhs(k), start=k == 0, stop=k == KT - 1)
            m.then_inc(slot_done.sem, 1)

        @on("pe")
        def _(e):
            for s, v in others:
                s.wait(e, v)
            for r in range(min(4, n)):
                one(e, 0, r)
            if n >= 8:
                with e.Fori(1, n // 4) as i:
                    for r in range(4):
                        one(e, i, r)
        return n0

    def evacuate(engine, name, n, op, done, before=None, banks=(0, 1, 2, 3)):
        n0 = START[name]
        done.plan(n)

        @on(engine)
        def _(e):
            if before:
                before(e)

            def one(i, r):
                slot_done.wait(e, i * 4 + (n0 + r + 1))
                op(e, i * 4 + r, PS[:, banks[r], :]).then_inc(done.sem, 1)
            if n < 8:
                for r in range(n):
                    one(0, r)
            else:
                with e.Fori(0, n // 4) as i:
                    for r in range(4):
                        one(i, r)

    s_sq, s_sqmm, s_root, s_h = sig("norm_sq"), sig("norm_mm"), sig("norm_root"), sig("norm_h")
    s_inv = sig("norm_inv")

    s_nh, s_np = sig("norm_hi"), sig("norm_product")

    def rms_norm(gain, dst=H, bank=7, ready=None, split=None):
        b_sq, b_mm, b_root, b_h, b_inv = (s_sq.plan(KT), s_sqmm.plan(KT), s_root.plan(1),
                                          s_h.plan(KT), s_inv.plan(1))
        if split:
            b_np, b_nh = s_np.plan(KT), s_nh.plan(KT)

        @on("act")
        def _(e):
            for k in range(KT):
                if ready:
                    ready[0].wait(e, ready[1] + k + 1)
                if k >= 2:
                    s_sqmm.wait(e, b_mm + k - 1)
                elif b_mm:
                    s_sqmm.wait(e, b_mm)
                e.activation(norm_sq[:, k % 2, :], X[:, k, :], ACT.Square).then_inc(s_sq.sem, 1)
            s_sqmm.wait(e, b_mm + KT)
            if b_h:
                s_h.wait(e, b_h)
            e.activation(norm_r[:, :], PS[:, bank, :], ACT.Sqrt, bias=c_("eps")).then_inc(s_root.sem, 1)
            if split:
                for k in range(KT):
                    s_np.wait(e, b_np + k + 1)
                    e.activation(Hh[:, k, :], split[1][:, k % 4, :], ACT.Copy).then_inc(s_nh.sem, 1)

        @on("pe")
        def _(e):
            for k in range(KT):
                s_sq.wait(e, b_sq + k + 1)
                e.matmul(PS[:, bank, :], mean, norm_sq[:, k % 2, :], start=k == 0,
                         stop=k == KT - 1).then_inc(s_sqmm.sem, 1)

        @on("dve")
        def _(e):
            s_root.wait(e, b_root + 1)
            e.reciprocal(norm_r[:, :], norm_r[:, :]).then_inc(s_inv.sem, 1)
            s_inv.wait(e, b_inv + 1)
            if split:
                low, t = split
                for k in range(KT + 1):
                    if k < KT:
                        e.scalar_tensor_tensor(out=t[:, k % 4, :], in0=X[:, k, :], scalar=c_(gain, k),
                                               in1=norm_r[:, :], op0=ALU.mult, op1=ALU.mult)\
                            .then_inc(s_np.sem, 1)
                    if k:
                        s_nh.wait(e, b_nh + k)
                        e.tensor_tensor(low[:, k - 1, :], t[:, (k - 1) % 4, :],
                                        Hh[:, k - 1, :].bitcast(F32), ALU.subtract).then_inc(s_h.sem, 1)
                return
            for k in range(KT):
                e.scalar_tensor_tensor(out=dst[:, k, :], in0=X[:, k, :], scalar=c_(gain, k),
                                       in1=norm_r[:, :], op0=ALU.mult, op1=ALU.mult).then_inc(s_h.sem, 1)
        return b_h

    def finish(last=None):
        s_out = sig("out").by_dma()
        want = s_h.n if last is None else last

        @on("sp")
        def _(e):
            if last is None:
                s_h.wait(e, want)
                src = H
            else:
                phase.wait(e, want)
                src = X
            e.dma_start(out.rearrange("(k p) s -> p k s", p=P), src[:, :, :]).then_inc(s_out.sem, 16)
            s_out.wait(e, 16)
        go = ctx.enter_context(nc.semaphore("s_go"))
        seeded = [x.sem for x in signals.values() if x.first]
        queues["pool"].insert(0, lambda e: [e.sem_inc(x, 1) for x in seeded + [go]])
        for name in ("pe", "act", "dve"):
            queues[name].insert(0, lambda e: e.wait_ge(go, 1))
        with nc.Block() as block:
            for name, deco in (("sp", block.sync), ("pe", block.tensor), ("act", block.scalar),
                               ("dve", block.vector), ("pool", block.gpsimd)):
                def program(e, name=name):
                    for f in queues[name]:
                        f(e)
                deco(program)
        ctx.close()


    def glu(name, pairs, tmp, act, func, value, first_wait, split=None, low=None):
        n0 = START[name]
        others = [(s, s.n) for s in (evac_act, evac_dve, glu_done)]
        b_gate, b_done = glu_gate.plan(pairs), glu_done.plan(pairs)

        def loop(e, one):
            for r in range(2):
                one(e, 0, r)
            with e.Fori(1, pairs // 2) as i:
                for r in range(2):
                    one(e, i, r)

        @on("pe")
        def _(e):
            for s, v in others:
                s.wait(e, v)

            def one(e, i, r):
                for j in range(2):
                    w = (split.use(e, i, 4, n0 + 2 * r + j) if split else
                         tiles_of(use_slot(e, n0, i, 4, 2 * r + j)))
                    glu_done.wait(e, i * 2 + (b_done + r - 1))
                    for k in range(KT):
                        if isinstance(i, int) and r == 0 and j == 0:
                            first_wait[0].wait(e, first_wait[1] + k + 1)
                        if split:
                            m = product3(e, PS[:, 2 * r + j, :], w, k, (Hh[:, k, :], low[:, k, :]),
                                         k == 0, k == KT - 1)
                            continue
                        m = e.matmul(PS[:, 2 * r + j, :], w[:, k, :], H[:, k, :], start=k == 0,
                                     stop=k == KT - 1)
                    m.then_inc(slot_done.sem, 1)
            loop(e, one)

        @on("act")
        def _(e):
            def one(e, i, r):
                if split:
                    split.hi(e, i, 4, n0 + 2 * r + 2)
                slot_done.wait(e, i * 4 + (n0 + 2 * r + 1))
                glu_done.wait(e, i * 2 + (b_done + r - 1))
                act(e, i * 2 + r, tmp[:, r, :], PS[:, 2 * r, :], func).then_inc(glu_gate.sem, 1)
                if split:
                    split.hi(e, i, 4, n0 + 2 * r + 3)
            loop(e, one)

        @on("dve")
        def _(e):
            def one(e, i, r):
                slot_done.wait(e, i * 4 + (n0 + 2 * r + 2))
                glu_gate.wait(e, i * 2 + (b_gate + r + 1))
                value(e, i * 2 + r, PS[:, 2 * r + 1, :], tmp[:, r, :]).then_inc(glu_done.sem, 1)
            loop(e, one)

    def evac_add(name, n, scale=1.0):
        def op(e, t, bank):
            return e.scalar_tensor_tensor(out=tile(X, t), in0=bank, scalar=scale, in1=tile(X, t),
                                          op0=ALU.mult, op1=ALU.add)
        evacuate("dve", name, n, op, evac_dve)

    def mixer1():
        m = ExitStack()
        U = sb(m, "conv_in", [P, KT, TAPS - 1 + S])
        Y = sb(m, "conv_out", [P, KT, S])
        Q = sb(m, "q_raw", [P, KT, S])
        O = sb(m, "attn_T", [P, KT, S])
        G = sb(m, "gates", [P, 2 * KT, S])
        kz = sb(m, "k_padded", [P, 4, P + S])
        V = sb(m, "v_tokens", [P, NB + 1, P])
        cos, sin = sb(m, "cos", [P, S]), sb(m, "sin", [P, S])
        M = sb(m, "band_mask", [P, NB, 2 * P])
        qr = sb(m, "q_roped", [P, 2, S])
        Sb = sb(m, "scores", [P, 2, NB, 2 * P])
        pT = sb(m, "probs_T", [P, 2, 2 * NB, P])
        ra, rb = sb(m, "rope_a", [P, S]), sb(m, "rope_b", [P, S])
        osb = sb(m, "o_tokens", [P, NB, P])
        sinks = sb(m, "sinks", [P, HEADS])
        bv = sb(m, "b_v", [P, P])
        st = sb(m, "stats", [P, 2, 6, NB])
        tmp2 = Sb[:, :, 0:2, :].rearrange("p a b c -> p a (b c)")

        s_in = sig("m1_in").by_dma()

        @on("act")
        def _(e):
            e.dma_start(rb[:, :].bitcast(I32), a["positions"].partition_broadcast(P)).then_inc(s_in.sem, 16)
            e.dma_start(M[:, :, :], a["band_mask"]).then_inc(s_in.sem, 16)
            e.dma_start(sinks[:, :], a["sinks"].partition_broadcast(P)).then_inc(s_in.sem, 16)
            e.dma_start(bv[:, :], a["b_v"].partition_broadcast(P)).then_inc(s_in.sem, 16)
            s_const.wait(e, CONST_IN)

        s_zero = sig("m1_zero")

        @on("pool")
        def _(e):
            e.memset(U[:, :, 0:TAPS - 1], 0.0)
            e.memset(kz[:, :, :], 0.0)
            e.memset(V[:, 0, :], 0.0).then_inc(s_zero.sem, 1)

        on("pe")(lambda e: s_const.wait(e, CONST_IN))
        on("dve")(lambda e: s_const.wait(e, CONST_IN))
        b_h = rms_norm("norm1")

        s_ang, s_trig = sig("m1_angles"), sig("m1_trig")

        @on("dve")
        def _(e):
            s_in.wait(e, 64)
            e.tensor_scalar(ra[:, :], rb[:, :].bitcast(I32), c_("inv_freq"), None, ALU.mult)
            for shift, dst in ((0.0, sin), (0.25, cos)):
                e.drain()
                e.tensor_scalar(dst[:, :], ra[:, :], 1.0 / TWO_PI, shift, ALU.mult, ALU.add)
                e.drain()
                e.tensor_scalar(dst[:, :], dst[:, :], MAGIC, None, ALU.add)
                e.drain()
                e.tensor_scalar(qr[:, 0, :], dst[:, :], MAGIC, None, ALU.subtract)
                e.drain()
                e.scalar_tensor_tensor(out=dst[:, :], in0=qr[:, 0, :], scalar=-6.28125,
                                       in1=ra[:, :], op0=ALU.mult, op1=ALU.add)
                for part in (-1.9350051879882812e-3, -3.01991598195675e-7):
                    e.drain()
                    e.scalar_tensor_tensor(out=dst[:, :], in0=qr[:, 0, :], scalar=part,
                                           in1=dst[:, :], op0=ALU.mult, op1=ALU.add)
                if shift:
                    e.drain()
                    e.tensor_scalar(dst[:, :], dst[:, :], TWO_PI / 4, None, ALU.add)
                e.drain()
                e.tensor_scalar(dst[:, :], dst[:, :], 3.1415925, -3.1415925, ALU.min, ALU.max)\
                    .then_inc(s_ang.sem, 1)

        @on("act")
        def _(e):
            for n, dst in enumerate((sin, cos)):
                s_ang.wait(e, n + 1)
                e.activation(dst[:, :], dst[:, :], ACT.Sin).then_inc(s_trig.sem, 1)

        on("dve")(lambda e: s_zero.wait(e, 1))
        glu("glu", KT, tmp2,
            lambda e, p, t, bank, f: e.activation(t, bank, f, bias=cd("b_glu", p * 2)),
            ACT.Sigmoid,
            lambda e, p, bank, t: e.scalar_tensor_tensor(
                out=(U[:, p, TAPS - 1:] if isinstance(p, int) else
                     U[:, bass.ds(p, 1), TAPS - 1:].rearrange("p a s -> p (a s)")),
                in0=bank, scalar=cd("b_glu", p * 2 + 1), in1=t, op0=ALU.add, op1=ALU.mult),
            (s_h, b_h))

        pe_gemm("q", KT, lambda k: H[:, k, :])
        evacuate("act", "q", KT,
                 lambda e, t, bank: e.activation(tile(Q, t), bank, ACT.Identity, bias=cd("b_q", t)),
                 evac_act)
        q_in = evac_act.n

        n_kv = START["kv"]
        e_act, e_dve = evac_act.n, evac_dve.n
        evac_act.plan(2)
        evac_dve.plan(1)
        s_kr, s_kc, s_kz, s_v = sig("k_rot"), sig("k_cos"), sig("k_done"), sig("v_done")

        @on("pe")
        def _(e):
            evac_act.wait(e, e_act)
            for j in range(2):
                w = tiles_of(use_slot(e, n_kv, 0, 4, j))
                for k in range(KT):
                    mm = e.matmul(PS[:, j, :], w[:, k, :], H[:, k, :], start=k == 0, stop=k == KT - 1)
                mm.then_inc(slot_done.sem, 1)
            w = tiles_of(use_slot(e, n_kv, 0, 4, 2))
            for n in range(NB):
                for k in range(KT):
                    mm = e.matmul(PS[:, 2, n * P:(n + 1) * P], H[:, k, n * P:(n + 1) * P],
                                  w[:, k, :], start=k == 0, stop=k == KT - 1)
            mm.then_inc(slot_done.sem, 1)
            for j in range(2):
                evac_act.wait(e, e_act + j + 1)
                e.matmul(PS[:, 4 + j, :], rot, O[:, j, :], start=True, stop=True).then_inc(s_kr.sem, 1)

        @on("act")
        def _(e):
            for j in range(2):
                slot_done.wait(e, n_kv + j + 1)
                e.activation(O[:, j, :], PS[:, j, :], ACT.Identity, bias=c_("b_k", j))\
                    .then_inc(evac_act.sem, 1)

        @on("pool")
        def _(e):
            s_trig.wait(e, 2)
            for j in range(2):
                evac_act.wait(e, e_act + j + 1)
                e.tensor_tensor(qr[:, j, :], O[:, j, :], cos[:, :], ALU.mult).then_inc(s_kc.sem, 1)

        @on("dve")
        def _(e):
            slot_done.wait(e, n_kv + 3)
            e.tensor_tensor(V[:, 1:, :], PS[:, 2, :].rearrange("p (n c) -> p n c", n=NB),
                            view(bv[:, :], [0, NB], [1, P]), ALU.add).then_inc(evac_dve.sem, 1)
            s_trig.wait(e, 2)
            for j in range(2):
                e.drain()
                s_kr.wait(e, j + 1)
                s_kc.wait(e, j + 1)
                e.tensor_tensor(rb[:, :], PS[:, 4 + j, :], sin[:, :], ALU.mult)
                e.drain()
                for half in range(2):
                    h = slice(64 * half, 64 * half + 64)
                    e.tensor_tensor(kz[h, 2 * j + half, P:], qr[h, j, :], rb[h, :], ALU.add)\
                        .then_inc(s_kz.sem, 1)
            for c in range(KT):
                e.tensor_scalar(Y[:, c, :], U[:, c, 0:S], c_("conv_w", c), c_("conv_b", c),
                                ALU.mult, ALU.add)

        def tap(e, w):
            e.drain()
            for c in range(KT):
                e.scalar_tensor_tensor(out=Y[:, c, :], in0=U[:, c, bass.ds(w, S)],
                                       scalar=cd("conv_w", w * KT + c), in1=Y[:, c, :],
                                       op0=ALU.mult, op1=ALU.add)

        n_g = START["gates"]
        g_base = evac_act.plan(16)
        (s_arot, s_aqc, s_qr, s_sc, s_sm, s_ex, s_tr, s_pt, s_pv, s_on, s_ot, s_oe) = [
            sig("at_" + x) for x in ("rot", "qcos", "qr", "scores", "max", "exp", "trans", "probsT",
                                     "pv", "norm", "oT", "o_out")]

        def tiles_loop(e, one):
            with e.Fori(0, 2) as g:
                with e.Fori(0, 2) as i:
                    for b in range(2):
                        one(g, g * 4 + i * 2 + b, g * 2 + i, b)

        @on("pe")
        def _(e):
            evac_act.wait(e, q_in + 2)
            evac_dve.wait(e, e_dve + 1)
            s_kz.wait(e, 4)

            def gemm(it, b, j, t):
                w = tiles_of(use_slot(e, n_g, it, 4, 2 * b + j))
                evac_act.wait(e, t * 2 + (g_base + j))
                for k in range(KT):
                    mm = e.matmul(PS[:, 7, :], w[:, k, :], H[:, k, :], start=k == 0, stop=k == KT - 1)
                mm.then_inc(slot_done.sem, 1)

            def one(g, t, it, b):
                s_on.wait(e, t * 2)
                e.matmul(PS[:, 6, :], rot, tile(Q, t), start=True, stop=True).then_inc(s_arot.sem, 1)
                gemm(it, b, 0, t)
                s_qr.wait(e, t + 1)
                for h in range(2):
                    (s_oe if h else s_pt).wait(e, t if h else t * 2)
                    for n in range(NB):
                        mm = e.matmul(PS[:, 2 * h + n // 2, (n % 2) * 256:(n % 2) * 256 + 256],
                                      qr[:, b, n * P:(n + 1) * P],
                                      kz[:, bass.ds(g * 2 + h, 1), n * P:(n + 2) * P]
                                      .rearrange("p a s -> p (a s)"), start=True, stop=True)
                    mm.then_inc(s_sc.sem, 1)
                gemm(it, b, 1, t)
                for h in range(2):
                    s_ex.wait(e, t * 2 + (h + 1))
                    for c in range(2 * NB):
                        bank = (0 if h else 4) + c // 4
                        mm = e.transpose(PS[:, bank, (c % 4) * P:(c % 4 + 1) * P],
                                         Sb[:, h, c // 2, (c % 2) * P:(c % 2 + 1) * P], ident)
                    mm.then_inc(s_tr.sem, 1)
                for h in range(2):
                    s_pt.wait(e, t * 2 + (h + 1))
                    for n in range(NB):
                        for c in range(2):
                            mm = e.matmul(PS[:, 3 if h else 6, n * HD:(n + 1) * HD],
                                          pT[:, h, 2 * n + c, :],
                                          V[:, n + c, bass.ds(g * HD, HD)], start=c == 0, stop=c == 1)
                    mm.then_inc(s_pv.sem, 1)
                s_on.wait(e, t * 2 + 2)
                for n in range(NB):
                    mm = e.transpose(PS[:, 2, n * P:(n + 1) * P], osb[:, n, :], ident)
                mm.then_inc(s_ot.sem, 1)
            tiles_loop(e, one)

        @on("pool")
        def _(e):
            s_kz.wait(e, 4)

            def one(g, t, it, b):
                s_qr.wait(e, t)
                e.tensor_tensor(ra[:, :], tile(Q, t), cos[:, :], ALU.mult).then_inc(s_aqc.sem, 1)
            tiles_loop(e, one)

        @on("dve")
        def _(e):
            def one(g, t, it, b):
                e.drain()
                s_arot.wait(e, t + 1)
                e.tensor_tensor(rb[:, :], PS[:, 6, :], sin[:, :], ALU.mult)
                e.drain()
                s_aqc.wait(e, t + 1)
                e.tensor_tensor(qr[:, b, :], ra[:, :], rb[:, :], ALU.add).then_inc(s_qr.sem, 1)
                for h in range(2):
                    s_sc.wait(e, t * 2 + (h + 1))
                    mx, nm, ds = st[:, h, 0, :], st[:, h, 1, :], st[:, h, 2, :]
                    e.scalar_tensor_tensor(
                        out=Sb[:, h, :, :].rearrange("p n k -> p (n k)"),
                        in0=PS[:, 2 * h:2 * h + 2, :].rearrange("p a b -> p (a b)"),
                        scalar=HD ** -0.5, in1=M[:, :, :].rearrange("p n k -> p (n k)"),
                        op0=ALU.mult, op1=ALU.add)
                    e.drain()
                    e.tensor_reduce(mx, Sb[:, h, :, :], AX.X, ALU.max)
                    e.drain()
                    e.tensor_scalar(nm, mx, col(sinks, t * 2 + h), -1.0, ALU.max, ALU.mult)
                    e.drain()
                    e.tensor_scalar(ds, nm, col(sinks, t * 2 + h), None, ALU.add).then_inc(s_sm.sem, 1)
                for h in range(2):
                    tap(e, t * 2 + (h + 1))
                    s_ex.wait(e, t * 2 + (h + 1))
                    e.tensor_tensor(st[:, h, 5, :], st[:, h, 3, :], st[:, h, 4, :], ALU.add)
                    e.drain()
                    e.reciprocal(st[:, h, 5, :], st[:, h, 5, :])
                    e.drain()
                    s_pv.wait(e, t * 2 + (h + 1))
                    if h == 0:
                        s_ot.wait(e, t)
                    e.tensor_tensor(osb[:, :, h * HD:(h + 1) * HD],
                                    PS[:, 3 if h else 6, 0:NB * HD]
                                    .rearrange("p (n c) -> p n c", n=NB),
                                    view(st[:, h, 5, :], [1, NB], [0, HD]), ALU.mult)\
                        .then_inc(s_on.sem, 1)
            tiles_loop(e, one)
            with e.Fori(2 * KT + 1, TAPS) as w:
                tap(e, w)

        @on("act")
        def _(e):
            def gate(t, j):
                slot_done.wait(e, t * 2 + (n_g + j + 1))
                e.activation(tile(G, t * 2 + j), PS[:, 7, :], ACT.Identity, bias=cd("b_gates", t * 2 + j))\
                    .then_inc(evac_act.sem, 1)

            def one(g, t, it, b):
                gate(t, 0)
                for h in range(2):
                    s_sm.wait(e, t * 2 + (h + 1))
                    for n in range(NB):
                        e.activation(Sb[:, h, n, :], Sb[:, h, n, :], ACT.Exp,
                                     bias=st[:, h, 1, n:n + 1], accum_out=st[:, h, 3, n:n + 1])
                    e.activation(st[:, h, 4, :], st[:, h, 2, :], ACT.Exp).then_inc(s_ex.sem, 1)
                gate(t, 1)
                for h in range(2):
                    s_tr.wait(e, t * 2 + (h + 1))
                    s_pv.wait(e, t * 2)
                    bank = 0 if h else 4
                    e.activation(pT[:, h, :, :].rearrange("p c k -> p (c k)"),
                                 PS[:, bank:bank + 2, :].rearrange("p a b -> p (a b)"), ACT.Copy)\
                        .then_inc(s_pt.sem, 1)
                s_ot.wait(e, t + 1)
                e.activation(tile(O, t), PS[:, 2, :], ACT.Copy).then_inc(s_oe.sem, 1)
            tiles_loop(e, one)

        s_ao, s_sg = sig("m1_attn_gated"), sig("m1_sigmoid")

        @on("act")
        def _(e):
            e.drain()
            with e.Fori(0, 2 * KT) as i:
                e.activation(tile(G, i), tile(G, i), ACT.Sigmoid).then_inc(s_sg.sem, 1)
        on("pe")(lambda e: s_oe.wait(e, KT))
        pe_gemm("attn_o", KT, lambda k: O[:, k, :])
        ao = evac_act.n
        evacuate("act", "attn_o", KT,
                 lambda e, t, bank: e.activation(tile(H, t), bank, ACT.Copy), evac_act)

        @on("pool")
        def _(e):
            s_sg.wait(e, 2 * KT)
            with e.Fori(0, KT) as i:
                evac_act.wait(e, i + (ao + 1))
                e.tensor_tensor(tile(H, i), tile(H, i), tile(G, i + KT), ALU.mult).then_inc(s_ao.sem, 1)

        s_y, s_mu, s_xc, s_lsq, s_lmm, s_lr, s_ln, s_silu = [
            sig("ln_" + x) for x in ("in", "mean", "centred", "square", "var", "root", "scaled", "silu")]

        @on("dve")
        def _(e):
            e.drain().then_inc(s_y.sem, 1)
            s_mu.wait(e, 1)
            for c in range(KT):
                e.tensor_tensor(Y[:, c, :], Y[:, c, :], PS[:, 5, :], ALU.subtract).then_inc(s_xc.sem, 1)
            s_lr.wait(e, 1)
            e.reciprocal(ra[:, :], ra[:, :])
            e.drain()
            for c in range(KT):
                e.scalar_tensor_tensor(out=Y[:, c, :], in0=Y[:, c, :], scalar=c_("ln_g", c),
                                       in1=ra[:, :], op0=ALU.mult, op1=ALU.mult).then_inc(s_ln.sem, 1)

        @on("pe")
        def _(e):
            s_y.wait(e, 1)
            for c in range(KT):
                mm = e.matmul(PS[:, 5, :], mean, Y[:, c, :], start=c == 0, stop=c == KT - 1)
            mm.then_inc(s_mu.sem, 1)
            for c in range(KT):
                s_lsq.wait(e, c + 1)
                e.matmul(PS[:, 6, :], mean, norm_sq[:, c % 2, :], start=c == 0, stop=c == KT - 1)\
                    .then_inc(s_lmm.sem, 1)

        @on("act")
        def _(e):
            for c in range(KT):
                s_xc.wait(e, c + 1)
                if c >= 2:
                    s_lmm.wait(e, c - 1)
                e.activation(norm_sq[:, c % 2, :], Y[:, c, :], ACT.Square).then_inc(s_lsq.sem, 1)
            s_lmm.wait(e, KT)
            e.activation(ra[:, :], PS[:, 6, :], ACT.Sqrt, bias=c_("eps")).then_inc(s_lr.sem, 1)
            for c in range(KT):
                s_ln.wait(e, c + 1)
                e.activation(Y[:, c, :], Y[:, c, :], ACT.Silu, bias=c_("ln_b", c)).then_inc(s_silu.sem, 1)

        pe_gemm("conv_out", KT, lambda k: Y[:, k, :], (s_silu, 0), free=evac_dve)
        merged = evac_dve.n

        def merge(e, t, bank):
            e.tensor_tensor(tile(G, t), bank, tile(G, t), ALU.mult)
            e.drain()
            s_ao.wait(e, t + 1)
            return e.tensor_tensor(tile(Q, t), tile(G, t), tile(H, t), ALU.add)
        evacuate("dve", "conv_out", KT, merge, evac_dve)
        pe_gemm("w_out", KT, lambda k: Q[:, k, :], (evac_dve, merged), free=evac_dve)
        evac_add("w_out", KT)
        barrier()
        m.close()

    def peer():
        m = ExitStack()
        low = sb(m, "peer_x_lo", [P, KT, S], F32R)
        A, A_lo = two_names(m, "experts", "experts_lo", [P, 2 * JQ, S])
        TT = sb(m, "picks_T", [P, 2, S])
        gate_row = norm_r
        split = Split(m, "peer_slots", START["peer_q_u0"], START["f1_in"] - START["peer_q_u0"], 2)
        sc = ExitStack()
        keysT = sb(sc, "sub_keys_T", [P, 2 * PH, NKEY])
        qh = sb(sc, "peer_q", [P, 2, S])
        raw = sb(sc, "peer_scores", [P, 8, NKEY])
        work = sb(sc, "scores_left", [P, 8, NKEY])
        cand = sb(sc, "sums", [P, NB, TOPK * TOPK])
        cand2 = sb(sc, "sums_left", [P, NB, TOPK * TOPK])
        with ExitStack() as only_norm:
            normed = sb(only_norm, "normed", [P, 4, S])
        eq_a, eq_b = sb(sc, "row_hot", [P, NB * TOPK, TOPK]), sb(sc, "col_hot", [P, NB * TOPK, TOPK])
        T = sb(sc, "picks", [P, 3, NB, PH * TOPK])
        top = sb(sc, "top", [P, 8, TOPK])
        idx, idxf = sb(sc, "top_index", [P, 8, TOPK], U32), sb(sc, "top_index_f", [P, 8, TOPK])
        best = sb(sc, "best", [P, NB, TOPK])
        pos = sb(sc, "best_pos", [P, NB, TOPK], U32)
        pa, pb = sb(sc, "pos_row", [P, NB, TOPK], U32), sb(sc, "pos_col", [P, NB, TOPK], U32)
        gsum = sb(sc, "gate_sum", [P, NB * PH])

        s_keys = sig("peer_keys").by_dma()
        s_qe, s_psc, s_top, s_u = [sig("peer_" + x) for x in ("q_out", "scores", "top", "u_out")]
        on("act")(lambda e: e.dma_start(keysT[:, :, :], a["keysT"]).then_inc(s_keys.sem, 16))
        nq = START["peer_q_u0"]
        on("act")(lambda e: split.hi(e, 0, 4, nq))
        split.lows(nq, 33)
        b_h = rms_norm("norm2", split=(low, normed))

        def heads_loop(e, one):
            with e.Fori(0, PH // 2) as i:
                for b in range(2):
                    one(i, i * 2 + b, b)

        on("pe")(lambda e: (s_keys.wait(e, 16), s_h.wait(e, b_h + KT)))

        x = lambda k: (Hh[:, k, :], low[:, k, :])

        @on("pe")
        def _(e):
            def product(bank, w):
                for k in range(KT):
                    mm = product3(e, PS[:, bank, :], w, k, x(k), k == 0, k == KT - 1)
                mm.then_inc(slot_done.sem, 1)

            def one(i, h, b):
                for c in range(2):
                    w = split.use(e, i, 8, nq + 4 * b + c)
                    s_qe.wait(e, h * 2)
                    product(c, w)
                for c in range(2):
                    s_qe.wait(e, h * 2 + (c + 1))
                    s_top.wait(e, h)
                    for n in range(NB):
                        mm = e.matmul(PS[:, 2 + c, n * P:(n + 1) * P], qh[:, c, n * P:(n + 1) * P],
                                      tile(keysT, h * 2 + c), start=True, stop=True)
                    mm.then_inc(s_psc.sem, 1)
                    w = split.use(e, i, 8, nq + 4 * b + 2 + c)
                    s_u.wait(e, h * 2)
                    product(4 + c, w)
            heads_loop(e, one)

        @on("act")
        def _(e):
            def one(i, h, b):
                for c in range(2):
                    split.hi(e, i, 8, nq + 4 * b + c + 1)
                    slot_done.wait(e, i * 8 + (nq + 4 * b + c + 1))
                    s_psc.wait(e, h * 2)
                    e.activation(qh[:, c, :], PS[:, c, :], ACT.Copy).then_inc(s_qe.sem, 1)
                for r in range(2):
                    split.hi(e, i, 8, nq + 4 * b + 3 + r)
                    slot_done.wait(e, i * 8 + (nq + 4 * b + 3 + r))
                    e.activation(tile(A, h * 2 + r), PS[:, 4 + r, :], ACT.Gelu).then_inc(s_u.sem, 1)
            heads_loop(e, one)
        @on("dve")
        def _(e):
            def top16(values, left, vals, index, n):
                for c in range(n):
                    e.max(vals[:, c, 0:8], values(c))
                e.drain()
                for c in range(n):
                    e.max_index(index[:, c, 0:8], vals[:, c, 0:8], values(c))
                    e.match_replace(left[:, c, :], vals[:, c, 0:8], values(c), TAKEN)
                e.drain()
                for c in range(n):
                    e.max(vals[:, c, 8:16], left[:, c, :])
                e.drain()
                for c in range(n):
                    e.max_index(index[:, c, 8:16], vals[:, c, 8:16], left[:, c, :])
                e.drain()

            def one(i, h, b):
                e.drain()
                s_psc.wait(e, h * 2 + 2)
                e.tensor_copy(raw[:, :, :].rearrange("p c n -> p (c n)"),
                              PS[:, 2:4, :].rearrange("p a b -> p (a b)")).then_inc(s_top.sem, 1)
                e.drain()
                top16(lambda c: raw[:, c, :], work, top, idx, 8)
                e.tensor_copy(idxf[:, :, :], idx[:, :, :])
                e.tensor_tensor(cand[:, :, :].rearrange("p n (r c) -> p n r c", r=TOPK),
                                view(top[:, 0, :], [TOPK, NB], [1, TOPK], [0, TOPK]),
                                view(top[:, NB, :], [TOPK, NB], [0, TOPK], [1, TOPK]), ALU.add)
                e.drain()
                top16(lambda c: cand[:, c, :], cand2, best, pos, NB)
                e.tensor_scalar(pa[:, :, :], pos[:, :, :], 4, None, ALU.logical_shift_right)
                e.tensor_scalar(pb[:, :, :], pos[:, :, :], 15, None, ALU.bitwise_and)
                e.tensor_copy(T[:, 2, :, bass.ds(h * TOPK, TOPK)], best[:, :, :])
                e.drain()
                for p_, eq in ((pa, eq_a), (pb, eq_b)):
                    e.tensor_tensor(eq[:, :, :], view(p_[:, 0, :], [1, NB * TOPK], [0, TOPK]),
                                    view(iota, [0, NB * TOPK], [1, TOPK]), ALU.is_equal)
                e.drain()
                for c, eq in enumerate((eq_a, eq_b)):
                    v = eq[:, :, :].rearrange("p (n k) r -> p n k r", n=NB)
                    e.tensor_tensor(v, v, view(idxf[:, c * NB, :], [TOPK, NB], [0, TOPK], [1, TOPK]),
                                    ALU.mult)
                e.drain()
                for c, eq in enumerate((eq_a, eq_b)):
                    e.tensor_reduce(T[:, c, :, bass.ds(h * TOPK, TOPK)],
                                    eq[:, :, :].rearrange("p (n k) r -> p n k r", n=NB), AX.X, ALU.add)
            heads_loop(e, one)

        s_gx, s_ge, s_tab, s_tt, s_tabT = [sig("gate_" + x) for x in
                                           ("shifted", "exp", "table", "turned", "table_T")]
        g2 = T[:, 2, :, :].rearrange("p n (h k) -> p (n h) k", k=TOPK)

        @on("dve")
        def _(e):
            e.drain()
            e.tensor_copy(gsum[:, :], view(T[:, 2, 0, 0:1], [TOPK, NB * PH]))
            e.drain()
            e.tensor_tensor(g2, g2, view(gsum[:, :], [1, NB * PH], [0, TOPK]), ALU.subtract)\
                .then_inc(s_gx.sem, 1)
            s_ge.wait(e, 1)
            e.tensor_reduce(gsum[:, :], g2, AX.X, ALU.add)
            e.drain()
            e.reciprocal(gsum[:, :], gsum[:, :])
            e.drain()
            e.tensor_tensor(g2, g2, view(gsum[:, :], [1, NB * PH], [0, TOPK]), ALU.mult)\
                .then_inc(s_tab.sem, 1)
            for v in range(3):
                s_tt.wait(e, v + 1)
                e.tensor_copy(TT[:, v, :] if v < 2 else gate_row[:, :], PS[:, v, :]).then_inc(s_tabT.sem, 1)
            e.tensor_copy(iota_b[:, :], iota)
            for v in range(3):
                e.drain()
                e.tensor_copy(gp[:, v, :], gate_row[:, :])
                e.drain()
                if v < 2:
                    e.tensor_tensor(gate_row[:, :], gate_row[:, :], gp[:, v, :], ALU.subtract)

        @on("act")
        def _(e):
            s_gx.wait(e, 1)
            v = T[:, 2, :, :]
            e.activation(v, v, ACT.Exp).then_inc(s_ge.sem, 1)

        @on("pe")
        def _(e):
            s_tab.wait(e, 1)
            s_qe.wait(e, 2 * PH)
            for v in range(3):
                for n in range(NB):
                    mm = e.transpose(PS[:, v, n * P:(n + 1) * P], T[:, v, n, :], ident)
                mm.then_inc(s_tt.sem, 1)
        on("act")(lambda e: s_tt.wait(e, 3))
        sc.close()
        gp = sb(m, "gate_parts", [P, 3, S], BF16)
        iota_b = sb(m, "iota_bf16", [P, P], BF16)
        hot_i = sb(m, "key1_one_hot", [P, 2, 16, P], BF16)
        hot_e = sb(m, "key2_one_hot", [P, 16, JQ], BF16)
        hot_j = sb(m, "gate_at_key2", [P, 2, 3, 16, JQ], BF16)
        G_hi = sb(m, "gated_hi", [P, JQ, S], F32R)

        s_hot, s_wm, s_g, s_ve, s_gh, s_gl = [sig("w_" + x_) for x_ in (
            "one_hot", "product", "gated", "v_out", "gated_hi", "gated_lo")]
        GROUPS = S // 16
        on("pe")(lambda e: e.sem_inc(s_wm.sem, 2))
        on("dve")(lambda e: e.sem_inc(s_g.sem, 2))

        class Group:

            def __init__(self, q0, o):
                self.q0, self.o = q0, o
                self.A = A[:, q0 % 2 * JQ:(q0 % 2 + 1) * JQ, :]
                self.A_lo = A_lo[:, q0 % 2 * JQ:(q0 % 2 + 1) * JQ, :]

            def at(self, per, x_):
                return self.o * (2 * per) + x_ + per * self.q0

        def slot_parts(e, n0, o, i, r):
            s_lo.wait(e, o * 64 + i * 4 + (n0 + r + split.base + 1))
            return [split.parts[:, (n0 + r) % 2, v, :] for v in range(2)]

        def u_slot(e, u, n0, i, r):
            w = [tiles_of(p_) for p_ in slot_parts(e, n0, u.o, i, r)]
            s_u.wait(e, u.at(JQ, i * 4 + (r - 1)))
            for k in range(KT):
                mm = product3(e, PS[:, 4 + r % 2, :], w, k, x(k), k == 0, k == KT - 1)
            mm.then_inc(slot_done.sem, 1)

        def v_slot(e, v, n0, s_):
            dh, t = s_ // 8, s_ % 8
            w = slot_parts(e, n0, v.o, 0, s_)
            if dh == 0:
                s_gl.wait(e, v.at(JQ, 2 * t + 2))
            for j in range(2):
                g_ = (G_hi[:, 2 * t + j, :], v.A_lo[:, 2 * t + j, :])
                for d in range(4):
                    if t == 0 and j == 0:
                        s_ve.wait(e, v.at(8, d + 1 if dh else 0))
                    at = j * (D // 2) + d * P
                    for y, (a_, b_) in enumerate(THREE):
                        mm = e.matmul(PS[:, d, :], w[a_][:, at:at + P], g_[b_],
                                      start=t == 0 and j == 0 and y == 0,
                                      stop=t == 7 and j == 1 and y == 2)
            mm.then_inc(slot_done.sem, 1)

        def w_group(e, w, g, parity):
            s_g.wait(e, w.at(GROUPS, g + 1))
            s_hot.wait(e, w.at(GROUPS, g + 1))
            for u in range(16):
                for v in range(3):
                    mm = e.matmul(PS[:, 6 + parity, u * JQ:(u + 1) * JQ], hot_i[:, parity, u, :],
                                  hot_j[:, parity, v, u, :], start=v == 0, stop=v == 2)
            mm.then_inc(s_wm.sem, 1)

        def one_hots(e, w, g, parity):
            s0 = g * 16
            first_key = w.o * (2 * JQ) + w.q0 * JQ
            e.drain()
            e.tensor_tensor(hot_e[:, :, :],
                            TT[:, 1, bass.ds(s0, 16)].unsqueeze(2).broadcast_to([P, 16, JQ]),
                            iota_b[:, bass.ds(first_key, JQ)].unsqueeze(1).broadcast_to([P, 16, JQ]),
                            ALU.is_equal)
            e.drain()
            s_wm.wait(e, w.at(GROUPS, g + 1))
            held(e)
            e.tensor_tensor(hot_i[:, parity, :, :],
                            TT[:, 0, bass.ds(s0, 16)].unsqueeze(2).broadcast_to([P, 16, P]),
                            view(iota_b[:, :], [0, 16], [1, P]), ALU.is_equal)
            e.tensor_tensor(hot_j[:, parity, :, :, :],
                            view(hot_e[:, 0, :], [0, 3], [1, 16 * JQ])
                            .rearrange("p v (s j) -> p v s j", j=JQ),
                            gp[:, :, bass.ds(s0, 16)].unsqueeze(3).broadcast_to([P, 3, 16, JQ]),
                            ALU.mult).then_inc(s_hot.sem, 1)

        def gate(e, w, g, parity):
            s_wm.wait(e, w.at(GROUPS, g + 3))
            held(e)
            At = w.A[:, :, bass.ds(g * 16, 16)]
            e.tensor_tensor(At, PS[:, 6 + parity, 0:16 * JQ].rearrange("p (s j) -> p j s", j=JQ),
                            At, ALU.mult).then_inc(s_g.sem, 1)

        def g_hi(e, v, j):
            s_g.wait(e, v.at(GROUPS, GROUPS + 2))
            e.activation(G_hi[:, j, :], v.A[:, j, :], ACT.Copy).then_inc(s_gh.sem, 1)

        def g_lo(e, v, j):
            s_gh.wait(e, v.at(JQ, j + 1))
            held(e)
            e.tensor_tensor(v.A_lo[:, j, :], v.A[:, j, :], G_hi[:, j, :].bitcast(F32),
                            ALU.subtract).then_inc(s_gl.sem, 1)

        class Window:

            def __init__(self, kind, q0, w0=None, g0=0, per_slot=1, early=False, ahead=None):
                self.kind, self.q0, self.w0, self.g0 = kind, q0, w0, g0
                self.per, self.early, self.ahead = per_slot, early, ahead
                self.n0 = START[f"{kind}{q0}"]

            def groups(self, s_):
                if self.w0 is None or (self.early and s_ == 15):
                    return []
                n = 2 * self.per if self.early and s_ == 14 else self.per
                return [(self.per * s_ + t, (self.per * s_ + t) % 2) for t in range(n)]

            def beside(self, e, o, f, i, r, regular):
                if self.w0 is None:
                    return
                w = Group(self.w0, o)
                if regular:
                    for g, parity in self.groups(r):
                        f(e, w, i * (4 * self.per) + (self.g0 + g), parity)
                else:
                    for g, parity in self.groups(4 * i + r):
                        f(e, w, self.g0 + g, parity)

            def steps(self, e, body):
                with e.Fori(0, 3) as i:
                    for r in range(4):
                        body(i, r, True)
                for r in range(4):
                    body(3, r, False)

            def pe(self, e, o):
                q = Group(self.q0, o)
                if self.kind == "u":
                    def body(i, r, regular):
                        u_slot(e, q, self.n0, i, r)
                        self.beside(e, o, w_group, i, r, regular)
                    self.steps(e, body)
                else:
                    for s_ in range(16):
                        v_slot(e, q, self.n0, s_)
                        self.beside(e, o, w_group, s_ // 4, s_ % 4, False)

            def next_hi(self, e, o, i, r):
                n = self.n0 + r + 1
                if isinstance(i, int) and n + 4 * i == START["f1_in"]:
                    return
                e.wait_ge(arrive[n % RING], o * 256 + i * 16 + 16 * (n // RING + 1))
                slot_done.wait(e, o * 64 + i * 4 + (n - 1))
                e.activation(split.parts[:, n % 2, 0, :], ring[:, n % RING, :], ACT.Copy)                    .then_inc(s_hi.sem, 1)

            def next_lo(self, e, o, i, r):
                n = self.n0 + r + 1
                if isinstance(i, int) and n + 4 * i == START["f1_in"]:
                    return
                s_hi.wait(e, o * 64 + i * 4 + (n + split.base + 1))
                held(e)
                e.tensor_tensor(split.parts[:, n % 2, 1, :], ring[:, n % RING, :],
                                split.parts[:, n % 2, 0, :].bitcast(F32), ALU.subtract)                    .then_inc(s_lo.sem, 1)

            def parts(self, e, o, i, r, regular, weights, gated):
                weights(e, o, i, r)
                s_ = None if regular else 4 * i + r
                if self.kind == "v" and s_ < 7:
                    for j in range(2):
                        gated(e, Group(self.q0, o), 2 * s_ + 2 + j)
                if s_ == 15 and self.ahead is not None:
                    for j in range(2):
                        gated(e, Group(self.ahead, o), j)

            def act(self, e, o):
                q = Group(self.q0, o)
                if self.kind == "u":
                    def body(i, r, regular):
                        self.parts(e, o, i, r, regular, self.next_hi, g_hi)
                        slot_done.wait(e, o * 64 + i * 4 + (self.n0 + r + 1))
                        e.activation(tile(q.A, i * 4 + r), PS[:, 4 + r % 2, :], ACT.Gelu)                            .then_inc(s_u.sem, 1)
                    self.steps(e, body)
                else:
                    for s_ in range(16):
                        self.parts(e, o, s_ // 4, s_ % 4, False, self.next_hi, g_hi)

            def pool(self, e, o):
                if self.kind == "u":
                    self.steps(e, lambda i, r, regular:
                               self.parts(e, o, i, r, regular, self.next_lo, g_lo))
                else:
                    for s_ in range(16):
                        self.parts(e, o, s_ // 4, s_ % 4, False, self.next_lo, g_lo)

            def dve(self, e, o):
                if self.w0 is not None:
                    s_u.wait(e, Group(self.w0, o).at(JQ, JQ))
                    held(e)
                if self.kind == "u":
                    def body(i, r, regular):
                        for f in (one_hots, gate):
                            self.beside(e, o, f, i, r, regular)
                    self.steps(e, body)
                else:
                    for s_ in range(16):
                        if self.w0 is not None:
                            self.beside(e, o, one_hots, s_ // 4, s_ % 4, False)
                        if s_ in (8, 15):
                            dh = int(s_ == 15)
                            slot_done.wait(e, o * 64 + (self.n0 + 8 * dh + 8))
                            for d in range(4):
                                e.tensor_tensor(X[:, dh * 4 + d, :], PS[:, d, :],
                                                X[:, dh * 4 + d, :], ALU.add).then_inc(s_ve.sem, 1)
                        if self.w0 is not None:
                            self.beside(e, o, gate, s_ // 4, s_ % 4, False)
                    e.drain()

        on("pe")(lambda e: s_tabT.wait(e, 3))
        HALF = GROUPS // 2
        before = [Window("u", 1, 0, 0, 2, early=True, ahead=0)]
        middle = []
        for q0 in range(2):
            middle += [Window("v", q0, q0 + 1),
                       Window("u", q0 + 2, q0 + 1, HALF, early=True, ahead=q0 + 1)]
        after = [Window("v", 6, 7, 0, 2, early=True, ahead=7), Window("v", 7)]
        for name in ("pe", "act", "dve", "pool"):
            def windows(e, name=name):
                def run(w, o):
                    {"pe": w.pe, "act": w.act, "dve": w.dve, "pool": w.pool}[name](e, o)
                for w in before:
                    run(w, 0)
                with e.Fori(0, 3) as o:
                    for w in middle:
                        run(w, o)
                for w in after:
                    run(w, 0)
            on(name)(windows)
        s_ve.n = NQ * 8
        rms_norm("final1", dst=X, ready=(s_ve, s_ve.n - KT))
        barrier()
        m.close()

    def ffn(n):
        m = ExitStack()
        F = [sb(m, f"ffn{n}_hidden_{v}", [P, FT, S], F32R) for v in ("hi", "lo")]
        low = sb(m, f"ffn{n}_x_lo", [P, KT, S], F32R)
        tmp = sb(m, f"ffn{n}_tmp", [P, 4, S])
        n0, nd = START[f"f{n}_in"], START[f"f{n}_out"]
        split = Split(m, f"ffn{n}_slots", n0, 3 * FT)
        split.lows(n0, 3 * FT)
        on("act")(lambda e: [split.hi(e, 0, 4, n0 + r) for r in range(2)])
        b_h = rms_norm(f"ffn{n}_n", split=(low, tmp))
        first = glu_done.n

        def hidden(e, p, bank, t):
            e.tensor_tensor(t, bank, t, ALU.mult)
            e.drain()
            e.tensor_copy(tile(F[0], p), t)
            e.drain()
            return e.tensor_tensor(tile(F[1], p), t, tile(F[0], p).bitcast(F32), ALU.subtract)
        glu(f"f{n}_in", FT, tmp, lambda e, p, t, bank, f: e.activation(t, bank, f), ACT.Silu,
            hidden, (s_h, b_h), split, low)

        @on("pe")
        def _(e):
            def slot(i, r, first_, last):
                glu_done.wait(e, i * 4 + (first + r + 1))
                w = split.use(e, i, 4, nd + r)
                x = [tile(F[v], i * 4 + r) for v in range(2)]
                for d in range(KT):
                    if first_ and d < 4:
                        glu_done.wait(e, first + FT)
                    mm = product3(e, PS[:, d, :], w, d, x, first_, last)
                mm.then_inc(slot_done.sem, 1)
            for r in range(4):
                slot(0, r, r == 0, False)
            with e.Fori(1, FT // 4) as i:
                for r in range(4):
                    slot(i, r, False, False)
            for r in range(FT % 4):
                slot(FT // 4, r, False, r == FT % 4 - 1)
        on("act")(lambda e: split.loop(e, split.hi, nd + 2, FT - 2))
        done = evac_dve.plan(KT)

        @on("dve")
        def _(e):
            slot_done.wait(e, nd + FT)
            for d in range(KT):
                e.scalar_tensor_tensor(out=X[:, d, :], in0=PS[:, d, :], scalar=0.5, in1=X[:, d, :],
                                       op0=ALU.mult, op1=ALU.add).then_inc(evac_dve.sem, 1)
        barrier()
        m.close()
        return done

    def mixer2():
        m = ExitStack()
        qk = sb(m, "gla_qk", [P, 2 * GH, S])
        v = sb(m, "gla_v", [P, NB, GH * GDV])
        wide = sb(m, "wide2", [P, 32, S])
        ckvT, ckv = sb(m, "ckv_T", [P, S]), sb(m, "ckv", [P, NB, P])
        sel = sb(m, "selection", [P, NB, S], mybir.dt.bfloat16)
        gl = ExitStack()
        la = sb(gl, "log_decay", [P, GH, S])
        lmask = sb(gl, "level_mask", [P, 8, P])
        iqT, ikT = wide[:, 0:4, :], wide[:, 4, :]
        gaT, alw = wide[0:16, 5, :], wide[0:16, 6, :]
        score = wide[:, 8:12, :]
        rel = wide[:, 12:14, :]
        ex = wide[:, 16:20, :]
        iw = sb(gl, "index_w", [P, NB, 8])
        i8 = sb(gl, "index_top", [P, 3, 8])
        tri = sb(gl, "causal", [P, P])

        s_in, s_hd = sig("m2_in").by_dma(), sig("m2_evac")
        b_in = s_in.plan(64)

        @on("act")
        def _(e):
            e.dma_start(alw, a["alpha_w"]).then_inc(s_in.sem, 16)
            e.dma_start(lmask[:, :, :], a["level_mask"]).then_inc(s_in.sem, 16)
            e.dma_start(tri[:, :], a["causal"]).then_inc(s_in.sem, 16)
        b_h = rms_norm("mix_n")
        nh = START["misc"]
        s_root2, s_csq, s_cmm, s_cn, s_ct, s_ce = [sig("ckv_" + x) for x in
                                                   ("root", "square", "mean", "normed", "turned", "tokens")]
        s_al, s_ax, s_dot, s_rel, s_acc = [sig("ix_" + x) for x in
                                           ("alpha", "log", "dots", "relu", "sum")]
        on("dve")(lambda e: e.sem_inc(s_acc.sem, 2))
        s_acc.n = 2
        combos = [(n, h) for n in range(1, NB) for h in range(8)]
        old = [(s, s.n) for s in (evac_act, evac_dve, glu_done)]

        @on("pe")
        def _(e):
            s_h.wait(e, b_h + KT)
            for s, x in old:
                s.wait(e, x)
            w = tiles_of(use_slot(e, nh, 0, 4, 0))
            for k in range(KT):
                e.matmul(PS[0:16, 0, :], w[:, k, 0:16], H[:, k, :], start=k == 0, stop=k == KT - 1)
            for n in range(NB):
                for k in range(KT):
                    mm = e.matmul(PS[:, 1, n * 8:(n + 1) * 8], H[:, k, n * P:(n + 1) * P],
                                  w[:, k, 16:24], start=k == 0, stop=k == KT - 1)
            mm.then_inc(slot_done.sem, 1)
            for j in range(6):
                w = tiles_of(use_slot(e, nh, 0, 4, j + 1))
                for k in range(KT):
                    mm = e.matmul(PS[:, 2 + j, :], w[:, k, :], H[:, k, :], start=k == 0, stop=k == KT - 1)
                mm.then_inc(slot_done.sem, 1)
            s_in.wait(e, 48)
            s_hd.wait(e, 2)
            for h in range(GH):
                if h >= 2:
                    s_hd.wait(e, h + 1)
                e.matmul(PS[:, h, :], alw[:, h * P:(h + 1) * P], gaT, start=True, stop=True)\
                    .then_inc(s_al.sem, 1)
            s_csq.wait(e, 1)
            e.matmul(PS[:, 7, :], mean, norm_sq[:, 0, :], start=True, stop=True).then_inc(s_cmm.sem, 1)
            for x, (n, h) in enumerate(combos):
                rows = slice(64 * (h % 2), 64 * (h % 2) + 64)
                s_rel.wait(e, max(x - 1, 0))
                e.matmul(PS[:, 4 + x % 2, 0:(n + 1) * P], iqT[rows, h // 2, n * P:(n + 1) * P],
                         ikT[rows, 0:(n + 1) * P], start=True, stop=True).then_inc(s_dot.sem, 1)
            s_cn.wait(e, 1)
            for n in range(NB):
                mm = e.transpose(PS[:, 6, n * P:(n + 1) * P], ckvT[:, n * P:(n + 1) * P], ident)
            mm.then_inc(s_ct.sem, 1)

        @on("act")
        def _(e):
            slot_done.wait(e, nh + 1)
            e.activation(gaT, PS[0:16, 0, :], ACT.Copy).then_inc(s_hd.sem, 1)
            e.activation(iw[:, :, :].rearrange("p n h -> p (n h)"), PS[:, 1, 0:32], ACT.Copy,
                         scale=8 ** -0.5).then_inc(s_hd.sem, 1)
            for j, dst in enumerate([ikT] + [iqT[:, t, :] for t in range(4)] + [ckvT[:, :]]):
                slot_done.wait(e, nh + j + 2)
                e.activation(dst, PS[:, 2 + j, :], ACT.Copy).then_inc(s_hd.sem, 1)
            s_hd.wait(e, 8)
            e.activation(norm_sq[:, 0, :], ckvT[:, :], ACT.Square).then_inc(s_csq.sem, 1)
            s_cmm.wait(e, 1)
            e.activation(norm_r[:, :], PS[:, 7, :], ACT.Sqrt, scale=float(KT), bias=c_("eps"))\
                .then_inc(s_root2.sem, 1)
            for h in range(GH):
                s_al.wait(e, h + 1)
                e.activation(la[:, h, :], PS[:, h, :], ACT.Identity, bias=c_("alpha_b", h))
            e.drain()
            flat, exf = la[:, :, :], ex
            e.activation(exf, flat, ACT.Abs)
            e.drain()
            e.activation(exf, exf, ACT.Exp, scale=-1.0)
            e.drain()
            e.activation(exf, exf, ACT.Ln, bias=c_("one")).then_inc(s_ax.sem, 1)
            for x, (n, h) in enumerate(combos):
                s_dot.wait(e, x + 1)
                s_acc.wait(e, x + 1)
                e.activation(rel[:, x % 2, 0:(n + 1) * P], PS[:, 4 + x % 2, 0:(n + 1) * P], ACT.Relu,
                             scale=0.125).then_inc(s_rel.sem, 1)
            s_ct.wait(e, 1)
            e.activation(ckv[:, :, :].rearrange("p n c -> p (n c)"), PS[:, 6, :], ACT.Copy)\
                .then_inc(s_ce.sem, 1)

        s_la = sig("m2_decay")

        @on("dve")
        def _(e):
            s_root2.wait(e, 1)
            e.reciprocal(norm_r[:, :], norm_r[:, :])
            e.drain()
            e.scalar_tensor_tensor(out=ckvT[:, :], in0=ckvT[:, :], scalar=c_("ckv_n"),
                                   in1=norm_r[:, :], op0=ALU.mult, op1=ALU.mult).then_inc(s_cn.sem, 1)
            s_ax.wait(e, 1)
            la2, ex2 = (x.rearrange("p h s -> p (h s)") for x in (la[:, :, :], ex))
            e.scalar_tensor_tensor(out=la2, in0=la2, scalar=0.0, in1=ex2, op0=ALU.min,
                                   op1=ALU.subtract)
            e.drain()
            e.tensor_scalar(la2, la2, 1.0 / 16, None, ALU.mult).then_inc(s_la.sem, 1)
            s_hd.wait(e, 8)
            for x, (n, h) in enumerate(combos):
                e.drain()
                s_rel.wait(e, x + 1)
                sc_, r_ = score[:, n, 0:(n + 1) * P], rel[:, x % 2, 0:(n + 1) * P]
                if h == 0:
                    e.tensor_scalar(sc_, r_, iw[:, n, 0:1], None, ALU.mult).then_inc(s_acc.sem, 1)
                else:
                    e.scalar_tensor_tensor(out=sc_, in0=r_, scalar=iw[:, n, h:h + 1], in1=sc_,
                                           op0=ALU.mult, op1=ALU.add).then_inc(s_acc.sem, 1)
            e.drain()
            s_in.wait(e, 48)
            for n in range(1, NB):
                d = score[:, n, n * P:(n + 1) * P]
                e.tensor_tensor(d, d, tri[:, :], ALU.add)
            with e.Fori(0, SEL // 8):
                e.drain()
                for n in range(1, NB):
                    e.max(i8[:, n - 1, :], score[:, n, 0:(n + 1) * P])
                e.drain()
                for n in range(1, NB):
                    w = score[:, n, 0:(n + 1) * P]
                    e.match_replace(w, i8[:, n - 1, :], w, TAKEN)
            e.drain()
            e.tensor_copy(sel[:, 0, 0:P], tri[:, :])
            for n in range(1, NB):
                e.tensor_scalar(sel[:, n, 0:(n + 1) * P], score[:, n, 0:(n + 1) * P], TAKEN / 2, NEG,
                                ALU.is_gt, ALU.mult)
            e.drain()

        s_ax_n = 1
        on("pe")(lambda e: s_ax.wait(e, s_ax_n))
        pe_gemm("gqk", 2 * GH, lambda k: H[:, k, :])
        n_qk = START["gqk"]
        qk_base = evac_act.plan(2 * GH)

        @on("act")
        def _(e):
            with e.Fori(0, 2) as i:
                for r in range(4):
                    slot_done.wait(e, i * 4 + (n_qk + r + 1))
                    e.activation(tile(qk, i * 4 + r), PS[:, r, :], ACT.Copy,
                                 scale=1.0 if r % 2 else P ** -0.5).then_inc(evac_act.sem, 1)
        nv = START["gv"]
        v_base = evac_act.plan(8)
        s_ce_n = 1

        @on("pe")
        def _(e):
            evac_act.wait(e, v_base)
            s_ce.wait(e, s_ce_n)
            for c in range(2):
                for kp in range(4):
                    w = use_slot(e, nv, 0, 4, 4 * c + kp).rearrange("p (k c) -> p k c", k=2)
                    for k in range(2):
                        for n in range(NB):
                            mm = e.matmul(PS[:, 4 * c + n, :], H[:, 2 * kp + k, n * P:(n + 1) * P],
                                          w[:, k, :], start=kp == 0 and k == 0, stop=kp == 3 and k == 1)
                    mm.then_inc(slot_done.sem, 1)

        @on("act")
        def _(e):
            for c in range(2):
                slot_done.wait(e, nv + 4 * c + 4)
                for n in range(NB):
                    e.activation(v[:, n, c * 512:(c + 1) * 512], PS[:, 4 * c + n, :], ACT.Copy)\
                        .then_inc(evac_act.sem, 1)

        b = sb(gl, "log_decay_sum", [P, S])
        dd = sb(gl, "decay_diff", [P, 2, S])
        E = sb(gl, "decay", [P, 2, S])
        ql, kl = sb(gl, "q_level", [P, 2, S]), sb(gl, "k_level", [P, 2, S])
        acc = sb(gl, "gla_scores_T", [P, S])
        qe = sb(gl, "q_decayed", [P, S])
        kdT = sb(gl, "k_decayed", [P, NB, P])
        St = sb(gl, "state", [P, 3, GDV])
        ot = sb(gl, "gla_o", [P, NB, GDV])
        gs = sb(gl, "gla_stats", [P, 3, NB])
        names = ("b", "diff", "exp", "q", "k", "scores", "picked", "el", "kd", "kdT", "kd_out", "kv",
                 "state", "o", "square", "root", "o_norm", "oT", "o_out")
        (s_b, s_d, s_e, s_q, s_k, s_s, s_p, s_el, s_kd, s_kt, s_ko, s_kv, s_st, s_o, s_os, s_or,
         s_on, s_ot, s_oo) = [sig("gla_" + x) for x in names]
        nw = START["wide2"]
        w_base = evac_act.plan(32)
        LV = 7

        @on("pe")
        def _(e):
            evac_act.wait(e, v_base + 8)

            def gemm(h, r):
                w = tiles_of(use_slot(e, nw, h, 8, r))
                evac_act.wait(e, h * 8 + (w_base + r - 1))
                for k in range(KT):
                    mm = e.matmul(PS[:, 6 + r % 2, :], w[:, k, :], H[:, k, :], start=k == 0,
                                  stop=k == KT - 1)
                mm.then_inc(slot_done.sem, 1)

            with e.Fori(0, GH) as h:
                for l in range(LV + 1):
                    if l < LV:
                        gemm(h, l)
                    s_q.wait(e, h * (LV + 1) + (l + 1))
                    s_k.wait(e, h * (LV + 1) + (l + 1))
                    if l >= 2:
                        s_p.wait(e, h * (LV + 1) + (l - 1))
                    elif True:
                        s_p.wait(e, h * (LV + 1))
                    for n in range(NB):
                        t = slice(n * P, (n + 1) * P)
                        mm = e.matmul(PS[:, l % 2, t], kl[:, l % 2, t], ql[:, l % 2, t],
                                      start=True, stop=True)
                    mm.then_inc(s_s.sem, 1)
                s_kd.wait(e, h + 1)
                for n in range(NB):
                    mm = e.transpose(PS[:, 4, n * P:(n + 1) * P], dd[:, 1, n * P:(n + 1) * P], ident)
                mm.then_inc(s_kt.sem, 1)
                gemm(h, 7)
                s_ko.wait(e, h + 1)
                for n in range(NB - 1):
                    mm = e.matmul(PS[:, 2 + n // 2, (n % 2) * GDV:(n % 2 + 1) * GDV], kdT[:, n, :],
                                  v[:, n, bass.ds(h * GDV, GDV)], start=True, stop=True)
                mm.then_inc(s_kv.sem, 1)
                s_st.wait(e, h + 1)
                for n in range(NB):
                    o_ = PS[:, 4 + n // 2, (n % 2) * GDV:(n % 2 + 1) * GDV]
                    mm = e.matmul(o_, acc[:, n * P:(n + 1) * P], v[:, n, bass.ds(h * GDV, GDV)],
                                  start=True, stop=n == 0)
                    if n:
                        mm = e.matmul(o_, qe[:, n * P:(n + 1) * P], St[:, n - 1, :], start=False,
                                      stop=True)
                mm.then_inc(s_o.sem, 1)
                s_on.wait(e, h + 1)
                for j in range(2):
                    for n in range(NB):
                        mm = e.transpose(PS[:, 2 + j, n * P:(n + 1) * P],
                                         ot[:, n, j * P:(j + 1) * P], ident)
                mm.then_inc(s_ot.sem, 1)

        @on("dve")
        def _(e):
            s_la.wait(e, 1)
            with e.Fori(0, GH) as h:
                e.drain()
                for n in range(NB):
                    t = slice(n * P, (n + 1) * P)
                    e.tensor_tensor_scan(dd[:, 0, t], view(c_("one"), [0, P]), la[:, bass.ds(h, 1), t]
                                         .rearrange("p a s -> p (a s)"), 0.0, ALU.mult, ALU.add)
                e.drain()
                e.tensor_copy(b[:, :], dd[:, 0, :]).then_inc(s_b.sem, 1)
                e.memset(acc[:, :], 0.0)
                e.drain()

                def diff(l):
                    half = 64 >> l
                    nb = S // (2 * half)
                    e.tensor_tensor(view(dd[:, l % 2, :], [2 * half, nb], [1, 2 * half]),
                                    view(b[:, :], [2 * half, nb], [1, 2 * half]),
                                    view(b[:, half - 1:half], [2 * half, nb], [0, 2 * half]),
                                    ALU.subtract).then_inc(s_d.sem, 1)

                def pick(l):
                    e.drain()
                    s_s.wait(e, h * (LV + 1) + (l + 1))
                    held(e)
                    e.copy_predicated(acc[:, :].rearrange("p (n t) -> p n t", n=NB),
                                      view(lmask[:, l, :].bitcast(I32), [0, NB], [1, P]),
                                      PS[:, l % 2, :].rearrange("p (n t) -> p n t", n=NB))\
                        .then_inc(s_p.sem, 1)
                diff(0)
                for l in range(LV):
                    if l + 1 < LV:
                        diff(l + 1)
                    s_e.wait(e, h * LV + (l + 1))
                    e.tensor_tensor(ql[:, l % 2, :], tile(qk, h * 2), E[:, l % 2, :], ALU.mult)\
                        .then_inc(s_q.sem, 1)
                    if l:
                        pick(l - 1)
                e.drain()
                e.tensor_copy(ql[:, LV % 2, :], tile(qk, h * 2)).then_inc(s_q.sem, 1)
                e.tensor_tensor(dd[:, 0, :].rearrange("p (n t) -> p n t", n=NB),
                                view(b[:, P - 1:P], [P, NB], [0, P]),
                                b[:, :].rearrange("p (n t) -> p n t", n=NB), ALU.subtract)\
                    .then_inc(s_d.sem, 1)
                pick(LV - 1)
                s_el.wait(e, h + 1)
                e.tensor_tensor(qe[:, :], tile(qk, h * 2), E[:, 0, :], ALU.mult)
                e.tensor_tensor(dd[:, 1, :], tile(qk, h * 2 + 1), E[:, 1, :], ALU.mult)\
                    .then_inc(s_kd.sem, 1)
                e.drain()
                pick(LV)
                s_kv.wait(e, h + 1)
                e.tensor_copy(St[:, 0, :], PS[:, 2, 0:GDV])
                for n in range(1, NB - 1):
                    e.drain()
                    ins = e.scalar_tensor_tensor(
                        out=St[:, n, :], in0=St[:, n - 1, :], scalar=gs[:, 0, n:n + 1],
                        in1=PS[:, 2 + n // 2, (n % 2) * GDV:(n % 2 + 1) * GDV],
                        op0=ALU.mult, op1=ALU.add)
                ins.then_inc(s_st.sem, 1)
                s_or.wait(e, h + 1)
                e.reciprocal(gs[:, 2, :], gs[:, 2, :])
                e.drain()
                for n in range(NB):
                    ins = e.tensor_scalar(ot[:, n, :], PS[:, 4 + n // 2, (n % 2) * GDV:(n % 2 + 1) * GDV],
                                          gs[:, 2, n:n + 1], None, ALU.mult)
                ins.then_inc(s_on.sem, 1)
                s_ot.wait(e, h + 1)
                for j in range(2):
                    e.tensor_scalar(tile(qk, h * 2 + j), PS[:, 2 + j, :], cd("gla_n", h * 2 + j), None,
                                    ALU.mult).then_inc(s_oo.sem, 1)

        @on("pool")
        def _(e):
            with e.Fori(0, GH) as h:
                for l in range(LV):
                    s_e.wait(e, h * LV + (l + 1))
                    if l >= 2:
                        s_s.wait(e, h * (LV + 1) + (l - 1))
                    held(e)
                    e.tensor_tensor(kl[:, l % 2, :], tile(qk, h * 2 + 1), E[:, l % 2, :], ALU.mult)\
                        .then_inc(s_k.sem, 1)
                s_s.wait(e, h * (LV + 1) + LV - 1)
                held(e)
                e.tensor_copy(kl[:, LV % 2, :], tile(qk, h * 2 + 1)).then_inc(s_k.sem, 1)

        @on("act")
        def _(e):
            def gate(h, r):
                slot_done.wait(e, h * 8 + (nw + r + 1))
                e.activation(tile(wide, h * 8 + r), PS[:, 6 + r % 2, :], ACT.Copy)\
                    .then_inc(evac_act.sem, 1)

            with e.Fori(0, GH) as h:
                for l in range(LV):
                    s_d.wait(e, h * (LV + 1) + (l + 1))
                    if l >= 2:
                        s_q.wait(e, h * (LV + 1) + (l - 1))
                        s_k.wait(e, h * (LV + 1) + (l - 1))
                    e.activation(E[:, l % 2, :], dd[:, l % 2, :], ACT.Abs)
                    e.drain()
                    e.activation(E[:, l % 2, :], E[:, l % 2, :], ACT.Exp, scale=-1.0)\
                        .then_inc(s_e.sem, 1)
                    gate(h, l)
                s_d.wait(e, h * (LV + 1) + (LV + 1))
                s_q.wait(e, h * (LV + 1) + LV)
                s_k.wait(e, h * (LV + 1) + LV)
                e.activation(E[:, 0, :], b[:, :], ACT.Exp)
                e.activation(E[:, 1, :], dd[:, 0, :], ACT.Exp)
                e.activation(gs[:, 0, :], view(b[:, P - 1:P], [P, NB]), ACT.Exp).then_inc(s_el.sem, 1)
                s_kt.wait(e, h + 1)
                e.activation(kdT[:, :, :].rearrange("p n k -> p (n k)"), PS[:, 4, :], ACT.Copy)\
                    .then_inc(s_ko.sem, 1)
                gate(h, 7)
                s_o.wait(e, h + 1)
                for n in range(NB):
                    e.activation(ot[:, n, :], PS[:, 4 + n // 2, (n % 2) * GDV:(n % 2 + 1) * GDV],
                                 ACT.Square, accum_out=gs[:, 1, n:n + 1])
                e.drain()
                e.activation(gs[:, 2, :], gs[:, 1, :], ACT.Sqrt, scale=1.0 / GDV, bias=c_("eps"))\
                    .then_inc(s_or.sem, 1)
        barrier()
        gl.close()

        ds_ = ExitStack()
        OFF = [P, 0, 2 * P, 0]
        LB = [1, 2, 1, 0]
        LO = [0, P, 3 * P, 6 * P, 10 * P]
        OFF = [0, 0, P, 0]
        bias = sb(ds_, "bias_by_distance", [P, DH, S])
        hot = sb(ds_, "bucket_one_hot", [32, 640])
        rb_ = sb(ds_, "rel_bias", [32, DH])
        rows_ = sb(ds_, "bias_rows", [DH, 640])
        qs = sb(ds_, "dq_static", [P, S])
        BS = sb(ds_, "bias_and_selection", [P, 10 * P])
        L = sb(ds_, "dsa_logits", [P, 10 * P])
        pT = sb(ds_, "dsa_probs_T", [P, 10, P])
        dst_ = sb(ds_, "dsa_stats", [P, 3, NB])
        staged = [x[:, j * S:(j + 1) * S] for x in (BS, L) for j in range(2)]
        staged += [pT[:, 4 * j:4 * j + 4, :].rearrange("p c k -> p (c k)") for j in range(2)]
        staged += [norm_sq[:, j, :] for j in range(2)]
        scratch = nc.dram_tensor("bias_rows_dram", (DH, 640), F32, kind="Internal").ap()
        s_rmm, s_row = sig("bias_product"), sig("bias_rows")
        s_rin, s_rdr, s_bias = [sig("bias_" + x).by_dma() for x in ("in", "dram", "tiles")]
        s_turn = sig("bias_turned")
        s_silu, s_og, s_sg = [sig("m2_" + x) for x in ("silu", "o_gated", "sigmoid")]
        (d_qs, d_bs, d_lg, d_l, d_nm, d_ex, d_nrm, d_tr, d_pt, d_pv, d_o) = [sig("dsa_" + x) for x in (
            "q", "bias", "logits", "summed", "max", "exp", "probs", "trans", "probsT", "pv", "out")]
        ng = START["gla_out"]
        y_base = evac_dve.plan(KT)

        @on("act")
        def _(e):
            e.dma_start(hot[:, :], a["buckets"]).then_inc(s_rin.sem, 16)
            e.dma_start(rb_[:, :], a["rel_bias"]).then_inc(s_rin.sem, 16)
            with e.Fori(0, KT) as i:
                e.activation(tile(wide, i + 16), tile(wide, i + 16), ACT.Silu).then_inc(s_silu.sem, 1)
            s_rmm.wait(e, 1)
            for j in range(2):
                e.activation(rows_[:, j * 320:(j + 1) * 320], PS[0:DH, 4 + j, 0:320], ACT.Copy)\
                    .then_inc(s_row.sem, 1)
            s_row.wait(e, 2)
            e.dma_start(scratch, rows_[:, :]).then_inc(s_rdr.sem, 16)
            s_rdr.wait(e, 16)
            for h in range(DH):
                e.dma_start(staged[h], bass.AP(tensor=scratch.tensor, offset=h * 640,
                                               ap=[[1, P], [1, S]])).then_inc(s_bias.sem, 16)
            with e.Fori(0, 2 * KT) as i:
                e.activation(tile(wide, i), tile(wide, i), ACT.Sigmoid).then_inc(s_sg.sem, 1)
            with e.Fori(0, 2) as i:
                for r in range(4):
                    h = i * 4 + r
                    d_nm.wait(e, h + 1)
                    for n in range(NB):
                        seg = L[:, LO[n]:LO[n + 1]]
                        ins = e.activation(seg, seg, ACT.Exp, bias=dst_[:, 0, n:n + 1],
                                           accum_out=dst_[:, 1, n:n + 1])
                    ins.then_inc(d_ex.sem, 1)
                    d_tr.wait(e, h + 1)
                    e.activation(pT[:, :, :].rearrange("p c k -> p (c k)"),
                                 view(PS[:, 4, 0:1], [1, 10 * P]), ACT.Copy).then_inc(d_pt.sem, 1)
                    d_pv.wait(e, h + 1)
                    e.activation(tile(H, h), PS[:, 7, :], ACT.Copy).then_inc(d_o.sem, 1)

        @on("pool")
        def _(e):
            with e.Fori(0, KT) as i:
                s_silu.wait(e, i + 1)
                held(e)
                e.tensor_tensor(tile(qk, i), tile(qk, i), tile(wide, i + 16), ALU.mult)\
                    .then_inc(s_og.sem, 1)
            s_turn.wait(e, DH)
            with e.Fori(0, DH) as h:
                d_lg.wait(e, h)
                held(e)
                e.tensor_copy(qs[:, :], tile(wide, h + 24)).then_inc(d_qs.sem, 1)
                d_l.wait(e, h)
                held(e)
                for n in range(NB):
                    ins = e.tensor_tensor(BS[:, LO[n]:LO[n + 1]],
                                          bias[:, bass.ds(h, 1), 384 - n * P:512]
                                          .rearrange("p a s -> p (a s)"),
                                          sel[:, n, 0:(n + 1) * P], ALU.add)
                ins.then_inc(d_bs.sem, 1)

        @on("pe")
        def _(e):
            s_rin.wait(e, 32)
            for j in range(2):
                mm = e.matmul(PS[0:DH, 4 + j, 0:320], rb_[:, :], hot[:, j * 320:(j + 1) * 320],
                              start=True, stop=True)
            mm.then_inc(s_rmm.sem, 1)
            s_row.wait(e, 2)
            with e.Fori(0, 2) as i:
                for r in range(4):
                    h = i * 4 + r
                    d_qs.wait(e, h + 1)
                    d_l.wait(e, h)
                    for n in range(NB):
                        mm = e.matmul(PS[:, LB[n], OFF[n]:OFF[n] + (n + 1) * P],
                                      qs[:, n * P:(n + 1) * P], ckvT[:, 0:(n + 1) * P],
                                      start=True, stop=True)
                    mm.then_inc(d_lg.sem, 1)
                    w = tiles_of(use_slot(e, ng, i, 4, r))
                    if r == 0:
                        s_og.wait(e, KT)
                    evac_dve.wait(e, h + y_base)
                    for k in range(KT):
                        mm = e.matmul(PS[:, 3, :], w[:, k, :], qk[:, k, :], start=k == 0,
                                      stop=k == KT - 1)
                    mm.then_inc(slot_done.sem, 1)
                    d_nrm.wait(e, h + 1)
                    c = 0
                    for n in range(NB):
                        for kb in range(n + 1):
                            mm = e.transpose(view(PS[:, 4, c * P:c * P + 1], [1, P]) if c < 4 else
                                             PS[:, 4 + c // 4, (c % 4) * P:(c % 4 + 1) * P],
                                             L[:, c * P:(c + 1) * P], ident)
                            c += 1
                    mm.then_inc(d_tr.sem, 1)
                    d_pt.wait(e, h + 1)
                    d_o.wait(e, h)
                    c = 0
                    for n in range(NB):
                        for kb in range(n + 1):
                            mm = e.matmul(PS[:, 7, n * P:(n + 1) * P], ckv[:, kb, :], pT[:, c, :],
                                          start=kb == 0, stop=kb == n)
                            c += 1
                    mm.then_inc(d_pv.sem, 1)

        @on("dve")
        def _(e):
            s_bias.wait(e, 16 * DH)
            for h in range(DH):
                e.tensor_copy(bias[:, h, :], view(staged[h][:, S - 1:S], [-1, S]))\
                    .then_inc(s_turn.sem, 1)
            e.drain()
            with e.Fori(0, 2) as i:
                for r in range(4):
                    h = i * 4 + r
                    d_lg.wait(e, h + 1)
                    d_bs.wait(e, h + 1)
                    d_tr.wait(e, h)
                    for n in range(NB):
                        ins = e.scalar_tensor_tensor(
                            out=L[:, LO[n]:LO[n + 1]], in0=PS[:, LB[n], OFF[n]:OFF[n] + (n + 1) * P],
                            scalar=P ** -0.5, in1=BS[:, LO[n]:LO[n + 1]], op0=ALU.mult, op1=ALU.add)
                    ins.then_inc(d_l.sem, 1)
                    e.drain()
                    for n in range(NB):
                        ins = e.tensor_reduce(dst_[:, 0, n:n + 1], L[:, LO[n]:LO[n + 1]], AX.X,
                                              ALU.max, negate=True)
                    ins.then_inc(d_nm.sem, 1)
                    e.drain()
                    d_ex.wait(e, h + 1)
                    e.reciprocal(dst_[:, 2, :], dst_[:, 1, :])
                    e.drain()
                    for n in range(NB):
                        seg = L[:, LO[n]:LO[n + 1]]
                        ins = e.tensor_scalar(seg, seg, dst_[:, 2, n:n + 1], None, ALU.mult)
                    ins.then_inc(d_nrm.sem, 1)
                    slot_done.wait(e, i * 4 + (ng + r + 1))
                    if r == 0:
                        s_sg.wait(e, 2 * KT)
                    e.tensor_tensor(tile(wide, h), PS[:, 3, :], tile(wide, h), ALU.mult)\
                        .then_inc(evac_dve.sem, 1)

        on("pe")(lambda e: d_o.wait(e, DH))
        pe_gemm("dsa_out", KT, lambda k: H[:, k, :], free=evac_dve)
        merged = evac_dve.n

        def merge(e, t, bank):
            e.tensor_tensor(tile(wide, t + KT), bank, tile(wide, t + KT), ALU.mult)
            e.drain()
            return e.tensor_tensor(tile(wide, t), tile(wide, t + KT), tile(wide, t), ALU.add)
        evacuate("dve", "dsa_out", KT, merge, evac_dve)
        pe_gemm("mix_out", KT, lambda k: wide[:, k, :], (evac_dve, merged), free=evac_dve)
        evac_add("mix_out", KT)
        barrier()
        ds_.close()
        m.close()

    def ple():
        m = ExitStack()
        pT_ = sb(m, "p_T", [P, 2, S])
        pp = sb(m, "p_projected", [P, KT, S])
        gt = sb(m, "ple_gate", [P, KT, S])
        s_pin, s_pp, s_pl = sig("ple_in").by_dma(), sig("ple_proj"), sig("ple_out")
        on("act")(lambda e: e.dma_start(pT_[:, :, :], a["pT"].rearrange("(k p) s -> p k s", p=P))
                  .then_inc(s_pin.sem, 16))
        npj = START["ple_proj"]

        @on("pe")
        def _(e):
            s_pin.wait(e, 16)
            for j in range(2):
                w = use_slot(e, npj, 0, 4, j).rearrange("p (t k c) -> p t k c", t=4, k=2)
                for t in range(4):
                    if j == 1 and t == 3:
                        s_pp.wait(e, 1)
                    for k in range(2):
                        mm = e.matmul(PS[:, (4 * j + t) % 7, :], w[:, t, k, :], pT_[:, k, :],
                                      start=k == 0, stop=k == 1)
                mm.then_inc(slot_done.sem, 1)

        @on("act")
        def _(e):
            for t in range(KT):
                slot_done.wait(e, npj + t // 4 + 1)
                e.activation(pp[:, t, :], PS[:, t % 7, :], ACT.Copy).then_inc(s_pp.sem, 1)
        b_h = rms_norm("ple_n")
        on("pe")(lambda e: s_pp.wait(e, KT))
        pe_gemm("ple_gate", KT, lambda k: H[:, k, :], (s_h, b_h))
        g0 = evac_act.n
        evacuate("act", "ple_gate", KT, lambda e, t, bank: e.activation(tile(gt, t), bank, ACT.Sigmoid),
                 evac_act)
        s_pl.plan(KT)

        @on("dve")
        def _(e):
            e.drain()
            for t in range(KT):
                evac_act.wait(e, g0 + t + 1)
                e.tensor_tensor(gt[:, t, :], gt[:, t, :], pp[:, t, :], ALU.mult)
                e.drain()
                e.tensor_tensor(X[:, t, :], X[:, t, :], gt[:, t, :], ALU.add).then_inc(s_pl.sem, 1)
        rms_norm("final2", ready=(s_pl, 0))
        m.close()

    phases = [mixer1, peer, lambda: ffn(1), mixer2, lambda: ffn(2), ple]
    if start:
        skip_constants()
    for n, f in enumerate(phases):
        if n >= start:
            f()
        if n + 1 == stop:
            return finish(phase.n)
    finish()


def tiles(w, K=KT):
    n = w.shape[1] // P
    return w.reshape(K, P, n, P).transpose(2, 1, 0, 3).reshape(n, P, K * P)


def columns(v):
    return v.reshape(-1, P).T


def stream_parts(i):
    w_in = i["w_in"][0]
    val, gate, q, k, v, gates = (w_in[:, s:e] for s, e in (
        (0, 1024), (1024, 2048), (2048, 3072), (3072, 3200), (3200, 3328), (3328, 5376)))
    yield "glu", np.stack([tiles(gate), tiles(val)], 1).reshape(16, P, D)
    yield "q", tiles(q)
    yield "kv", tiles(np.concatenate([k[:, :64], k[:, :64], k[:, 64:], k[:, 64:], v], 1))
    yield "gates", tiles(gates)
    yield "attn_o", tiles(i["w_attn_o"][0])
    yield "conv_out", tiles(i["w_conv_out"][0])
    yield "w_out", tiles(i["w_out"][0])
    u = i["peer_u"][0].reshape(NKEY, NKEY, KT, P).transpose(1, 3, 2, 0).reshape(NKEY, P, D)
    pq = tiles(i["w_peer_q"][0]).reshape(PH, 2, P, D)
    yield "peer_q_u0", np.concatenate([pq, u[:JQ].reshape(PH, 2, P, D)], 1).reshape(32, P, D)
    v = i["peer_v"][0].reshape(NKEY, NQ, JQ // 2, 2, 2, D // 2).transpose(1, 4, 2, 0, 3, 5)
    for q_ in range(NQ):
        if q_:
            yield f"u{q_}", u[q_ * JQ:(q_ + 1) * JQ]
        yield f"v{q_}", v[q_].reshape(JQ, P, D)


def stream_parts2(i):
    for n in (1, 2):
        w = i[f"ffn{n}_w_in_2"][0]
        yield f"f{n}_in", np.stack([tiles(w[:, :FT * P]), tiles(w[:, FT * P:])], 1).reshape(-1, P, D)
        yield f"f{n}_out", i[f"ffn{n}_w_out_2"][0].reshape(FT, P, D)
    w = i["mix_w_in_2"][0]
    at = np.cumsum([0, 512, 512, 1024, 1024, 16, 1024, 128, 512, 64, 8, 2048])
    gq, gk, gv, gr, ga, dq, dkv, iq, ik, iw, gates = (w[:, s:e] for s, e in zip(at[:-1], at[1:]))
    yield "misc", tiles(np.concatenate([ga, iw, np.zeros((D, P - 24), np.float32)], 1))
    yield "ik", tiles(np.concatenate([ik, ik], 1))
    yield "iq", tiles(iq)
    yield "dkv", tiles(dkv)
    yield "gqk", np.stack([tiles(gq), tiles(gk)], 1).reshape(8, P, D)
    yield "gv", gv.reshape(4, 2, P, 2, 512).transpose(3, 0, 2, 1, 4).reshape(8, P, D)
    yield "wide2", tiles(np.concatenate([gates, gr, dq], 1))
    yield "gla_out", tiles(i["gla_w_out_2"][0])
    yield "dsa_out", tiles(i["dsa_w_out_2"][0])
    yield "mix_out", tiles(i["mix_w_out_2"][0])
    yield "ple_proj", i["ple_w_proj_2"][0].reshape(2, P, 2, 4, P).transpose(2, 1, 3, 0, 4).reshape(2, P, D)
    yield "ple_gate", tiles(i["ple_w_gate_2"][0])


def level_masks():
    s_, t_ = np.arange(P)[:, None], np.arange(P)[None]
    m_ = [(s_ // (2 * h) == t_ // (2 * h)) & (s_ % (2 * h) < h) & (t_ % (2 * h) >= h)
          for h in (64 >> l for l in range(7))]
    return np.stack(m_ + [s_ == t_], 1).astype(np.float32)


def bucket_rows():
    dist = np.maximum(np.arange(640) - (P - 1), 0)
    large = 16 + (np.log(np.maximum(dist, 1) / 16.0) / np.log(8.0) * 16).astype(np.int32)
    bucket = np.where(dist < 16, dist, np.minimum(large, 31))
    return (np.arange(32)[:, None] == bucket[None]).astype(np.float32)


def lay_out(i):
    stream = np.zeros((SLOTS, P, D), np.float32)
    for name, part in [*stream_parts(i), *stream_parts2(i)]:
        stream[START[name]:START[name] + len(part)] = part
    b = i["b_in"][0]
    d = np.arange(P)
    rot = np.zeros((P, P), np.float32)
    for m_ in range(P):
        if m_ % 64 < 32:
            rot[m_ + 32, m_] = -1.0
        else:
            rot[m_ - 32, m_] = 1.0
    squares = np.concatenate([np.eye(P), np.full((P, P), 1.0 / D), rot,
                              np.broadcast_to(d, (P, P))], 1).astype(np.float32)
    inv = (10000.0 ** (-(np.arange(32) * 2.0 / HD))).astype(np.float32)
    one = np.ones((P, 1), np.float32)
    cols = {
        "norm1": columns(i["norm1_g"]),
        "b_glu": np.stack([columns(b[1024:2048]), columns(b[:1024])], 2).reshape(P, 16),
        "b_q": columns(b[2048:3072]),
        "b_k": columns(np.concatenate([b[3072:3136], b[3072:3136], b[3136:3200], b[3136:3200]])),
        "b_gates": columns(b[3328:5376]),
        "conv_w": i["conv_w"][0].reshape(TAPS, KT, P).transpose(2, 0, 1).reshape(P, -1),
        "conv_b": columns(i["conv_b"]), "ln_g": columns(i["conv_ln_g"]),
        "ln_b": columns(i["conv_ln_b"]), "norm2": columns(i["norm2_g"]),
        "final1": columns(i["final_g"]), "ffn1_n": columns(i["ffn1_norm_2"]),
        "mix_n": columns(i["mix_norm_2"]), "alpha_b": columns(i["gla_alpha_b_2"]),
        "gla_n": columns(i["gla_out_norm_2"]), "ckv_n": columns(i["ckv_norm_2"]),
        "ffn2_n": columns(i["ffn2_norm_2"]), "ple_n": columns(i["ple_norm_2"]),
        "final2": columns(i["final_norm_2"]), "inv_freq": inv[d % 32][:, None],
        "eps": EPS * one, "half_pi": np.float32(np.pi / 2) * one, "one": one, "zero": 0 * one,
    }
    q, k = np.arange(P)[:, None], np.arange(2 * P)[None]
    rel = q + P - k
    band = (rel >= 0) & (rel < P)
    band = np.stack([band & ((k >= P) | (n > 0)) for n in range(NB)], 1)
    return {
        "alpha_w": i["gla_alpha_w_2"][0], "level_mask": level_masks(),
        "causal": np.where(np.arange(P)[None] <= np.arange(P)[:, None], 0.0, NEG).astype(np.float32),
        "buckets": bucket_rows(), "rel_bias": i["rel_bias_2"], "pT": i["p_2"][0, 0].T,
        "keysT": i["peer_sub_keys"][0].reshape(2 * PH, NKEY, P).transpose(2, 0, 1),
        "xT": i["x"][0].T, "stream": stream,
        "cols": np.concatenate([cols[n] for n, _ in COLS], 1).astype(np.float32),
        "squares": squares, "band_mask": np.where(band, 0.0, NEG).astype(np.float32),
        "positions": i["positions"][0], "sinks": i["attn_sinks"][0], "b_v": b[3200:3328],
    }


def kernel(**inputs):
    import concourse.bacc as bacc
    from concourse.bass_utils import run_bass_kernel_spmd
    arrays = {k: np.ascontiguousarray(v) for k, v in
              lay_out({k: np.asarray(v) for k, v in inputs.items()}).items()}
    nc = bacc.Bacc("TRN2", target_bir_lowering=False, num_devices=1)
    a = {n: nc.dram_tensor("in_" + n, v.shape, mybir.dt.from_np(v.dtype), kind="ExternalInput").ap()
         for n, v in arrays.items()}
    out = nc.dram_tensor("out", (D, S), F32, kind="ExternalOutput").ap()
    build(nc, a, out)
    r = run_bass_kernel_spmd(nc, [{"in_" + n: v for n, v in arrays.items()}], core_ids=[0])
    return np.ascontiguousarray(r.results[0]["out"].T)[None]
```

```python
from contextlib import ExitStack

import numpy as np
import concourse.bass as bass
from concourse import mybir

F32 = mybir.dt.float32
BF16 = mybir.dt.bfloat16
F32R = mybir.dt.float32r
I32 = mybir.dt.int32
U32 = mybir.dt.uint32
ALU = mybir.AluOpType
ACT = mybir.ActivationFunctionType
AX = mybir.AxisListType

P = 128
S = 512
D = 1024
KT = D // P
NB = S // P
TAPS = 31
HEADS, HD = 16, 64
PH, NKEY, TOPK = 8, 128, 16
NQ = 8
JQ = NKEY // NQ
FT = 2816 // P
GH, GDV = 4, 256
DH = 8
SEL = 128
EPS = 1e-6
NEG = -1e30
TAKEN = -3e38
RING = 4
THREE = ((0, 0), (0, 1), (1, 0))
TWO_PI = 6.283185307179586
MAGIC = 12582912.0

STREAM = [
    ("glu", 16), ("q", 8), ("kv", 3), ("gates", 16), ("attn_o", 8), ("conv_out", 8), ("w_out", 8),
    ("peer_q_u0", 32), ("u1", 16),
    *[(f"{kind}{q_ + 2 * (kind == 'u')}", 16) for q_ in range(6) for kind in "vu"],
    ("v6", 16), ("v7", 16),
    ("f1_in", 44), ("f1_out", 22),
    ("misc", 1), ("ik", 1), ("iq", 4), ("dkv", 1), ("gqk", 8), ("gv", 8), ("wide2", 32),
    ("gla_out", 8), ("dsa_out", 8), ("mix_out", 8),
    ("f2_in", 44), ("f2_out", 22), ("ple_proj", 2), ("ple_gate", 8),
]
START = {}
SLOTS = 0
for _name, _k in STREAM:
    START[_name] = SLOTS
    SLOTS += _k

COLS = [
    ("norm1", 8), ("b_glu", 16), ("b_q", 8), ("b_k", 2), ("b_gates", 16), ("conv_w", 8 * TAPS),
    ("conv_b", 8), ("ln_g", 8), ("ln_b", 8), ("norm2", 8), ("final1", 8), ("ffn1_n", 8),
    ("mix_n", 8), ("alpha_b", 4), ("gla_n", 8), ("ckv_n", 1), ("ffn2_n", 8), ("ple_n", 8),
    ("final2", 8), ("inv_freq", 1), ("eps", 1), ("half_pi", 1), ("one", 1), ("zero", 1),
]
COL = {}
_n = 0
for _name, _k in COLS:
    COL[_name] = _n
    _n += _k
NCOLS = _n
SQ = {"ident": 0, "mean": 128, "rot": 256, "iota": 384}
MAXD = 639


class Signal:

    def __init__(self, nc, ctx, name):
        self.sem = ctx.enter_context(nc.semaphore(name))
        self.n = 0
        self.first = 1

    def by_dma(self):
        self.first = 0
        return self

    def plan(self, k):
        base = self.n
        self.n += k
        return base

    def wait(self, e, value):
        e.wait_ge(self.sem, value + self.first)


def build(nc, a, out, stop=99, start=0):
    ctx = ExitStack()
    queues = {"pe": [], "act": [], "dve": [], "pool": [], "sp": []}

    def on(engine):
        def put(f):
            queues[engine].append(f)
            return f
        return put

    def sb(c, name, shape, dt=F32):
        return c.enter_context(nc.sbuf_tensor(name, shape, dt))

    def names(c, shape, plain, *rounded):
        out = []
        for n_, name in enumerate((plain, *rounded)):
            with ExitStack() as here:
                out.append(sb(c if n_ == len(rounded) else here, name, shape, F32R if n_ else F32))
        return out

    total = {1: START["peer_q_u0"], 2: START["f1_in"], 3: START["misc"], 4: START["f2_in"],
             5: START["ple_proj"]}.get(stop, SLOTS)
    signals = {}

    def sig(name):
        if name not in signals:
            signals[name] = Signal(nc, ctx, "s_" + name)
        return signals[name]

    def tile(T, t):
        if isinstance(t, int):
            return T[:, t, :]
        return T[:, bass.ds(t, 1), :].rearrange("p a s -> p (a s)")

    def col(T, c):
        return T[:, c:c + 1] if isinstance(c, int) else T[:, bass.ds(c, 1)]

    def view(ap, *dims):
        return bass.AP(tensor=ap.tensor, offset=ap.offset, ap=[ap.ap[0], *[list(d) for d in dims]])

    X = sb(ctx, "x_res", [P, KT, S])
    H, Hh, Hl = names(ctx, [P, KT, S], "h_norm", "h_norm_hi", "h_low")
    ring = sb(ctx, "ring", [P, RING, D])
    cst = sb(ctx, "cst", [P, NCOLS])
    sq = sb(ctx, "squares_const", [P, 512])
    norm_sq = sb(ctx, "norm_sq", [P, 2, S])
    norm_r = sb(ctx, "norm_r", [P, S])
    root_warm = sb(ctx, "root_warm", [P, 1])
    PS = ctx.enter_context(nc.psum_tensor("ps", [P, 8, 512], F32))
    ident = sq[:, SQ["ident"]:SQ["ident"] + P]
    mean = sq[:, SQ["mean"]:SQ["mean"] + P]
    rot = sq[:, SQ["rot"]:SQ["rot"] + P]
    iota = sq[:, SQ["iota"]:SQ["iota"] + P]

    def c_(name, i=0):
        return cst[:, COL[name] + i:COL[name] + i + 1]

    def cd(name, i):
        return col(cst, i + COL[name])

    arrive = [ctx.enter_context(nc.semaphore(f"s_slot{r}")) for r in range(RING)]
    slot_done = sig("slot_done")
    s_const = sig("const").by_dma()
    evac_act = sig("evac_act")
    evac_dve = sig("evac_dve")
    phase = sig("phase")

    on("act")(lambda e: e.sem_inc(evac_act.sem, 4))
    on("dve")(lambda e: e.sem_inc(evac_dve.sem, 4))
    evac_act.n = evac_dve.n = 4
    glu_gate = sig("glu_gate")
    glu_done = sig("glu_done")
    on("dve")(lambda e: e.sem_inc(glu_done.sem, 2))
    glu_done.n = 2
    slot_done.n = 0

    @on("sp")
    def _(e):
        e.dma_start(cst[:, :], a["cols"]).then_inc(s_const.sem, 16)
        e.dma_start(X[:, :, :], a["xT"].rearrange("(k p) s -> p k s", p=P)).then_inc(s_const.sem, 16)
        e.dma_start(sq[:, :], a["squares"]).then_inc(s_const.sem, 16)
        for r in range(RING):
            e.dma_start(ring[:, r, :], a["stream"][r]).then_inc(arrive[r], 16)
        with e.Fori(1, total // RING) as i:
            for r in range(RING):
                slot_done.wait(e, (i - 1) * RING + r + 1)
                e.dma_start(ring[:, r, :], a["stream"][i * RING + r]).then_inc(arrive[r], 16)
        for n in range(total // RING * RING, total):
            slot_done.wait(e, n - RING + 1)
            e.dma_start(ring[:, n % RING, :], a["stream"][n]).then_inc(arrive[n % RING], 16)
    CONST_IN = 48

    s_held = sig("held")

    def held(e):
        e.sem_inc(s_held.sem, 1)

    def skip_constants():
        for name in ("pe", "act", "dve", "pool"):
            on(name)(lambda e: s_const.wait(e, CONST_IN))

    def barrier():
        phase.plan(4)
        want = phase.n
        for name in ("pe", "act", "dve", "pool"):
            def f(e):
                e.drain().then_inc(phase.sem, 1)
                phase.wait(e, want)
            on(name)(f)

    def use_slot(e, n0, i, per, r):
        n = n0 + r
        e.wait_ge(arrive[n % RING], i * (16 * per // RING) + 16 * (n // RING + 1))
        return ring[:, n % RING, :]

    def tiles_of(slot):
        return slot.rearrange("p (k c) -> p k c", k=KT)

    s_hi, s_lo = sig("slot_hi"), sig("slot_lo")

    class Split:

        def __init__(self, m, name, first, count, buffers=RING, later=False):
            self.parts = sb(m, name, [P, buffers, 2, D], F32R)
            self.buffers = buffers
            self.first, self.count = first, count
            if not later:
                self.plan()

        def plan(self):
            self.base = s_hi.plan(self.count) - self.first
            s_lo.plan(self.count)

        def hi(self, e, i, per, n):
            b = n % self.buffers
            e.wait_ge(arrive[n % RING], i * (16 * per // RING) + 16 * (n // RING + 1))
            slot_done.wait(e, i * per + (n - self.buffers + 1))
            e.activation(self.parts[:, b, 0, :], ring[:, n % RING, :], ACT.Copy)\
                .then_inc(s_hi.sem, 1)

        def lo(self, e, i, per, n):
            b = n % self.buffers
            s_hi.wait(e, i * per + (n + self.base + 1))
            held(e)
            e.tensor_tensor(self.parts[:, b, 1, :], ring[:, n % RING, :],
                            self.parts[:, b, 0, :].bitcast(F32), ALU.subtract).then_inc(s_lo.sem, 1)

        def use(self, e, i, per, n):
            s_lo.wait(e, i * per + (n + self.base + 1))
            return [tiles_of(self.parts[:, n % self.buffers, v, :]) for v in range(2)]

        def lows(self, first, count):
            @on("pool")
            def _(e):
                self.loop(e, self.lo, first, count)

        def loop(self, e, f, first, count):
            if count >= 8:
                with e.Fori(0, count // 4) as i:
                    for r in range(4):
                        f(e, i, 4, first + r)
                first, count = first + count // 4 * 4, count % 4
            for r in range(count):
                f(e, 0, 4, first + r)

    def product3(e, psum, w, k, x, start, stop):
        for v, (a_, b_) in enumerate(THREE):
            mm = e.matmul(psum, w[a_][:, k, :], x[b_], start=start and v == 0, stop=stop and v == 2)
        return mm

    def pe_gemm(name, n, rhs, first_wait=None, free=evac_act, banks=(0, 1, 2, 3), split=None):
        n0 = START[name]
        fbase = free.n
        others = [(s, s.n) for s in (evac_act, evac_dve, glu_done)]

        def one(e, i, r):
            w = split.use(e, i, 4, n0 + r) if split else tiles_of(use_slot(e, n0, i, 4, r))
            free.wait(e, i * 4 + (fbase + r - 3))
            for k in range(KT):
                if first_wait and isinstance(i, int) and i == 0 and r == 0:
                    first_wait[0].wait(e, first_wait[1] + k + 1)
                if split:
                    m = product3(e, PS[:, banks[r], :], w, k, rhs(k), k == 0, k == KT - 1)
                else:
                    m = e.matmul(PS[:, banks[r], :], w[:, k, :], rhs(k), start=k == 0,
                                 stop=k == KT - 1)
            m.then_inc(slot_done.sem, 1)

        @on("pe")
        def _(e):
            for s, v in others:
                s.wait(e, v)
            for r in range(min(4, n)):
                one(e, 0, r)
            if n >= 8:
                with e.Fori(1, n // 4) as i:
                    for r in range(4):
                        one(e, i, r)
        return n0

    def evacuate(engine, name, n, op, done, before=None, banks=(0, 1, 2, 3), split=None, ahead=2,
                 slots_after=0):
        n0 = START[name]
        done.plan(n)

        @on(engine)
        def _(e):
            if before:
                before(e)

            def one(i, r):
                if split and not (isinstance(i, int) and 4 * i + r + ahead >= n + slots_after):
                    split.hi(e, i, 4, n0 + r + ahead)
                slot_done.wait(e, i * 4 + (n0 + r + 1))
                op(e, i * 4 + r, PS[:, banks[r], :]).then_inc(done.sem, 1)
            if n < 8:
                for r in range(n):
                    one(0, r)
            else:
                with e.Fori(0, n // 4 - 1) as i:
                    for r in range(4):
                        one(i, r)
                for r in range(4):
                    one(n // 4 - 1, r)

    s_sq, s_sqmm, s_root, s_h = sig("norm_sq"), sig("norm_mm"), sig("norm_root"), sig("norm_h")
    s_inv = sig("norm_inv")

    s_nh, s_np = sig("norm_hi"), sig("norm_product")

    def norm_root(bank=7, ready=None):
        b_sq, b_mm, b_root, b_inv = s_sq.plan(KT), s_sqmm.plan(KT), s_root.plan(1), s_inv.plan(1)
        b_h = s_h.n

        @on("act")
        def _(e):
            e.activation(root_warm[:, :], c_("one"), ACT.Sqrt)
            for k in range(KT):
                if ready:
                    ready[0].wait(e, ready[1] + k + 1)
                if k >= 2:
                    s_sqmm.wait(e, b_mm + k - 1)
                elif b_mm:
                    s_sqmm.wait(e, b_mm)
                e.activation(norm_sq[:, k % 2, :], X[:, k, :], ACT.Square).then_inc(s_sq.sem, 1)
            s_sqmm.wait(e, b_mm + KT)
            if b_h:
                s_h.wait(e, b_h)
            e.activation(norm_r[:, :], PS[:, bank, :], ACT.Sqrt, bias=c_("eps")).then_inc(s_root.sem, 1)

        @on("pe")
        def _(e):
            for k in range(KT):
                s_sq.wait(e, b_sq + k + 1)
                e.matmul(PS[:, bank, :], mean, norm_sq[:, k % 2, :], start=k == 0,
                         stop=k == KT - 1).then_inc(s_sqmm.sem, 1)

        @on("dve")
        def _(e):
            s_root.wait(e, b_root + 1)
            e.reciprocal(norm_r[:, :], norm_r[:, :]).then_inc(s_inv.sem, 1)
            s_inv.wait(e, b_inv + 1)

    def norm_apply(gain, dst=H, split=None, parts_last=False):
        b_h = s_h.plan(KT)
        if split:
            b_np, b_nh = s_np.plan(KT), s_nh.plan(KT)

            @on("act")
            def _(e):
                for k in range(KT):
                    s_np.wait(e, b_np + k + 1)
                    e.activation(split[0][:, k, :], split[2][:, k % split[2].shape[1], :], ACT.Copy)\
                        .then_inc(s_nh.sem, 1)

        @on("dve")
        def _(e):
            def product(t, k):
                return e.scalar_tensor_tensor(out=t, in0=X[:, k, :], scalar=c_(gain, k),
                                              in1=norm_r[:, :], op0=ALU.mult, op1=ALU.mult)
            if not split:
                for k in range(KT):
                    product(dst[:, k, :], k).then_inc(s_h.sem, 1)
                return
            high, low, t = split
            late = KT if parts_last else 1
            for k in range(KT + late):
                if k < KT:
                    product(t[:, k % t.shape[1], :], k).then_inc(s_np.sem, 1)
                if k >= late:
                    j = k - late
                    s_nh.wait(e, b_nh + j + 1)
                    e.tensor_tensor(low[:, j, :], t[:, j % t.shape[1], :],
                                    high[:, j, :].bitcast(F32), ALU.subtract)\
                        .then_inc(s_h.sem, 1)
        return b_h

    def finish(last=None):
        s_out = sig("out").by_dma()
        want = s_h.n if last is None else last

        @on("sp")
        def _(e):
            if last is None:
                s_h.wait(e, want)
                src = H
            else:
                phase.wait(e, want)
                src = X
            e.dma_start(out.rearrange("(k p) s -> p k s", p=P), src[:, :, :]).then_inc(s_out.sem, 16)
            s_out.wait(e, 16)
        go = ctx.enter_context(nc.semaphore("s_go"))
        seeded = [x.sem for x in signals.values() if x.first]
        queues["pool"].insert(0, lambda e: [e.sem_inc(x, 1) for x in seeded + [go]])
        for name in ("pe", "act", "dve"):
            queues[name].insert(0, lambda e: e.wait_ge(go, 1))
        with nc.Block() as block:
            for name, deco in (("sp", block.sync), ("pe", block.tensor), ("act", block.scalar),
                               ("dve", block.vector), ("pool", block.gpsimd)):
                def program(e, name=name):
                    for f in queues[name]:
                        f(e)
                deco(program)
        ctx.close()


    def glu(name, pairs, tmp, act, func, value, first_wait, split=None, x=None, ahead=2):
        n0 = START[name]
        others = [(s, s.n) for s in (evac_act, evac_dve, glu_done)]
        b_gate, b_done = glu_gate.plan(pairs), glu_done.plan(pairs)

        def loop(e, one):
            for r in range(2):
                one(e, 0, r)
            with e.Fori(1, pairs // 2) as i:
                for r in range(2):
                    one(e, i, r)

        @on("pe")
        def _(e):
            for s, v in others:
                s.wait(e, v)

            def one(e, i, r):
                for j in range(2):
                    w = (split.use(e, i, 4, n0 + 2 * r + j) if split else
                         tiles_of(use_slot(e, n0, i, 4, 2 * r + j)))
                    glu_done.wait(e, i * 2 + (b_done + r - 1))
                    for k in range(KT):
                        if isinstance(i, int) and r == 0 and j == 0:
                            first_wait[0].wait(e, first_wait[1] + k + 1)
                        if split:
                            m = product3(e, PS[:, 2 * r + j, :], w, k, (x[0][:, k, :], x[1][:, k, :]),
                                         k == 0, k == KT - 1)
                            continue
                        m = e.matmul(PS[:, 2 * r + j, :], w[:, k, :], H[:, k, :], start=k == 0,
                                     stop=k == KT - 1)
                    m.then_inc(slot_done.sem, 1)
            loop(e, one)

        @on("act")
        def _(e):
            def one(e, i, r):
                if split:
                    split.hi(e, i, 4, n0 + 2 * r + ahead)
                slot_done.wait(e, i * 4 + (n0 + 2 * r + 1))
                glu_done.wait(e, i * 2 + (b_done + r - 1))
                act(e, i * 2 + r, tmp[:, r, :], PS[:, 2 * r, :], func).then_inc(glu_gate.sem, 1)
                if split:
                    split.hi(e, i, 4, n0 + 2 * r + ahead + 1)
            loop(e, one)

        @on("dve")
        def _(e):
            def one(e, i, r):
                slot_done.wait(e, i * 4 + (n0 + 2 * r + 2))
                glu_gate.wait(e, i * 2 + (b_gate + r + 1))
                value(e, i * 2 + r, PS[:, 2 * r + 1, :], tmp[:, r, :]).then_inc(glu_done.sem, 1)
            loop(e, one)

    def evac_add(name, n, scale=1.0):
        def op(e, t, bank):
            return e.scalar_tensor_tensor(out=tile(X, t), in0=bank, scalar=scale, in1=tile(X, t),
                                          op0=ALU.mult, op1=ALU.add)
        evacuate("dve", name, n, op, evac_dve)

    def mixer1():
        m = ExitStack()
        with ExitStack() as last:
            q_hi = sb(last, "m1_merged_hi", [P, KT, S], F32R)
        U = sb(m, "conv_in", [P, KT, TAPS - 1 + S])
        Y, Y_lo = names(m, [P, KT, S], "conv_out", "conv_out_lo")
        Q, Q_lo = names(m, [P, KT, S], "q_raw", "m1_merged_lo")
        with ExitStack() as last:
            O_lo = sb(last, "attn_lo", [P, KT, S], F32R)
        with ExitStack() as first:
            xh, xl = [sb(first, "m1_x_" + v, [P, KT, S], F32R) for v in ("hi", "lo")]
            split = Split(first, "m1_slots", 0, START["gates"], 2)
        O = sb(m, "attn_T", [P, KT, S])
        G = sb(m, "gates", [P, 2 * KT, S])
        with ExitStack() as last:
            tail = Split(last, "m1_last_slots", START["attn_o"], 3 * KT, 2, later=True)
            z_hi = sb(last, "m1_rhs_hi", [P, KT, S], F32R)
        kz = sb(m, "k_padded", [P, 4, P + S])
        V = sb(m, "v_tokens", [P, NB + 1, P])
        cos, sin = sb(m, "cos", [P, S]), sb(m, "sin", [P, S])
        M = sb(m, "band_mask", [P, NB, 2 * P])
        qr = sb(m, "q_roped", [P, 2, S])
        Sb = sb(m, "scores", [P, 2, NB, 2 * P])
        pT = sb(m, "probs_T", [P, 2, 2 * NB, P])
        ra, rb = sb(m, "rope_a", [P, S]), sb(m, "rope_b", [P, S])
        osb = sb(m, "o_tokens", [P, NB, P])
        sinks = sb(m, "sinks", [P, HEADS])
        bv = sb(m, "b_v", [P, P])
        st = sb(m, "stats", [P, 2, 6, NB])
        tmp2 = Sb[:, :, 0:2, :].rearrange("p a b c -> p a (b c)")

        s_in, s_pos = sig("m1_in").by_dma(), sig("positions").by_dma()

        @on("act")
        def _(e):
            e.dma_start(rb[:, :].bitcast(I32), a["positions"].partition_broadcast(P)).then_inc(s_pos.sem, 16)
            e.dma_start(M[:, :, :], a["band_mask"]).then_inc(s_in.sem, 16)
            e.dma_start(sinks[:, :], a["sinks"].partition_broadcast(P)).then_inc(s_in.sem, 16)
            e.dma_start(bv[:, :], a["b_v"].partition_broadcast(P)).then_inc(s_in.sem, 16)
            s_const.wait(e, CONST_IN)

        s_zero = sig("m1_zero")

        @on("pool")
        def _(e):
            e.memset(U[:, :, 0:TAPS - 1], 0.0)
            e.memset(kz[:, :, :], 0.0)
            e.memset(V[:, 0, :], 0.0).then_inc(s_zero.sem, 1)

        on("pe")(lambda e: s_const.wait(e, CONST_IN))
        on("dve")(lambda e: s_const.wait(e, CONST_IN))

        s_ang, s_trig = sig("m1_angles"), sig("m1_trig")

        @on("dve")
        def _(e):
            s_pos.wait(e, 16)
            e.tensor_scalar(ra[:, :], rb[:, :].bitcast(I32), c_("inv_freq"), None, ALU.mult)
            for shift, dst in ((0.0, sin), (0.25, cos)):
                e.drain()
                e.tensor_scalar(dst[:, :], ra[:, :], 1.0 / TWO_PI, shift, ALU.mult, ALU.add)
                e.drain()
                e.tensor_scalar(dst[:, :], dst[:, :], MAGIC, None, ALU.add)
                e.drain()
                e.tensor_scalar(qr[:, 0, :], dst[:, :], MAGIC, None, ALU.subtract)
                e.drain()
                e.scalar_tensor_tensor(out=dst[:, :], in0=qr[:, 0, :], scalar=-6.28125,
                                       in1=ra[:, :], op0=ALU.mult, op1=ALU.add)
                for part in (-1.9350051879882812e-3, -3.01991598195675e-7):
                    e.drain()
                    e.scalar_tensor_tensor(out=dst[:, :], in0=qr[:, 0, :], scalar=part,
                                           in1=dst[:, :], op0=ALU.mult, op1=ALU.add)
                if shift:
                    e.drain()
                    e.tensor_scalar(dst[:, :], dst[:, :], TWO_PI / 4, None, ALU.add)
                e.drain()
                e.tensor_scalar(dst[:, :], dst[:, :], 3.1415925, -3.1415925, ALU.min, ALU.max)\
                    .then_inc(s_ang.sem, 1)

        norm_root()
        split.lows(0, START["gates"])
        on("act")(lambda e: split.hi(e, 0, 4, 0))
        b_h = norm_apply("norm1", split=(xh, xl, H))

        @on("act")
        def _(e):
            for n, dst in enumerate((sin, cos)):
                s_ang.wait(e, n + 1)
                e.activation(dst[:, :], dst[:, :], ACT.Sin).then_inc(s_trig.sem, 1)

        on("dve")(lambda e: s_in.wait(e, 48))

        on("dve")(lambda e: s_zero.wait(e, 1))
        glu("glu", KT, tmp2,
            lambda e, p, t, bank, f: e.activation(t, bank, f, bias=cd("b_glu", p * 2)),
            ACT.Sigmoid,
            lambda e, p, bank, t: e.scalar_tensor_tensor(
                out=(U[:, p, TAPS - 1:] if isinstance(p, int) else
                     U[:, bass.ds(p, 1), TAPS - 1:].rearrange("p a s -> p (a s)")),
                in0=bank, scalar=cd("b_glu", p * 2 + 1), in1=t, op0=ALU.add, op1=ALU.mult),
            (s_h, b_h), split, (xh, xl), 1)

        pe_gemm("q", KT, lambda k: (xh[:, k, :], xl[:, k, :]), split=split)
        evacuate("act", "q", KT,
                 lambda e, t, bank: e.activation(tile(Q, t), bank, ACT.Identity, bias=cd("b_q", t)),
                 evac_act, split=split, ahead=1, slots_after=1)
        q_in = evac_act.n

        n_kv = START["kv"]
        k_raw = pT[:, :, 0:NB, :].rearrange("p a n c -> p a (n c)")
        e_act, e_dve = evac_act.n, evac_dve.n
        evac_act.plan(2)
        evac_dve.plan(1)
        s_kr, s_kc, s_kz, s_v = sig("k_rot"), sig("k_cos"), sig("k_done"), sig("v_done")

        @on("pe")
        def _(e):
            evac_act.wait(e, e_act)
            for j in range(2):
                w = split.use(e, 0, 4, n_kv + j)
                for k in range(KT):
                    mm = product3(e, PS[:, j, :], w, k, (xh[:, k, :], xl[:, k, :]), k == 0,
                                  k == KT - 1)
                mm.then_inc(slot_done.sem, 1)
            w = split.use(e, 0, 4, n_kv + 2)
            for n in range(NB):
                for k in range(KT):
                    for y, (a_, b_) in enumerate(THREE):
                        mm = e.matmul(PS[:, 2, n * P:(n + 1) * P],
                                      (xh, xl)[b_][:, k, n * P:(n + 1) * P], w[a_][:, k, :],
                                      start=k == 0 and y == 0, stop=k == KT - 1 and y == 2)
            mm.then_inc(slot_done.sem, 1)
            for j in range(2):
                evac_act.wait(e, e_act + j + 1)
                e.matmul(PS[:, 4 + j, :], rot, k_raw[:, j, :], start=True, stop=True).then_inc(s_kr.sem, 1)

        @on("act")
        def _(e):
            for j in range(2):
                split.hi(e, 0, 4, n_kv + j + 1)
                slot_done.wait(e, n_kv + j + 1)
                e.activation(k_raw[:, j, :], PS[:, j, :], ACT.Identity, bias=c_("b_k", j))\
                    .then_inc(evac_act.sem, 1)

        @on("pool")
        def _(e):
            s_trig.wait(e, 2)
            for j in range(2):
                evac_act.wait(e, e_act + j + 1)
                e.tensor_tensor(qr[:, j, :], k_raw[:, j, :], cos[:, :], ALU.mult).then_inc(s_kc.sem, 1)

        EARLY = 9

        @on("dve")
        def _(e):
            e.drain()
            for c in range(KT):
                e.tensor_scalar(Y[:, c, :], U[:, c, 0:S], c_("conv_w", c), c_("conv_b", c),
                                ALU.mult, ALU.add)
            with e.Fori(1, 1 + EARLY) as w:
                tap(e, w)

        @on("dve")
        def _(e):
            slot_done.wait(e, n_kv + 3)
            e.tensor_tensor(V[:, 1:, :], PS[:, 2, :].rearrange("p (n c) -> p n c", n=NB),
                            view(bv[:, :], [0, NB], [1, P]), ALU.add).then_inc(evac_dve.sem, 1)
            s_trig.wait(e, 2)
            for j in range(2):
                e.drain()
                s_kr.wait(e, j + 1)
                s_kc.wait(e, j + 1)
                e.tensor_tensor(rb[:, :], PS[:, 4 + j, :], sin[:, :], ALU.mult)
                e.drain()
                for half in range(2):
                    h = slice(64 * half, 64 * half + 64)
                    e.tensor_tensor(kz[h, 2 * j + half, P:], qr[h, j, :], rb[h, :], ALU.add)\
                        .then_inc(s_kz.sem, 1)

        def tap(e, w):
            e.drain()
            for c in range(KT):
                e.scalar_tensor_tensor(out=Y[:, c, :], in0=U[:, c, bass.ds(w, S)],
                                       scalar=cd("conv_w", w * KT + c), in1=Y[:, c, :],
                                       op0=ALU.mult, op1=ALU.add)

        n_g = START["gates"]
        g_base = evac_act.plan(16)
        (s_arot, s_aqc, s_qr, s_sc, s_sm, s_ex, s_tr, s_pt, s_pv, s_on, s_ot, s_oe) = [
            sig("at_" + x) for x in ("rot", "qcos", "qr", "scores", "max", "exp", "trans", "probsT",
                                     "pv", "norm", "oT", "o_out")]

        def tiles_loop(e, one):
            with e.Fori(0, 2) as g:
                with e.Fori(0, 2) as i:
                    for b in range(2):
                        one(g, g * 4 + i * 2 + b, g * 2 + i, b)

        @on("pe")
        def _(e):
            evac_act.wait(e, q_in + 2)
            evac_dve.wait(e, e_dve + 1)
            s_kz.wait(e, 4)

            def gemm(it, b, j, t):
                w = tiles_of(use_slot(e, n_g, it, 4, 2 * b + j))
                evac_act.wait(e, t * 2 + (g_base + j))
                for k in range(KT):
                    mm = e.matmul(PS[:, 7, :], w[:, k, :], H[:, k, :], start=k == 0, stop=k == KT - 1)
                mm.then_inc(slot_done.sem, 1)

            def one(g, t, it, b):
                s_on.wait(e, t * 2)
                e.matmul(PS[:, 6, :], rot, tile(Q, t), start=True, stop=True).then_inc(s_arot.sem, 1)
                gemm(it, b, 0, t)
                s_qr.wait(e, t + 1)
                for h in range(2):
                    (s_oe if h else s_pt).wait(e, t if h else t * 2)
                    for n in range(NB):
                        mm = e.matmul(PS[:, 2 * h + n // 2, (n % 2) * 256:(n % 2) * 256 + 256],
                                      qr[:, b, n * P:(n + 1) * P],
                                      kz[:, bass.ds(g * 2 + h, 1), n * P:(n + 2) * P]
                                      .rearrange("p a s -> p (a s)"), start=True, stop=True)
                    mm.then_inc(s_sc.sem, 1)
                gemm(it, b, 1, t)
                for h in range(2):
                    s_ex.wait(e, t * 2 + (h + 1))
                    for c in range(2 * NB):
                        bank = (0 if h else 4) + c // 4
                        mm = e.transpose(PS[:, bank, (c % 4) * P:(c % 4 + 1) * P],
                                         Sb[:, h, c // 2, (c % 2) * P:(c % 2 + 1) * P], ident)
                    mm.then_inc(s_tr.sem, 1)
                for h in range(2):
                    s_pt.wait(e, t * 2 + (h + 1))
                    for n in range(NB):
                        for c in range(2):
                            mm = e.matmul(PS[:, 3 if h else 6, n * HD:(n + 1) * HD],
                                          pT[:, h, 2 * n + c, :],
                                          V[:, n + c, bass.ds(g * HD, HD)], start=c == 0, stop=c == 1)
                    mm.then_inc(s_pv.sem, 1)
                s_on.wait(e, t * 2 + 2)
                for n in range(NB):
                    mm = e.transpose(PS[:, 2, n * P:(n + 1) * P], osb[:, n, :], ident)
                mm.then_inc(s_ot.sem, 1)
            tiles_loop(e, one)

        @on("pool")
        def _(e):
            s_kz.wait(e, 4)

            def one(g, t, it, b):
                s_qr.wait(e, t)
                e.tensor_tensor(ra[:, :], tile(Q, t), cos[:, :], ALU.mult).then_inc(s_aqc.sem, 1)
            tiles_loop(e, one)

        @on("dve")
        def _(e):
            def one(g, t, it, b):
                e.drain()
                s_arot.wait(e, t + 1)
                e.tensor_tensor(rb[:, :], PS[:, 6, :], sin[:, :], ALU.mult)
                e.drain()
                s_aqc.wait(e, t + 1)
                e.tensor_tensor(qr[:, b, :], ra[:, :], rb[:, :], ALU.add).then_inc(s_qr.sem, 1)
                for h in range(2):
                    s_sc.wait(e, t * 2 + (h + 1))
                    mx, nm, ds = st[:, h, 0, :], st[:, h, 1, :], st[:, h, 2, :]
                    e.scalar_tensor_tensor(
                        out=Sb[:, h, :, :].rearrange("p n k -> p (n k)"),
                        in0=PS[:, 2 * h:2 * h + 2, :].rearrange("p a b -> p (a b)"),
                        scalar=HD ** -0.5, in1=M[:, :, :].rearrange("p n k -> p (n k)"),
                        op0=ALU.mult, op1=ALU.add)
                    e.drain()
                    e.tensor_reduce(mx, Sb[:, h, :, :], AX.X, ALU.max)
                    e.drain()
                    e.tensor_scalar(nm, mx, col(sinks, t * 2 + h), -1.0, ALU.max, ALU.mult)
                    e.drain()
                    e.tensor_scalar(ds, nm, col(sinks, t * 2 + h), None, ALU.add).then_inc(s_sm.sem, 1)
                for h in range(2):
                    tap(e, t * 2 + (h + 1 + EARLY))
                    s_ex.wait(e, t * 2 + (h + 1))
                    e.tensor_tensor(st[:, h, 5, :], st[:, h, 3, :], st[:, h, 4, :], ALU.add)
                    e.drain()
                    e.reciprocal(st[:, h, 5, :], st[:, h, 5, :])
                    e.drain()
                    s_pv.wait(e, t * 2 + (h + 1))
                    if h == 0:
                        s_ot.wait(e, t)
                    e.tensor_tensor(osb[:, :, h * HD:(h + 1) * HD],
                                    PS[:, 3 if h else 6, 0:NB * HD]
                                    .rearrange("p (n c) -> p n c", n=NB),
                                    view(st[:, h, 5, :], [1, NB], [0, HD]), ALU.mult)\
                        .then_inc(s_on.sem, 1)
            tiles_loop(e, one)
            with e.Fori(2 * KT + 1 + EARLY, TAPS) as w:
                tap(e, w)

        @on("act")
        def _(e):
            def gate(t, j):
                slot_done.wait(e, t * 2 + (n_g + j + 1))
                e.activation(tile(G, t * 2 + j), PS[:, 7, :], ACT.Identity, bias=cd("b_gates", t * 2 + j))\
                    .then_inc(evac_act.sem, 1)

            def one(g, t, it, b):
                gate(t, 0)
                for h in range(2):
                    s_sm.wait(e, t * 2 + (h + 1))
                    for n in range(NB):
                        e.activation(Sb[:, h, n, :], Sb[:, h, n, :], ACT.Exp,
                                     bias=st[:, h, 1, n:n + 1], accum_out=st[:, h, 3, n:n + 1])
                    e.activation(st[:, h, 4, :], st[:, h, 2, :], ACT.Exp).then_inc(s_ex.sem, 1)
                gate(t, 1)
                for h in range(2):
                    s_tr.wait(e, t * 2 + (h + 1))
                    s_pv.wait(e, t * 2)
                    bank = 0 if h else 4
                    e.activation(pT[:, h, :, :].rearrange("p c k -> p (c k)"),
                                 PS[:, bank:bank + 2, :].rearrange("p a b -> p (a b)"), ACT.Copy)\
                        .then_inc(s_pt.sem, 1)
                s_ot.wait(e, t + 1)
                e.activation(tile(O, t), PS[:, 2, :], ACT.Copy).then_inc(s_oe.sem, 1)
            tiles_loop(e, one)

        s_ao, s_sg = sig("m1_attn_gated"), sig("m1_sigmoid")
        s_zh, s_zl = sig("m1_rhs_hi"), sig("m1_rhs_lo")
        tail.plan()
        n_ao, n_co = START["attn_o"], START["conv_out"]

        def rhs_hi(e, src):
            for t in range(KT):
                e.activation(z_hi[:, t, :], src[:, t, :], ACT.Copy).then_inc(s_zh.sem, 1)

        def rhs_lo(e, src, low, base):
            for t in range(KT):
                s_zh.wait(e, base + t + 1)
                e.tensor_tensor(low[:, t, :], src[:, t, :], z_hi[:, t, :].bitcast(F32),
                                ALU.subtract).then_inc(s_zl.sem, 1)

        @on("act")
        def _(e):
            e.drain()
            tail.hi(e, 0, 4, n_ao)
            rhs_hi(e, O)
            tail.hi(e, 0, 4, n_ao + 1)
            for t in range(2 * KT):
                e.activation(G[:, t, :], G[:, t, :], ACT.Sigmoid).then_inc(s_sg.sem, 1)
        pe_gemm("attn_o", KT, lambda k: (z_hi[:, k, :], O_lo[:, k, :]), (s_zl, 0), split=tail)
        ao = evac_act.n
        evac_act.plan(KT)

        @on("act")
        def _(e):
            for t in range(KT):
                if t:
                    tail.hi(e, 0, 4, n_ao + t + 1)
                slot_done.wait(e, n_ao + t + 1)
                e.activation(H[:, t, :], PS[:, t % 4, :], ACT.Copy).then_inc(evac_act.sem, 1)

        @on("pool")
        def _(e):
            tail.lo(e, 0, 4, n_ao)
            rhs_lo(e, O, O_lo, 0)
            tail.lo(e, 0, 4, n_ao + 1)
            s_sg.wait(e, 2 * KT)
            for t in range(KT):
                if t:
                    tail.lo(e, 0, 4, n_ao + t + 1)
                evac_act.wait(e, ao + t + 1)
                e.tensor_tensor(H[:, t, :], H[:, t, :], G[:, t + KT, :], ALU.mult)\
                    .then_inc(s_ao.sem, 1)
            rhs_lo(e, Y, Y_lo, KT)
            tail.loop(e, tail.lo, n_co + 1, 2 * KT - 1)

        s_y, s_mu, s_xc, s_lsq, s_lmm, s_lr, s_ln, s_silu = [
            sig("ln_" + x) for x in ("in", "mean", "centred", "square", "var", "root", "scaled", "silu")]

        @on("dve")
        def _(e):
            e.drain().then_inc(s_y.sem, 1)
            s_mu.wait(e, 1)
            for c in range(KT):
                e.tensor_tensor(Y[:, c, :], Y[:, c, :], PS[:, 5, :], ALU.subtract).then_inc(s_xc.sem, 1)
            s_lr.wait(e, 1)
            e.reciprocal(ra[:, :], ra[:, :])
            e.drain()
            for c in range(KT):
                e.scalar_tensor_tensor(out=Y[:, c, :], in0=Y[:, c, :], scalar=c_("ln_g", c),
                                       in1=ra[:, :], op0=ALU.mult, op1=ALU.mult).then_inc(s_ln.sem, 1)

        @on("pe")
        def _(e):
            s_y.wait(e, 1)
            for c in range(KT):
                mm = e.matmul(PS[:, 5, :], mean, Y[:, c, :], start=c == 0, stop=c == KT - 1)
            mm.then_inc(s_mu.sem, 1)
            for c in range(KT):
                s_lsq.wait(e, c + 1)
                e.matmul(PS[:, 6, :], mean, norm_sq[:, c % 2, :], start=c == 0, stop=c == KT - 1)\
                    .then_inc(s_lmm.sem, 1)

        @on("act")
        def _(e):
            for c in range(KT):
                s_xc.wait(e, c + 1)
                if c >= 2:
                    s_lmm.wait(e, c - 1)
                e.activation(norm_sq[:, c % 2, :], Y[:, c, :], ACT.Square).then_inc(s_lsq.sem, 1)
            s_lmm.wait(e, KT)
            e.activation(ra[:, :], PS[:, 6, :], ACT.Sqrt, bias=c_("eps")).then_inc(s_lr.sem, 1)
            for c in range(KT):
                s_ln.wait(e, c + 1)
                e.activation(Y[:, c, :], Y[:, c, :], ACT.Silu, bias=c_("ln_b", c)).then_inc(s_silu.sem, 1)
                s_silu.wait(e, c + 1)
                e.activation(z_hi[:, c, :], Y[:, c, :], ACT.Copy).then_inc(s_zh.sem, 1)
            tail.loop(e, tail.hi, n_co + 1, 2 * KT - 1)

        pe_gemm("conv_out", KT, lambda k: (z_hi[:, k, :], Y_lo[:, k, :]), (s_zl, KT),
                free=evac_dve, split=tail)
        merged = evac_dve.n

        def merge(e, t, bank):
            e.tensor_tensor(tile(G, t), bank, tile(G, t), ALU.mult)
            e.drain()
            s_ao.wait(e, t + 1)
            held(e)
            e.tensor_tensor(tile(Q, t), tile(G, t), tile(H, t), ALU.add)
            e.drain()
            e.tensor_copy(tile(q_hi, t), tile(Q, t))
            e.drain()
            return e.tensor_tensor(tile(Q_lo, t), tile(Q, t), tile(q_hi, t).bitcast(F32),
                                   ALU.subtract)
        evacuate("dve", "conv_out", KT, merge, evac_dve)
        pe_gemm("w_out", KT, lambda k: (q_hi[:, k, :], Q_lo[:, k, :]), (evac_dve, merged),
                free=evac_dve, split=tail)
        added = evac_dve.n
        evac_add("w_out", KT)
        norm_root(ready=(evac_dve, added))
        barrier()
        m.close()

    def peer():
        m = ExitStack()
        low = sb(m, "peer_x_lo", [P, KT, S], F32R)
        A, A_lo = names(m, [P, 2 * JQ, S], "experts", "experts_lo")
        TT = sb(m, "picks_T", [P, 2, S])
        gate_row = norm_r
        split = Split(m, "peer_slots", START["peer_q_u0"], START["f1_in"] - START["peer_q_u0"], 2)
        sc = ExitStack()
        keysT = sb(sc, "sub_keys_T", [P, 2 * PH, NKEY])
        qh = sb(sc, "peer_q", [P, 2, S])
        work = sb(sc, "scores_left", [P, 8, NKEY])
        cand = sb(sc, "sums", [P, NB, TOPK * TOPK])
        cand2 = sb(sc, "sums_left", [P, NB, TOPK * TOPK])
        with ExitStack() as only_norm:
            normed = sb(only_norm, "normed", [P, 4, S])
        eq_a, eq_b = [sb(sc, x_ + "_hot", [P, NB * TOPK, TOPK], BF16) for x_ in ("row", "col")]
        T = sb(sc, "picks", [P, 3, NB, PH * TOPK])
        top = sb(sc, "top", [P, 8, TOPK])
        idx = sb(sc, "top_index", [P, 8, TOPK], U32)
        idxf = sb(sc, "top_index_f", [P, 8, TOPK], BF16)
        best = sb(sc, "best", [P, NB, TOPK])
        pos = sb(sc, "best_pos", [P, NB, TOPK], U32)
        pa, pb = sb(sc, "pos_row", [P, NB, TOPK], U32), sb(sc, "pos_col", [P, NB, TOPK], U32)
        gsum = sb(sc, "gate_sum", [P, NB * PH])

        s_keys = sig("peer_keys").by_dma()
        s_qe, s_psc, s_top, s_u = [sig("peer_" + x) for x in ("q_out", "scores", "top", "u_out")]
        on("act")(lambda e: e.dma_start(keysT[:, :, :], a["keysT"]).then_inc(s_keys.sem, 16))
        nq = START["peer_q_u0"]
        on("act")(lambda e: split.hi(e, 0, 4, nq))
        split.lows(nq, 33)
        b_h = norm_apply("norm2", split=(Hh, low, normed))

        def heads_loop(e, one):
            with e.Fori(0, PH // 2) as i:
                for b in range(2):
                    one(i, i * 2 + b, b)

        on("pe")(lambda e: s_keys.wait(e, 16))

        x = lambda k: (Hh[:, k, :], low[:, k, :])

        @on("pe")
        def _(e):
            def product(bank, w):
                for k in range(KT):
                    if bank == 0:
                        s_h.wait(e, b_h + k + 1)
                    mm = product3(e, PS[:, bank, :], w, k, x(k), k == 0, k == KT - 1)
                mm.then_inc(slot_done.sem, 1)

            def one(i, h, b):
                for c in range(2):
                    w = split.use(e, i, 8, nq + 4 * b + c)
                    s_qe.wait(e, h * 2)
                    product(c, w)
                for c in range(2):
                    s_qe.wait(e, h * 2 + (c + 1))
                    s_top.wait(e, h)
                    for n in range(NB):
                        mm = e.matmul(PS[:, 2 + c, n * P:(n + 1) * P], qh[:, c, n * P:(n + 1) * P],
                                      tile(keysT, h * 2 + c), start=True, stop=True)
                    mm.then_inc(s_psc.sem, 1)
                    w = split.use(e, i, 8, nq + 4 * b + 2 + c)
                    s_u.wait(e, h * 2)
                    product(4 + c, w)
            heads_loop(e, one)

        @on("act")
        def _(e):
            def one(i, h, b):
                for c in range(2):
                    split.hi(e, i, 8, nq + 4 * b + c + 1)
                    slot_done.wait(e, i * 8 + (nq + 4 * b + c + 1))
                    s_psc.wait(e, h * 2)
                    e.activation(qh[:, c, :], PS[:, c, :], ACT.Copy).then_inc(s_qe.sem, 1)
                for r in range(2):
                    split.hi(e, i, 8, nq + 4 * b + 3 + r)
                    slot_done.wait(e, i * 8 + (nq + 4 * b + 3 + r))
                    e.activation(tile(A, h * 2 + r), PS[:, 4 + r, :], ACT.Gelu).then_inc(s_u.sem, 1)
            heads_loop(e, one)
        @on("dve")
        def _(e):
            def top16(values, left, vals, index, n, read=None):
                for c in range(n):
                    e.max(vals[:, c, 0:8], values(c))
                e.drain()
                for c in range(n):
                    e.max_index(index[:, c, 0:8], vals[:, c, 0:8], values(c))
                    ins = e.match_replace(left[:, c, :], vals[:, c, 0:8], values(c), TAKEN)
                if read:
                    ins.then_inc(read, 1)
                e.drain()
                for c in range(n):
                    e.max(vals[:, c, 8:16], left[:, c, :])
                e.drain()
                for c in range(n):
                    e.max_index(index[:, c, 8:16], vals[:, c, 8:16], left[:, c, :])
                e.drain()

            def one(i, h, b):
                e.drain()
                s_psc.wait(e, h * 2 + 2)
                held(e)
                top16(lambda c: PS[:, 2 + c // NB, c % NB * NKEY:(c % NB + 1) * NKEY], work, top, idx,
                      8, s_top.sem)
                e.tensor_copy(idxf[:, :, :], idx[:, :, :])
                e.tensor_tensor(cand[:, :, :].rearrange("p n (r c) -> p n r c", r=TOPK),
                                view(top[:, 0, :], [TOPK, NB], [1, TOPK], [0, TOPK]),
                                view(top[:, NB, :], [TOPK, NB], [0, TOPK], [1, TOPK]), ALU.add)
                e.drain()
                top16(lambda c: cand[:, c, :], cand2, best, pos, NB)
                e.tensor_scalar(pa[:, :, :], pos[:, :, :], 4, None, ALU.logical_shift_right)
                e.tensor_scalar(pb[:, :, :], pos[:, :, :], 15, None, ALU.bitwise_and)
                e.tensor_copy(T[:, 2, :, bass.ds(h * TOPK, TOPK)], best[:, :, :])
                e.drain()
                for p_, eq in ((pa, eq_a), (pb, eq_b)):
                    e.tensor_tensor(eq[:, :, :], view(p_[:, 0, :], [1, NB * TOPK], [0, TOPK]),
                                    view(iota, [0, NB * TOPK], [1, TOPK]), ALU.is_equal)
                e.drain()
                for c, eq in enumerate((eq_a, eq_b)):
                    v = eq[:, :, :].rearrange("p (n k) r -> p n k r", n=NB)
                    e.tensor_tensor(v, v, view(idxf[:, c * NB, :], [TOPK, NB], [0, TOPK], [1, TOPK]),
                                    ALU.mult)
                e.drain()
                for c, eq in enumerate((eq_a, eq_b)):
                    e.tensor_reduce(T[:, c, :, bass.ds(h * TOPK, TOPK)],
                                    eq[:, :, :].rearrange("p (n k) r -> p n k r", n=NB), AX.X, ALU.add)
            heads_loop(e, one)

        s_gx, s_ge, s_tab, s_tt, s_tabT = [sig("gate_" + x) for x in
                                           ("shifted", "exp", "table", "turned", "table_T")]
        g2 = T[:, 2, :, :].rearrange("p n (h k) -> p (n h) k", k=TOPK)

        @on("dve")
        def _(e):
            e.drain()
            e.tensor_copy(gsum[:, :], view(T[:, 2, 0, 0:1], [TOPK, NB * PH]))
            e.drain()
            e.tensor_tensor(g2, g2, view(gsum[:, :], [1, NB * PH], [0, TOPK]), ALU.subtract)\
                .then_inc(s_gx.sem, 1)
            s_ge.wait(e, 1)
            e.tensor_reduce(gsum[:, :], g2, AX.X, ALU.add)
            e.drain()
            e.reciprocal(gsum[:, :], gsum[:, :])
            e.drain()
            e.tensor_tensor(g2, g2, view(gsum[:, :], [1, NB * PH], [0, TOPK]), ALU.mult)\
                .then_inc(s_tab.sem, 1)
            for v in range(3):
                s_tt.wait(e, v + 1)
                e.tensor_copy(TT[:, v, :] if v < 2 else gate_row[:, :], PS[:, v, :]).then_inc(s_tabT.sem, 1)
            e.tensor_copy(iota_b[:, :], iota)
            for v in range(3):
                e.drain()
                e.tensor_copy(gp[:, v, :], gate_row[:, :])
                e.drain()
                if v < 2:
                    e.tensor_tensor(gate_row[:, :], gate_row[:, :], gp[:, v, :], ALU.subtract)

        @on("act")
        def _(e):
            s_gx.wait(e, 1)
            v = T[:, 2, :, :]
            e.activation(v, v, ACT.Exp).then_inc(s_ge.sem, 1)

        @on("pe")
        def _(e):
            s_tab.wait(e, 1)
            s_qe.wait(e, 2 * PH)
            for v in range(3):
                for n in range(NB):
                    mm = e.transpose(PS[:, v, n * P:(n + 1) * P], T[:, v, n, :], ident)
                mm.then_inc(s_tt.sem, 1)
        on("act")(lambda e: s_tt.wait(e, 3))
        sc.close()
        gp = sb(m, "gate_parts", [P, 3, S], BF16)
        iota_b = sb(m, "iota_bf16", [P, P], BF16)
        hot_i = sb(m, "key1_one_hot", [P, 2, 16, P], BF16)
        hot_e = sb(m, "key2_one_hot", [P, 16, JQ], BF16)
        hot_j = sb(m, "gate_at_key2", [P, 2, 16, 3, JQ], BF16)
        two_w = sb(m, "gate_sum_of_parts", [P, 16, JQ])
        G_hi = sb(m, "gated_hi", [P, JQ, S], F32R)

        s_hot, s_wm, s_g, s_ve, s_gh, s_gl = [sig("w_" + x_) for x_ in (
            "one_hot", "product", "gated", "v_out", "gated_hi", "gated_lo")]
        GROUPS = S // 16
        on("pe")(lambda e: e.sem_inc(s_wm.sem, 2))
        on("dve")(lambda e: e.sem_inc(s_g.sem, 2))

        class Group:

            def __init__(self, q0, o):
                self.q0, self.o = q0, o
                self.A = A[:, q0 % 2 * JQ:(q0 % 2 + 1) * JQ, :]
                self.A_lo = A_lo[:, q0 % 2 * JQ:(q0 % 2 + 1) * JQ, :]

            def at(self, per, x_):
                return self.o * (2 * per) + x_ + per * self.q0

        def slot_parts(e, n0, o, i, r):
            s_lo.wait(e, o * 64 + i * 4 + (n0 + r + split.base + 1))
            return [split.parts[:, (n0 + r) % 2, v, :] for v in range(2)]

        def u_slot(e, u, n0, i, r):
            w = [tiles_of(p_) for p_ in slot_parts(e, n0, u.o, i, r)]
            s_u.wait(e, u.at(JQ, i * 4 + (r - 1)))
            for k in range(KT):
                mm = product3(e, PS[:, 4 + r % 2, :], w, k, x(k), k == 0, k == KT - 1)
            mm.then_inc(slot_done.sem, 1)

        def v_slot(e, v, n0, s_):
            dh, t = s_ // 8, s_ % 8
            w = slot_parts(e, n0, v.o, 0, s_)
            if dh == 0:
                s_gl.wait(e, v.at(JQ, 2 * t + 2))
            for j in range(2):
                g_ = (G_hi[:, 2 * t + j, :], v.A_lo[:, 2 * t + j, :])
                for d in range(4):
                    if t == 0 and j == 0:
                        s_ve.wait(e, v.at(8, d + 1 if dh else 0))
                    at = j * (D // 2) + d * P
                    for y, (a_, b_) in enumerate(THREE):
                        mm = e.matmul(PS[:, d, :], w[a_][:, at:at + P], g_[b_],
                                      start=t == 0 and j == 0 and y == 0,
                                      stop=t == 7 and j == 1 and y == 2)
            mm.then_inc(slot_done.sem, 1)

        def w_group(e, w, g, parity):
            s_g.wait(e, w.at(GROUPS, g + 1))
            s_hot.wait(e, w.at(GROUPS, g + 1))
            for u in range(16):
                c = 2 * u * JQ
                e.matmul(PS[:, 6 + parity, c:c + 2 * JQ], hot_i[:, parity, u, :],
                         hot_j[:, parity, u, 0:2, :].rearrange("p v j -> p (v j)"),
                         start=True, stop=False)
                mm = e.matmul(PS[:, 6 + parity, c + JQ:c + 2 * JQ], hot_i[:, parity, u, :],
                              hot_j[:, parity, u, 2, :], start=False, stop=True)
            mm.then_inc(s_wm.sem, 1)

        def one_hots(e, w, g, parity):
            s0 = g * 16
            first_key = w.o * (2 * JQ) + w.q0 * JQ
            e.drain()
            e.tensor_tensor(hot_e[:, :, :],
                            TT[:, 1, bass.ds(s0, 16)].unsqueeze(2).broadcast_to([P, 16, JQ]),
                            iota_b[:, bass.ds(first_key, JQ)].unsqueeze(1).broadcast_to([P, 16, JQ]),
                            ALU.is_equal)
            e.drain()
            s_wm.wait(e, w.at(GROUPS, g + 1))
            held(e)
            e.tensor_tensor(hot_i[:, parity, :, :],
                            TT[:, 0, bass.ds(s0, 16)].unsqueeze(2).broadcast_to([P, 16, P]),
                            view(iota_b[:, :], [0, 16], [1, P]), ALU.is_equal)
            e.tensor_tensor(hot_j[:, parity, :, :, :].rearrange("p s v j -> p v s j"),
                            view(hot_e[:, 0, :], [0, 3], [1, 16 * JQ])
                            .rearrange("p v (s j) -> p v s j", j=JQ),
                            gp[:, :, bass.ds(s0, 16)].unsqueeze(3).broadcast_to([P, 3, 16, JQ]),
                            ALU.mult).then_inc(s_hot.sem, 1)

        def gate(e, w, g, parity):
            e.drain()
            s_wm.wait(e, w.at(GROUPS, g + 3))
            e.tensor_reduce(two_w[:, :, :],
                            PS[:, 6 + parity, :].rearrange("p (s v j) -> p s j v", v=2, j=JQ),
                            AX.X, ALU.add)
            e.drain()
            At = w.A[:, :, bass.ds(g * 16, 16)]
            e.tensor_tensor(At, two_w[:, :, :].rearrange("p s j -> p j s"), At, ALU.mult).then_inc(s_g.sem, 1)

        def g_hi(e, v, j):
            s_g.wait(e, v.at(GROUPS, GROUPS + 2))
            e.activation(G_hi[:, j, :], v.A[:, j, :], ACT.Copy).then_inc(s_gh.sem, 1)

        def g_lo(e, v, j):
            s_gh.wait(e, v.at(JQ, j + 1))
            held(e)
            e.tensor_tensor(v.A_lo[:, j, :], v.A[:, j, :], G_hi[:, j, :].bitcast(F32),
                            ALU.subtract).then_inc(s_gl.sem, 1)

        class Window:

            def __init__(self, kind, q0, w0=None, g0=0, per_slot=1, early=False, ahead=None,
                         next_w=None):
                self.next_w = next_w
                self.kind, self.q0, self.w0, self.g0 = kind, q0, w0, g0
                self.per, self.early, self.ahead = per_slot, early, ahead
                self.n0 = START[f"{kind}{q0}"]

            def groups(self, s_):
                if self.w0 is None or (self.early and s_ == 15):
                    return []
                n = 2 * self.per if self.early and s_ == 14 else self.per
                return [(self.per * s_ + t, (self.per * s_ + t) % 2) for t in range(n)]

            def beside(self, e, o, f, i, r, regular):
                if self.w0 is None:
                    return
                w = Group(self.w0, o)
                if regular:
                    for g, parity in self.groups(r):
                        f(e, w, i * (4 * self.per) + (self.g0 + g), parity)
                else:
                    for g, parity in self.groups(4 * i + r):
                        f(e, w, self.g0 + g, parity)

            def steps(self, e, body):
                with e.Fori(0, 3) as i:
                    for r in range(4):
                        body(i, r, True)
                for r in range(4):
                    body(3, r, False)

            def pe(self, e, o):
                q = Group(self.q0, o)
                if self.kind == "u":
                    def body(i, r, regular):
                        u_slot(e, q, self.n0, i, r)
                        self.beside(e, o, w_group, i, r, regular)
                    self.steps(e, body)
                else:
                    for s_ in range(16):
                        v_slot(e, q, self.n0, s_)
                        self.beside(e, o, w_group, s_ // 4, s_ % 4, False)

            def next_hi(self, e, o, i, r):
                n = self.n0 + r + 1
                if isinstance(i, int) and n + 4 * i == START["f1_in"]:
                    return
                e.wait_ge(arrive[n % RING], o * 256 + i * 16 + 16 * (n // RING + 1))
                slot_done.wait(e, o * 64 + i * 4 + (n - 1))
                e.activation(split.parts[:, n % 2, 0, :], ring[:, n % RING, :], ACT.Copy)                    .then_inc(s_hi.sem, 1)

            def next_lo(self, e, o, i, r):
                n = self.n0 + r + 1
                if isinstance(i, int) and n + 4 * i == START["f1_in"]:
                    return
                s_hi.wait(e, o * 64 + i * 4 + (n + split.base + 1))
                held(e)
                e.tensor_tensor(split.parts[:, n % 2, 1, :], ring[:, n % RING, :],
                                split.parts[:, n % 2, 0, :].bitcast(F32), ALU.subtract)                    .then_inc(s_lo.sem, 1)

            def parts(self, e, o, i, r, regular, weights, gated):
                weights(e, o, i, r)
                s_ = None if regular else 4 * i + r
                if self.kind == "v" and s_ < 7:
                    for j in range(2):
                        gated(e, Group(self.q0, o), 2 * s_ + 2 + j)
                if s_ == 15 and self.ahead is not None:
                    for j in range(2):
                        gated(e, Group(self.ahead, o), j)

            def act(self, e, o):
                q = Group(self.q0, o)
                if self.kind == "u":
                    def body(i, r, regular):
                        self.parts(e, o, i, r, regular, self.next_hi, g_hi)
                        slot_done.wait(e, o * 64 + i * 4 + (self.n0 + r + 1))
                        e.activation(tile(q.A, i * 4 + r), PS[:, 4 + r % 2, :], ACT.Gelu)                            .then_inc(s_u.sem, 1)
                    self.steps(e, body)
                else:
                    for s_ in range(16):
                        self.parts(e, o, s_ // 4, s_ % 4, False, self.next_hi, g_hi)

            def pool(self, e, o):
                if self.kind == "u":
                    self.steps(e, lambda i, r, regular:
                               self.parts(e, o, i, r, regular, self.next_lo, g_lo))
                else:
                    for s_ in range(16):
                        self.parts(e, o, s_ // 4, s_ % 4, False, self.next_lo, g_lo)

            def dve(self, e, o):
                if self.w0 is not None:
                    s_u.wait(e, Group(self.w0, o).at(JQ, JQ))
                    held(e)

                def hots(i, r, regular, g, parity):
                    w = Group(self.w0, o)
                    if regular:
                        one_hots(e, w, i * (4 * self.per) + (self.g0 + g + 1), 1 - parity)
                    elif g + 1 < 16 * self.per:
                        one_hots(e, w, self.g0 + g + 1, 1 - parity)
                    elif self.next_w is not None:
                        one_hots(e, Group(self.next_w, o), (self.g0 + g + 1) % GROUPS, 1 - parity)

                def gates(i, r, regular, g, parity):
                    gate(e, Group(self.w0, o), (i * (4 * self.per) if regular else 0) + (self.g0 + g),
                         parity)

                def groups(i, r, regular):
                    return self.groups(r if regular else 4 * i + r)

                if self.kind == "u":
                    def body(i, r, regular):
                        for g, parity in groups(i, r, regular):
                            hots(i, r, regular, g, parity)
                            gates(i, r, regular, g, parity)
                    self.steps(e, body)
                    return
                for s_ in range(16):
                    first = True
                    for g, parity in self.groups(s_) or [(None, None)]:
                        if g is not None:
                            hots(0, s_, False, g, parity)
                        if first and s_ in (7, 15):
                            dh = s_ // 8
                            slot_done.wait(e, o * 64 + (self.n0 + 8 * dh + 8))
                            for d in range(4):
                                e.tensor_tensor(X[:, dh * 4 + d, :], PS[:, d, :],
                                                X[:, dh * 4 + d, :], ALU.add).then_inc(s_ve.sem, 1)
                        first = False
                        if g is not None:
                            gates(0, s_, False, g, parity)
                e.drain()

        on("pe")(lambda e: s_tabT.wait(e, 3))
        HALF = GROUPS // 2
        before = [Window("u", 1, 0, 0, 2, early=True, ahead=0, next_w=1)]
        middle = []
        for q0 in range(2):
            middle += [Window("v", q0, q0 + 1, next_w=q0 + 1),
                       Window("u", q0 + 2, q0 + 1, HALF, early=True, ahead=q0 + 1, next_w=q0 + 2)]
        after = [Window("v", 6, 7, 0, 2, early=True, ahead=7), Window("v", 7)]
        for name in ("pe", "act", "dve", "pool"):
            def windows(e, name=name):
                if name == "dve":
                    one_hots(e, Group(0, 0), 0, 0)

                def run(w, o):
                    {"pe": w.pe, "act": w.act, "dve": w.dve, "pool": w.pool}[name](e, o)
                for w in before:
                    run(w, 0)
                with e.Fori(0, 3) as o:
                    for w in middle:
                        run(w, o)
                for w in after:
                    run(w, 0)
            on(name)(windows)
        s_ve.n = NQ * 8
        norm_root(ready=(s_ve, s_ve.n - KT))
        final = norm_apply("final1", dst=X)
        norm_root(ready=(s_h, final))
        barrier()
        m.close()

    def ffn(n):
        m = ExitStack()
        F = [sb(m, f"ffn{n}_hidden_{v}", [P, FT, S], F32R) for v in ("hi", "lo")]
        low = sb(m, f"ffn{n}_x_lo", [P, KT, S], F32R)
        tmp = sb(m, f"ffn{n}_tmp", [P, 4, S])
        n0, nd = START[f"f{n}_in"], START[f"f{n}_out"]
        s_down = sig("ffn_down")
        b_down = s_down.plan(KT - 1)
        split = Split(m, f"ffn{n}_slots", n0, 3 * FT)
        split.lows(n0, 3 * FT)
        on("act")(lambda e: [split.hi(e, 0, 4, n0 + r) for r in range(2)])
        b_h = norm_apply(f"ffn{n}_n", split=(Hh, low, tmp))
        first = glu_done.n

        def hidden(e, p, bank, t):
            e.tensor_tensor(t, bank, t, ALU.mult)
            e.drain()
            e.tensor_copy(tile(F[0], p), t)
            e.drain()
            return e.tensor_tensor(tile(F[1], p), t, tile(F[0], p).bitcast(F32), ALU.subtract)
        glu(f"f{n}_in", FT, tmp, lambda e, p, t, bank, f: e.activation(t, bank, f), ACT.Silu,
            hidden, (s_h, b_h), split, (Hh, low))

        @on("pe")
        def _(e):
            def slot(i, r, first_, last):
                glu_done.wait(e, i * 4 + (first + r + 1))
                w = split.use(e, i, 4, nd + r)
                x = [tile(F[v], i * 4 + r) for v in range(2)]
                for d in range(KT):
                    if first_ and d < 4:
                        glu_done.wait(e, first + FT)
                    mm = product3(e, PS[:, d, :], w, d, x, first_, last)
                    if last and d < KT - 1:
                        mm.then_inc(s_down.sem, 1)
                mm.then_inc(slot_done.sem, 1)
            for r in range(4):
                slot(0, r, r == 0, False)
            with e.Fori(1, FT // 4) as i:
                for r in range(4):
                    slot(i, r, False, False)
            for r in range(FT % 4):
                slot(FT // 4, r, False, r == FT % 4 - 1)
        on("act")(lambda e: split.loop(e, split.hi, nd + 2, FT - 2))
        done = evac_dve.plan(KT)

        @on("dve")
        def _(e):
            for d in range(KT):
                if d < KT - 1:
                    s_down.wait(e, b_down + d + 1)
                else:
                    slot_done.wait(e, nd + FT)
                e.scalar_tensor_tensor(out=X[:, d, :], in0=PS[:, d, :], scalar=0.5, in1=X[:, d, :],
                                       op0=ALU.mult, op1=ALU.add).then_inc(evac_dve.sem, 1)
        norm_root(bank=0, ready=(evac_dve, done))
        barrier()
        m.close()
        return done

    def mixer2():
        m = ExitStack()
        qk = sb(m, "gla_qk", [P, 2 * GH, S])
        with ExitStack() as last:
            tail = Split(last, "m2_last_slots", START["dsa_out"], 2 * KT, 2, later=True)
        v = sb(m, "gla_v", [P, NB, GH * GDV])
        with ExitStack() as first:
            sb(first, "m2_below", [P, 16, S])
            xh, xl = [sb(first, "m2_x_" + v_, [P, KT, S], F32R) for v_ in ("hi", "lo")]
        with ExitStack() as last:
            merged_lo = sb(last, "merged_lo", [P, KT, S], F32R)
            sb(last, "m2_between", [P, KT, S])
            att_hi = sb(last, "attended_hi", [P, KT, S], F32R)
            merged_hi = sb(last, "merged_hi", [P, KT, S], F32R)
        wide = sb(m, "wide2", [P, 32, S])
        ckvT, ckv = sb(m, "ckv_T", [P, S]), sb(m, "ckv", [P, NB, P])
        sel = sb(m, "selection", [P, NB, S], mybir.dt.bfloat16)
        gl = ExitStack()
        la = sb(gl, "log_decay", [P, GH, S])
        lmask = sb(gl, "level_mask", [P, 8, P])
        iqT, ikT = wide[:, 0:4, :], wide[:, 4, :]
        gaT, alw = wide[0:16, 5, :], wide[0:16, 6, :]
        score = wide[:, 8:12, :]
        rel = wide[:, 12:14, :]
        iw = sb(gl, "index_w", [P, NB, 8])
        i8 = sb(gl, "index_top", [P, 3, 8])
        tri = sb(gl, "causal", [P, P])
        with ExitStack() as first:
            split = Split(first, "m2_slots", START["gqk"], 16, 2)
            ex = sb(first, "log_scratch", [P, GH, S])[:, :, :]
        split.lows(START["gqk"], 16)

        flat = qk[:, :, :].rearrange("p a s -> p (a s)")
        rows_, hot, rb_ = flat[0:DH, 0:640], flat[0:32, 1024:1664], flat[0:32, 2048:2048 + DH]
        scratch = nc.dram_tensor("bias_rows_dram", (DH, 640), F32, kind="Internal").ap()
        s_rmm, s_row = sig("bias_product"), sig("bias_rows")
        s_rin, s_rdr = [sig("bias_" + x).by_dma() for x in ("in", "dram")]

        s_in, s_hd = sig("m2_in").by_dma(), sig("m2_evac")
        b_in = s_in.plan(64)

        @on("act")
        def _(e):
            e.dma_start(hot, a["buckets"]).then_inc(s_rin.sem, 16)
            e.dma_start(rb_, a["rel_bias"]).then_inc(s_rin.sem, 16)
            e.dma_start(alw, a["alpha_w"]).then_inc(s_in.sem, 16)
            e.dma_start(lmask[:, :, :], a["level_mask"]).then_inc(s_in.sem, 16)
            e.dma_start(tri[:, :], a["causal"]).then_inc(s_in.sem, 16)
        b_h = norm_apply("mix_n", split=(xh, xl, H), parts_last=True)
        normed = s_np.n - KT
        nh = START["misc"]
        s_root2, s_csq, s_cmm, s_cn, s_ct, s_ce = [sig("ckv_" + x) for x in
                                                   ("root", "square", "mean", "normed", "turned", "tokens")]
        s_alo = sig("ix_alpha_out")
        s_al, s_ax, s_dot, s_rel, s_acc = [sig("ix_" + x) for x in
                                           ("alpha", "log", "dots", "relu", "sum")]
        on("dve")(lambda e: e.sem_inc(s_acc.sem, 2))
        s_acc.n = 2
        combos = [(n, h) for n in range(1, NB) for h in range(8)]
        n_qk = START["gqk"]
        qk_base = evac_act.n
        old = [(s, s.n) for s in (evac_act, evac_dve, glu_done)]
        evac_act.plan(2 * GH)

        @on("pe")
        def _(e):
            for s, x in old:
                s.wait(e, x)
            w = tiles_of(use_slot(e, nh, 0, 4, 0))
            for k in range(KT):
                s_np.wait(e, normed + k + 1)
                e.matmul(PS[0:16, 0, :], w[:, k, 0:16], H[:, k, :], start=k == 0, stop=k == KT - 1)
            for n in range(NB):
                for k in range(KT):
                    mm = e.matmul(PS[:, 1, n * 8:(n + 1) * 8], H[:, k, n * P:(n + 1) * P],
                                  w[:, k, 16:24], start=k == 0, stop=k == KT - 1)
            mm.then_inc(slot_done.sem, 1)
            for j in range(6):
                w = tiles_of(use_slot(e, nh, 0, 4, j + 1))
                for k in range(KT):
                    mm = e.matmul(PS[:, 2 + j, :], w[:, k, :], H[:, k, :], start=k == 0, stop=k == KT - 1)
                mm.then_inc(slot_done.sem, 1)
            s_in.wait(e, 48)
            s_hd.wait(e, 2)
            for h in range(GH):
                if h >= 2:
                    s_hd.wait(e, h + 1)
                e.matmul(PS[:, h, :], alw[:, h * P:(h + 1) * P], gaT, start=True, stop=True)\
                    .then_inc(s_al.sem, 1)
            s_csq.wait(e, 1)
            e.matmul(PS[:, 7, :], mean, norm_sq[:, 0, :], start=True, stop=True).then_inc(s_cmm.sem, 1)
            s_rin.wait(e, 32)
            s_hd.wait(e, 8)
            for j in range(2):
                mm = e.matmul(PS[0:DH, 4 + j, 0:320], rb_, hot[:, j * 320:(j + 1) * 320],
                              start=True, stop=True)
            mm.then_inc(s_rmm.sem, 1)
            s_row.wait(e, 2)
            s_alo.wait(e, 1)
            s_h.wait(e, b_h + KT)
            for x, (n, h) in enumerate(combos):
                if x % 3 == 0:
                    t = x // 3
                    w = split.use(e, 0, 4, n_qk + t)
                    if t >= 4:
                        evac_act.wait(e, qk_base + t - 3)
                    for k in range(KT):
                        mm = product3(e, PS[:, t % 4, :], w, k, (xh[:, k, :], xl[:, k, :]), k == 0,
                                      k == KT - 1)
                    mm.then_inc(slot_done.sem, 1)
                rows = slice(64 * (h % 2), 64 * (h % 2) + 64)
                s_rel.wait(e, max(x - 1, 0))
                e.matmul(PS[:, 4 + x % 2, 0:(n + 1) * P], iqT[rows, h // 2, n * P:(n + 1) * P],
                         ikT[rows, 0:(n + 1) * P], start=True, stop=True).then_inc(s_dot.sem, 1)
            s_cn.wait(e, 1)
            for n in range(NB):
                mm = e.transpose(PS[:, 6, n * P:(n + 1) * P], ckvT[:, n * P:(n + 1) * P], ident)
            mm.then_inc(s_ct.sem, 1)

        @on("act")
        def _(e):
            slot_done.wait(e, nh + 1)
            e.activation(gaT, PS[0:16, 0, :], ACT.Copy).then_inc(s_hd.sem, 1)
            e.activation(iw[:, :, :].rearrange("p n h -> p (n h)"), PS[:, 1, 0:32], ACT.Copy,
                         scale=8 ** -0.5).then_inc(s_hd.sem, 1)
            for j, dst in enumerate([ikT] + [iqT[:, t, :] for t in range(4)] + [ckvT[:, :]]):
                slot_done.wait(e, nh + j + 2)
                e.activation(dst, PS[:, 2 + j, :], ACT.Copy).then_inc(s_hd.sem, 1)
            s_hd.wait(e, 8)
            e.activation(norm_sq[:, 0, :], ckvT[:, :], ACT.Square).then_inc(s_csq.sem, 1)
            s_cmm.wait(e, 1)
            e.activation(norm_r[:, :], PS[:, 7, :], ACT.Sqrt, scale=float(KT), bias=c_("eps"))\
                .then_inc(s_root2.sem, 1)
            for h in range(GH):
                s_al.wait(e, h + 1)
                ins = e.activation(la[:, h, :], PS[:, h, :], ACT.Identity, bias=c_("alpha_b", h))
            ins.then_inc(s_alo.sem, 1)
            split.hi(e, 0, 4, START["gqk"])
            s_rmm.wait(e, 1)
            for j in range(2):
                e.activation(rows_[:, j * 320:(j + 1) * 320], PS[0:DH, 4 + j, 0:320], ACT.Copy)\
                    .then_inc(s_row.sem, 1)
            s_row.wait(e, 2)
            e.dma_start(scratch, rows_).then_inc(s_rdr.sem, 16)
            s_rdr.wait(e, 16)
            for x, (n, h) in enumerate(combos):
                if x % 3 == 0:
                    t = x // 3
                    split.hi(e, 0, 4, n_qk + t + 1)
                    slot_done.wait(e, n_qk + t + 1)
                    e.activation(qk[:, t, :], PS[:, t % 4, :], ACT.Copy,
                                 scale=1.0 if t % 2 else P ** -0.5).then_inc(evac_act.sem, 1)
                s_dot.wait(e, x + 1)
                s_acc.wait(e, x + 1)
                e.activation(rel[:, x % 2, 0:(n + 1) * P], PS[:, 4 + x % 2, 0:(n + 1) * P], ACT.Relu,
                             scale=0.125).then_inc(s_rel.sem, 1)
            s_ct.wait(e, 1)
            e.activation(ckv[:, :, :].rearrange("p n c -> p (n c)"), PS[:, 6, :], ACT.Copy)\
                .then_inc(s_ce.sem, 1)
            e.drain()
            e.activation(ex, la[:, :, :], ACT.Abs)
            e.drain()
            e.activation(ex, ex, ACT.Exp, scale=-1.0)
            e.drain()
            e.activation(ex, ex, ACT.Ln, bias=c_("one")).then_inc(s_ax.sem, 1)

        s_la = sig("m2_decay")

        @on("dve")
        def _(e):
            s_root2.wait(e, 1)
            e.reciprocal(norm_r[:, :], norm_r[:, :])
            e.drain()
            e.scalar_tensor_tensor(out=ckvT[:, :], in0=ckvT[:, :], scalar=c_("ckv_n"),
                                   in1=norm_r[:, :], op0=ALU.mult, op1=ALU.mult).then_inc(s_cn.sem, 1)
            s_hd.wait(e, 8)
            for x, (n, h) in enumerate(combos):
                e.drain()
                s_rel.wait(e, x + 1)
                sc_, r_ = score[:, n, 0:(n + 1) * P], rel[:, x % 2, 0:(n + 1) * P]
                if h == 0:
                    e.tensor_scalar(sc_, r_, iw[:, n, 0:1], None, ALU.mult).then_inc(s_acc.sem, 1)
                else:
                    e.scalar_tensor_tensor(out=sc_, in0=r_, scalar=iw[:, n, h:h + 1], in1=sc_,
                                           op0=ALU.mult, op1=ALU.add).then_inc(s_acc.sem, 1)
            e.drain()
            s_in.wait(e, 48)
            for n in range(1, NB):
                d = score[:, n, n * P:(n + 1) * P]
                e.tensor_tensor(d, d, tri[:, :], ALU.add)
            with e.Fori(0, SEL // 8):
                e.drain()
                for n in range(1, NB):
                    e.max(i8[:, n - 1, :], score[:, n, 0:(n + 1) * P])
                e.drain()
                for n in range(1, NB):
                    w = score[:, n, 0:(n + 1) * P]
                    e.match_replace(w, i8[:, n - 1, :], w, TAKEN)
            e.drain()
            e.tensor_copy(sel[:, 0, 0:P], tri[:, :])
            for n in range(1, NB):
                e.tensor_scalar(sel[:, n, 0:(n + 1) * P], score[:, n, 0:(n + 1) * P], TAKEN / 2, NEG,
                                ALU.is_gt, ALU.mult)
            e.drain()
            s_ax.wait(e, 1)
            la2, ex2 = (x.rearrange("p h s -> p (h s)") for x in (la[:, :, :], ex))
            e.scalar_tensor_tensor(out=la2, in0=la2, scalar=0.0, in1=ex2, op0=ALU.min,
                                   op1=ALU.subtract)
            e.drain()
            e.tensor_scalar(la2, la2, 1.0 / 16, None, ALU.mult).then_inc(s_la.sem, 1)

        nv = START["gv"]
        v_base = evac_act.plan(8)
        s_ce_n = 1

        @on("pe")
        def _(e):
            evac_act.wait(e, v_base)
            s_ce.wait(e, s_ce_n)
            for c in range(2):
                for kp in range(4):
                    n_ = nv + 4 * c + kp
                    split.use(e, 0, 4, n_)
                    w = [split.parts[:, n_ % 2, y, :].rearrange("p (k c) -> p k c", k=2)
                         for y in range(2)]
                    for k in range(2):
                        for n in range(NB):
                            for y, (a_, b_) in enumerate(THREE):
                                mm = e.matmul(PS[:, 4 * c + n, :],
                                              (xh, xl)[b_][:, 2 * kp + k, n * P:(n + 1) * P],
                                              w[a_][:, k, :], start=kp == 0 and k == 0 and y == 0,
                                              stop=kp == 3 and k == 1 and y == 2)
                    mm.then_inc(slot_done.sem, 1)

        @on("act")
        def _(e):
            for c in range(2):
                for kp in range(4):
                    if 4 * c + kp < 7:
                        split.hi(e, 0, 4, nv + 4 * c + kp + 1)
                slot_done.wait(e, nv + 4 * c + 4)
                for n in range(NB):
                    e.activation(v[:, n, c * 512:(c + 1) * 512], PS[:, 4 * c + n, :], ACT.Copy)\
                        .then_inc(evac_act.sem, 1)

        b = sb(gl, "log_decay_sum", [P, S])
        dd = sb(gl, "decay_diff", [P, 2, S])
        E = sb(gl, "decay", [P, 2, S])
        ql, kl = sb(gl, "q_level", [P, 2, S]), sb(gl, "k_level", [P, 2, S])
        acc = sb(gl, "gla_scores_T", [P, S])
        qe = sb(gl, "q_decayed", [P, S])
        kdT = sb(gl, "k_decayed", [P, NB, P])
        St = sb(gl, "state", [P, 3, GDV])
        ot = sb(gl, "gla_o", [P, NB, GDV])
        gs = sb(gl, "gla_stats", [P, 3, NB])
        names = ("b", "diff", "exp", "q", "k", "scores", "picked", "el", "kd", "kdT", "kd_out", "kv",
                 "state", "o", "square", "root", "o_norm", "oT", "o_out")
        (s_b, s_d, s_e, s_q, s_k, s_s, s_p, s_el, s_kd, s_kt, s_ko, s_kv, s_st, s_o, s_os, s_or,
         s_on, s_ot, s_oo) = [sig("gla_" + x) for x in names]
        nw = START["wide2"]
        w_base = evac_act.plan(32)
        LV = 7

        @on("pe")
        def _(e):
            evac_act.wait(e, v_base + 8)

            def gemm(h, r):
                w = tiles_of(use_slot(e, nw, h, 8, r))
                evac_act.wait(e, h * 8 + (w_base + r - 1))
                for k in range(KT):
                    mm = e.matmul(PS[:, 6 + r % 2, :], w[:, k, :], H[:, k, :], start=k == 0,
                                  stop=k == KT - 1)
                mm.then_inc(slot_done.sem, 1)

            with e.Fori(0, GH) as h:
                for l in range(LV + 1):
                    if l < LV:
                        gemm(h, l)
                    s_q.wait(e, h * (LV + 1) + (l + 1))
                    s_k.wait(e, h * (LV + 1) + (l + 1))
                    if l >= 2:
                        s_p.wait(e, h * (LV + 1) + (l - 1))
                    else:
                        s_p.wait(e, h * (LV + 1))
                    for n in range(NB):
                        t = slice(n * P, (n + 1) * P)
                        mm = e.matmul(PS[:, l % 2, t], kl[:, l % 2, t], ql[:, l % 2, t],
                                      start=True, stop=True)
                    mm.then_inc(s_s.sem, 1)
                s_kd.wait(e, h + 1)
                for n in range(NB):
                    mm = e.transpose(PS[:, 4, n * P:(n + 1) * P], dd[:, 1, n * P:(n + 1) * P], ident)
                mm.then_inc(s_kt.sem, 1)
                gemm(h, 7)
                s_ko.wait(e, h + 1)
                for n in range(NB - 1):
                    mm = e.matmul(PS[:, 2 + n // 2, (n % 2) * GDV:(n % 2 + 1) * GDV], kdT[:, n, :],
                                  v[:, n, bass.ds(h * GDV, GDV)], start=True, stop=True)
                mm.then_inc(s_kv.sem, 1)
                s_st.wait(e, h + 1)
                for n in range(NB):
                    o_ = PS[:, 4 + n // 2, (n % 2) * GDV:(n % 2 + 1) * GDV]
                    mm = e.matmul(o_, acc[:, n * P:(n + 1) * P], v[:, n, bass.ds(h * GDV, GDV)],
                                  start=True, stop=n == 0)
                    if n:
                        mm = e.matmul(o_, qe[:, n * P:(n + 1) * P], St[:, n - 1, :], start=False,
                                      stop=True)
                mm.then_inc(s_o.sem, 1)
                s_on.wait(e, h + 1)
                for j in range(2):
                    for n in range(NB):
                        mm = e.transpose(PS[:, 2 + j, n * P:(n + 1) * P],
                                         ot[:, n, j * P:(j + 1) * P], ident)
                mm.then_inc(s_ot.sem, 1)

        @on("dve")
        def _(e):
            s_la.wait(e, 1)
            slot_done.wait(e, nv + 8)
            with e.Fori(0, GH) as h:
                e.drain()
                for n in range(NB):
                    t = slice(n * P, (n + 1) * P)
                    e.tensor_tensor_scan(dd[:, 0, t], view(c_("one"), [0, P]), la[:, bass.ds(h, 1), t]
                                         .rearrange("p a s -> p (a s)"), 0.0, ALU.mult, ALU.add)
                e.drain()
                e.tensor_copy(b[:, :], dd[:, 0, :]).then_inc(s_b.sem, 1)
                e.memset(acc[:, :], 0.0)
                e.drain()

                def diff(l):
                    half = 64 >> l
                    nb = S // (2 * half)
                    e.tensor_tensor(view(dd[:, l % 2, :], [2 * half, nb], [1, 2 * half]),
                                    view(b[:, :], [2 * half, nb], [1, 2 * half]),
                                    view(b[:, half - 1:half], [2 * half, nb], [0, 2 * half]),
                                    ALU.subtract).then_inc(s_d.sem, 1)

                def pick(l):
                    e.drain()
                    s_s.wait(e, h * (LV + 1) + (l + 1))
                    held(e)
                    e.copy_predicated(acc[:, :].rearrange("p (n t) -> p n t", n=NB),
                                      view(lmask[:, l, :].bitcast(I32), [0, NB], [1, P]),
                                      PS[:, l % 2, :].rearrange("p (n t) -> p n t", n=NB))\
                        .then_inc(s_p.sem, 1)
                diff(0)
                for l in range(LV):
                    if l + 1 < LV:
                        diff(l + 1)
                    s_e.wait(e, h * LV + (l + 1))
                    e.tensor_tensor(ql[:, l % 2, :], tile(qk, h * 2), E[:, l % 2, :], ALU.mult)\
                        .then_inc(s_q.sem, 1)
                    if l:
                        pick(l - 1)
                e.drain()
                e.tensor_copy(ql[:, LV % 2, :], tile(qk, h * 2)).then_inc(s_q.sem, 1)
                e.tensor_tensor(dd[:, 0, :].rearrange("p (n t) -> p n t", n=NB),
                                view(b[:, P - 1:P], [P, NB], [0, P]),
                                b[:, :].rearrange("p (n t) -> p n t", n=NB), ALU.subtract)\
                    .then_inc(s_d.sem, 1)
                pick(LV - 1)
                s_el.wait(e, h + 1)
                e.tensor_tensor(qe[:, :], tile(qk, h * 2), E[:, 0, :], ALU.mult)
                e.tensor_tensor(dd[:, 1, :], tile(qk, h * 2 + 1), E[:, 1, :], ALU.mult)\
                    .then_inc(s_kd.sem, 1)
                e.drain()
                pick(LV)
                s_kv.wait(e, h + 1)
                e.tensor_copy(St[:, 0, :], PS[:, 2, 0:GDV])
                for n in range(1, NB - 1):
                    e.drain()
                    ins = e.scalar_tensor_tensor(
                        out=St[:, n, :], in0=St[:, n - 1, :], scalar=gs[:, 0, n:n + 1],
                        in1=PS[:, 2 + n // 2, (n % 2) * GDV:(n % 2 + 1) * GDV],
                        op0=ALU.mult, op1=ALU.add)
                ins.then_inc(s_st.sem, 1)
                s_or.wait(e, h + 1)
                e.reciprocal(gs[:, 2, :], gs[:, 2, :])
                e.drain()
                for n in range(NB):
                    ins = e.tensor_scalar(ot[:, n, :], PS[:, 4 + n // 2, (n % 2) * GDV:(n % 2 + 1) * GDV],
                                          gs[:, 2, n:n + 1], None, ALU.mult)
                ins.then_inc(s_on.sem, 1)
                s_ot.wait(e, h + 1)
                for j in range(2):
                    e.tensor_scalar(tile(qk, h * 2 + j), PS[:, 2 + j, :], cd("gla_n", h * 2 + j), None,
                                    ALU.mult).then_inc(s_oo.sem, 1)

        @on("pool")
        def _(e):
            with e.Fori(0, GH) as h:
                for l in range(LV):
                    s_e.wait(e, h * LV + (l + 1))
                    if l >= 2:
                        s_s.wait(e, h * (LV + 1) + (l - 1))
                    held(e)
                    e.tensor_tensor(kl[:, l % 2, :], tile(qk, h * 2 + 1), E[:, l % 2, :], ALU.mult)\
                        .then_inc(s_k.sem, 1)
                s_s.wait(e, h * (LV + 1) + LV - 1)
                held(e)
                e.tensor_copy(kl[:, LV % 2, :], tile(qk, h * 2 + 1)).then_inc(s_k.sem, 1)

        @on("act")
        def _(e):
            def gate(h, r):
                slot_done.wait(e, h * 8 + (nw + r + 1))
                e.activation(tile(wide, h * 8 + r), PS[:, 6 + r % 2, :], ACT.Copy)\
                    .then_inc(evac_act.sem, 1)

            with e.Fori(0, GH) as h:
                for l in range(LV):
                    s_d.wait(e, h * (LV + 1) + (l + 1))
                    if l >= 2:
                        s_q.wait(e, h * (LV + 1) + (l - 1))
                        s_k.wait(e, h * (LV + 1) + (l - 1))
                    e.activation(E[:, l % 2, :], dd[:, l % 2, :], ACT.Abs)
                    e.drain()
                    e.activation(E[:, l % 2, :], E[:, l % 2, :], ACT.Exp, scale=-1.0)\
                        .then_inc(s_e.sem, 1)
                    gate(h, l)
                s_d.wait(e, h * (LV + 1) + (LV + 1))
                s_q.wait(e, h * (LV + 1) + LV)
                s_k.wait(e, h * (LV + 1) + LV)
                e.activation(E[:, 0, :], b[:, :], ACT.Exp)
                e.activation(E[:, 1, :], dd[:, 0, :], ACT.Exp)
                e.activation(gs[:, 0, :], view(b[:, P - 1:P], [P, NB]), ACT.Exp).then_inc(s_el.sem, 1)
                s_kt.wait(e, h + 1)
                e.activation(kdT[:, :, :].rearrange("p n k -> p (n k)"), PS[:, 4, :], ACT.Copy)\
                    .then_inc(s_ko.sem, 1)
                gate(h, 7)
                s_o.wait(e, h + 1)
                for n in range(NB):
                    e.activation(ot[:, n, :], PS[:, 4 + n // 2, (n % 2) * GDV:(n % 2 + 1) * GDV],
                                 ACT.Square, accum_out=gs[:, 1, n:n + 1])
                e.drain()
                e.activation(gs[:, 2, :], gs[:, 1, :], ACT.Sqrt, scale=1.0 / GDV, bias=c_("eps"))\
                    .then_inc(s_or.sem, 1)
        barrier()
        gl.close()

        ds_ = ExitStack()
        tail.plan()
        OFF = [P, 0, 2 * P, 0]
        LB = [1, 2, 1, 0]
        LO = [0, P, 3 * P, 6 * P, 10 * P]
        OFF = [0, 0, P, 0]
        bias = sb(ds_, "bias_by_distance", [P, DH, S])
        qs = sb(ds_, "dq_static", [P, S])
        BS = sb(ds_, "bias_and_selection", [P, 10 * P])
        L = sb(ds_, "dsa_logits", [P, 10 * P])
        pT = sb(ds_, "dsa_probs_T", [P, 10, P])
        dst_ = sb(ds_, "dsa_stats", [P, 3, NB])
        staged = [x[:, j * S:(j + 1) * S] for x in (BS, L) for j in range(2)]
        staged += [pT[:, 4 * j:4 * j + 4, :].rearrange("p c k -> p (c k)") for j in range(2)]
        staged += [norm_sq[:, j, :] for j in range(2)]
        s_bias = sig("bias_tiles").by_dma()
        s_turn = sig("bias_turned")
        s_silu, s_og, s_sg = [sig("m2_" + x) for x in ("silu", "o_gated", "sigmoid")]
        (d_qs, d_bs, d_lg, d_l, d_nm, d_ex, d_nrm, d_tr, d_pt, d_pv, d_o, d_hi,
         d_lo) = [sig("dsa_" + x) for x in (
            "q", "bias", "logits", "summed", "max", "exp", "probs", "trans", "probsT", "pv", "out",
            "out_hi", "out_lo")]
        ng = START["gla_out"]
        y_base = evac_dve.plan(KT)

        @on("act")
        def _(e):
            for t in range(16, 16 + KT):
                e.activation(wide[:, t, :], wide[:, t, :], ACT.Silu).then_inc(s_silu.sem, 1)
            for h in range(DH):
                e.dma_start(staged[h], bass.AP(tensor=scratch.tensor, offset=h * 640,
                                               ap=[[1, P], [1, S]])).then_inc(s_bias.sem, 16)
            with e.Fori(0, 2) as i:
                for r in range(4):
                    h = i * 4 + r
                    d_nm.wait(e, h + 1)
                    for n in range(NB):
                        seg = L[:, LO[n]:LO[n + 1]]
                        ins = e.activation(seg, seg, ACT.Exp, bias=dst_[:, 0, n:n + 1],
                                           accum_out=dst_[:, 1, n:n + 1])
                    ins.then_inc(d_ex.sem, 1)
                    d_tr.wait(e, h + 1)
                    e.activation(pT[:, :, :].rearrange("p c k -> p (c k)"),
                                 view(PS[:, 4, 0:1], [1, 10 * P]), ACT.Copy).then_inc(d_pt.sem, 1)
                    for t in (h, h + KT):
                        e.activation(tile(wide, t), tile(wide, t), ACT.Sigmoid).then_inc(s_sg.sem, 1)
                    d_pv.wait(e, h + 1)
                    e.activation(tile(H, h), PS[:, 7, :], ACT.Copy).then_inc(d_o.sem, 1)
                    d_o.wait(e, h + 1)
                    e.activation(tile(att_hi, h), tile(H, h), ACT.Copy).then_inc(d_hi.sem, 1)
            tail.loop(e, tail.hi, START["dsa_out"], 2 * KT)

        def low(e, t):
            d_hi.wait(e, t + 1)
            held(e)
            e.tensor_tensor(tile(Hl, t), tile(H, t), tile(att_hi, t).bitcast(F32),
                            ALU.subtract).then_inc(d_lo.sem, 1)

        @on("pool")
        def _(e):
            def one(h):
                d_lg.wait(e, h)
                held(e)
                e.tensor_copy(qs[:, :], tile(wide, h + 24)).then_inc(d_qs.sem, 1)
                s_turn.wait(e, DH)
                d_l.wait(e, h)
                held(e)
                for n in range(NB):
                    ins = e.tensor_tensor(BS[:, LO[n]:LO[n + 1]],
                                          bias[:, bass.ds(h, 1), 384 - n * P:512]
                                          .rearrange("p a s -> p (a s)"),
                                          sel[:, n, 0:(n + 1) * P], ALU.add)
                ins.then_inc(d_bs.sem, 1)
            one(0)
            with e.Fori(1, DH) as h:
                one(h)
                low(e, h - 1)
            low(e, KT - 1)

        @on("pe")
        def _(e):
            with e.Fori(0, 2) as i:
                for r in range(4):
                    h = i * 4 + r
                    d_qs.wait(e, h + 1)
                    d_l.wait(e, h)
                    for n in range(NB):
                        mm = e.matmul(PS[:, LB[n], OFF[n]:OFF[n] + (n + 1) * P],
                                      qs[:, n * P:(n + 1) * P], ckvT[:, 0:(n + 1) * P],
                                      start=True, stop=True)
                    mm.then_inc(d_lg.sem, 1)
                    w = tiles_of(use_slot(e, ng, i, 4, r))
                    if r == 0:
                        s_og.wait(e, KT)
                    evac_dve.wait(e, h + y_base)
                    for k in range(KT):
                        mm = e.matmul(PS[:, 3, :], w[:, k, :], qk[:, k, :], start=k == 0,
                                      stop=k == KT - 1)
                    mm.then_inc(slot_done.sem, 1)
                    d_nrm.wait(e, h + 1)
                    c = 0
                    for n in range(NB):
                        for kb in range(n + 1):
                            mm = e.transpose(view(PS[:, 4, c * P:c * P + 1], [1, P]) if c < 4 else
                                             PS[:, 4 + c // 4, (c % 4) * P:(c % 4 + 1) * P],
                                             L[:, c * P:(c + 1) * P], ident)
                            c += 1
                    mm.then_inc(d_tr.sem, 1)
                    d_pt.wait(e, h + 1)
                    d_o.wait(e, h)
                    c = 0
                    for n in range(NB):
                        for kb in range(n + 1):
                            mm = e.matmul(PS[:, 7, n * P:(n + 1) * P], ckv[:, kb, :], pT[:, c, :],
                                          start=kb == 0, stop=kb == n)
                            c += 1
                    mm.then_inc(d_pv.sem, 1)

        @on("dve")
        def _(e):
            for t in range(KT):
                s_silu.wait(e, t + 1)
                e.tensor_tensor(qk[:, t, :], qk[:, t, :], wide[:, t + 16, :], ALU.mult)\
                    .then_inc(s_og.sem, 1)
            s_bias.wait(e, 16 * DH)
            for h in range(DH):
                e.tensor_copy(bias[:, h, :], view(staged[h][:, S - 1:S], [-1, S]))\
                    .then_inc(s_turn.sem, 1)
            e.drain()
            with e.Fori(0, 2) as i:
                for r in range(4):
                    h = i * 4 + r
                    d_lg.wait(e, h + 1)
                    d_bs.wait(e, h + 1)
                    d_tr.wait(e, h)
                    for n in range(NB):
                        ins = e.scalar_tensor_tensor(
                            out=L[:, LO[n]:LO[n + 1]], in0=PS[:, LB[n], OFF[n]:OFF[n] + (n + 1) * P],
                            scalar=P ** -0.5, in1=BS[:, LO[n]:LO[n + 1]], op0=ALU.mult, op1=ALU.add)
                    ins.then_inc(d_l.sem, 1)
                    e.drain()
                    for n in range(NB):
                        ins = e.tensor_reduce(dst_[:, 0, n:n + 1], L[:, LO[n]:LO[n + 1]], AX.X,
                                              ALU.max, negate=True)
                    ins.then_inc(d_nm.sem, 1)
                    e.drain()
                    d_ex.wait(e, h + 1)
                    e.reciprocal(dst_[:, 2, :], dst_[:, 1, :])
                    e.drain()
                    for n in range(NB):
                        seg = L[:, LO[n]:LO[n + 1]]
                        ins = e.tensor_scalar(seg, seg, dst_[:, 2, n:n + 1], None, ALU.mult)
                    ins.then_inc(d_nrm.sem, 1)
                    slot_done.wait(e, i * 4 + (ng + r + 1))
                    s_sg.wait(e, h * 2 + 2)
                    e.tensor_tensor(tile(wide, h), PS[:, 3, :], tile(wide, h), ALU.mult)\
                        .then_inc(evac_dve.sem, 1)

        tail.lows(START["dsa_out"], 2 * KT)
        pe_gemm("dsa_out", KT, lambda k: (att_hi[:, k, :], Hl[:, k, :]), (d_lo, 0), free=evac_dve,
                split=tail)
        merged = evac_dve.n

        def merge(e, t, bank):
            e.tensor_tensor(tile(wide, t + KT), bank, tile(wide, t + KT), ALU.mult)
            e.drain()
            e.tensor_tensor(tile(wide, t), tile(wide, t + KT), tile(wide, t), ALU.add)
            e.drain()
            e.tensor_copy(tile(merged_hi, t), tile(wide, t))
            e.drain()
            return e.tensor_tensor(tile(merged_lo, t), tile(wide, t), tile(merged_hi, t).bitcast(F32),
                                   ALU.subtract)
        evacuate("dve", "dsa_out", KT, merge, evac_dve)
        pe_gemm("mix_out", KT, lambda k: (merged_hi[:, k, :], merged_lo[:, k, :]),
                (evac_dve, merged), free=evac_dve, split=tail)
        added = evac_dve.n
        evac_add("mix_out", KT)
        norm_root(ready=(evac_dve, added))
        barrier()
        ds_.close()
        m.close()

    def ple():
        m = ExitStack()
        pT_ = sb(m, "p_T", [P, 2, S])
        pp = sb(m, "p_projected", [P, KT, S])
        gt = sb(m, "ple_gate", [P, KT, S])
        s_pin, s_pp, s_pl = sig("ple_in").by_dma(), sig("ple_proj"), sig("ple_out")
        on("act")(lambda e: e.dma_start(pT_[:, :, :], a["pT"].rearrange("(k p) s -> p k s", p=P))
                  .then_inc(s_pin.sem, 16))
        npj, npg = START["ple_proj"], START["ple_gate"]
        low = sb(m, "ple_x_lo", [P, KT, S], F32R)
        normed = sb(m, "ple_normed", [P, 4, S])
        split = Split(m, "ple_slots", npg, KT)
        split.lows(npg, KT)

        @on("pe")
        def _(e):
            s_pin.wait(e, 16)
            for j in range(2):
                w = use_slot(e, npj, 0, 4, j).rearrange("p (t k c) -> p t k c", t=4, k=2)
                for t in range(4):
                    if j == 1 and t == 3:
                        s_pp.wait(e, 1)
                    for k in range(2):
                        mm = e.matmul(PS[:, (4 * j + t) % 7, :], w[:, t, k, :], pT_[:, k, :],
                                      start=k == 0, stop=k == 1)
                mm.then_inc(slot_done.sem, 1)

        @on("act")
        def _(e):
            for t in range(KT):
                slot_done.wait(e, npj + t // 4 + 1)
                e.activation(pp[:, t, :], PS[:, t % 7, :], ACT.Copy).then_inc(s_pp.sem, 1)
        split_first = 2
        on("act")(lambda e: [split.hi(e, 0, 4, npg + r) for r in range(split_first)])
        b_h = norm_apply("ple_n", split=(Hh, low, normed))
        on("pe")(lambda e: s_pp.wait(e, KT))
        pe_gemm("ple_gate", KT, lambda k: (Hh[:, k, :], low[:, k, :]), (s_h, b_h), split=split)
        g0 = evac_act.n
        evacuate("act", "ple_gate", KT, lambda e, t, bank: e.activation(tile(gt, t), bank, ACT.Sigmoid),
                 evac_act, split=split)
        s_pl.plan(KT)

        @on("dve")
        def _(e):
            e.drain()
            for t in range(KT):
                evac_act.wait(e, g0 + t + 1)
                e.tensor_tensor(gt[:, t, :], gt[:, t, :], pp[:, t, :], ALU.mult)
                e.drain()
                e.tensor_tensor(X[:, t, :], X[:, t, :], gt[:, t, :], ALU.add).then_inc(s_pl.sem, 1)
        norm_root(ready=(s_pl, 0))
        norm_apply("final2")
        m.close()

    phases = [mixer1, peer, lambda: ffn(1), mixer2, lambda: ffn(2), ple]
    if start:
        skip_constants()
        norm_root()
    for n, f in enumerate(phases):
        if n >= start:
            f()
        if n + 1 == stop:
            return finish(phase.n)
    finish()


def tiles(w, K=KT):
    n = w.shape[1] // P
    return w.reshape(K, P, n, P).transpose(2, 1, 0, 3).reshape(n, P, K * P)


def columns(v):
    return v.reshape(-1, P).T


def stream_parts(i):
    w_in = i["w_in"][0]
    val, gate, q, k, v, gates = (w_in[:, s:e] for s, e in (
        (0, 1024), (1024, 2048), (2048, 3072), (3072, 3200), (3200, 3328), (3328, 5376)))
    yield "glu", np.stack([tiles(gate), tiles(val)], 1).reshape(16, P, D)
    yield "q", tiles(q)
    yield "kv", tiles(np.concatenate([k[:, :64], k[:, :64], k[:, 64:], k[:, 64:], v], 1))
    yield "gates", tiles(gates)
    yield "attn_o", tiles(i["w_attn_o"][0])
    yield "conv_out", tiles(i["w_conv_out"][0])
    yield "w_out", tiles(i["w_out"][0])
    u = i["peer_u"][0].reshape(NKEY, NKEY, KT, P).transpose(1, 3, 2, 0).reshape(NKEY, P, D)
    pq = tiles(i["w_peer_q"][0]).reshape(PH, 2, P, D)
    yield "peer_q_u0", np.concatenate([pq, u[:JQ].reshape(PH, 2, P, D)], 1).reshape(32, P, D)
    v = i["peer_v"][0].reshape(NKEY, NQ, JQ // 2, 2, 2, D // 2).transpose(1, 4, 2, 0, 3, 5)
    for q_ in range(NQ):
        if q_:
            yield f"u{q_}", u[q_ * JQ:(q_ + 1) * JQ]
        yield f"v{q_}", v[q_].reshape(JQ, P, D)


def stream_parts2(i):
    for n in (1, 2):
        w = i[f"ffn{n}_w_in_2"][0]
        yield f"f{n}_in", np.stack([tiles(w[:, :FT * P]), tiles(w[:, FT * P:])], 1).reshape(-1, P, D)
        yield f"f{n}_out", i[f"ffn{n}_w_out_2"][0].reshape(FT, P, D)
    w = i["mix_w_in_2"][0]
    at = np.cumsum([0, 512, 512, 1024, 1024, 16, 1024, 128, 512, 64, 8, 2048])
    gq, gk, gv, gr, ga, dq, dkv, iq, ik, iw, gates = (w[:, s:e] for s, e in zip(at[:-1], at[1:]))
    yield "misc", tiles(np.concatenate([ga, iw, np.zeros((D, P - 24), np.float32)], 1))
    yield "ik", tiles(np.concatenate([ik, ik], 1))
    yield "iq", tiles(iq)
    yield "dkv", tiles(dkv)
    yield "gqk", np.stack([tiles(gq), tiles(gk)], 1).reshape(8, P, D)
    yield "gv", gv.reshape(4, 2, P, 2, 512).transpose(3, 0, 2, 1, 4).reshape(8, P, D)
    yield "wide2", tiles(np.concatenate([gates, gr, dq], 1))
    yield "gla_out", tiles(i["gla_w_out_2"][0])
    yield "dsa_out", tiles(i["dsa_w_out_2"][0])
    yield "mix_out", tiles(i["mix_w_out_2"][0])
    yield "ple_proj", i["ple_w_proj_2"][0].reshape(2, P, 2, 4, P).transpose(2, 1, 3, 0, 4).reshape(2, P, D)
    yield "ple_gate", tiles(i["ple_w_gate_2"][0])


def level_masks():
    s_, t_ = np.arange(P)[:, None], np.arange(P)[None]
    m_ = [(s_ // (2 * h) == t_ // (2 * h)) & (s_ % (2 * h) < h) & (t_ % (2 * h) >= h)
          for h in (64 >> l for l in range(7))]
    return np.stack(m_ + [s_ == t_], 1).astype(np.float32)


def bucket_rows():
    dist = np.maximum(np.arange(640) - (P - 1), 0)
    large = 16 + (np.log(np.maximum(dist, 1) / 16.0) / np.log(8.0) * 16).astype(np.int32)
    bucket = np.where(dist < 16, dist, np.minimum(large, 31))
    return (np.arange(32)[:, None] == bucket[None]).astype(np.float32)


def lay_out(i):
    stream = np.zeros((SLOTS, P, D), np.float32)
    for name, part in [*stream_parts(i), *stream_parts2(i)]:
        stream[START[name]:START[name] + len(part)] = part
    b = i["b_in"][0]
    d = np.arange(P)
    rot = np.zeros((P, P), np.float32)
    for m_ in range(P):
        if m_ % 64 < 32:
            rot[m_ + 32, m_] = -1.0
        else:
            rot[m_ - 32, m_] = 1.0
    squares = np.concatenate([np.eye(P), np.full((P, P), 1.0 / D), rot,
                              np.broadcast_to(d, (P, P))], 1).astype(np.float32)
    inv = (10000.0 ** (-(np.arange(32) * 2.0 / HD))).astype(np.float32)
    one = np.ones((P, 1), np.float32)
    cols = {
        "norm1": columns(i["norm1_g"]),
        "b_glu": np.stack([columns(b[1024:2048]), columns(b[:1024])], 2).reshape(P, 16),
        "b_q": columns(b[2048:3072]),
        "b_k": columns(np.concatenate([b[3072:3136], b[3072:3136], b[3136:3200], b[3136:3200]])),
        "b_gates": columns(b[3328:5376]),
        "conv_w": i["conv_w"][0].reshape(TAPS, KT, P).transpose(2, 0, 1).reshape(P, -1),
        "conv_b": columns(i["conv_b"]), "ln_g": columns(i["conv_ln_g"]),
        "ln_b": columns(i["conv_ln_b"]), "norm2": columns(i["norm2_g"]),
        "final1": columns(i["final_g"]), "ffn1_n": columns(i["ffn1_norm_2"]),
        "mix_n": columns(i["mix_norm_2"]), "alpha_b": columns(i["gla_alpha_b_2"]),
        "gla_n": columns(i["gla_out_norm_2"]), "ckv_n": columns(i["ckv_norm_2"]),
        "ffn2_n": columns(i["ffn2_norm_2"]), "ple_n": columns(i["ple_norm_2"]),
        "final2": columns(i["final_norm_2"]), "inv_freq": inv[d % 32][:, None],
        "eps": EPS * one, "half_pi": np.float32(np.pi / 2) * one, "one": one, "zero": 0 * one,
    }
    q, k = np.arange(P)[:, None], np.arange(2 * P)[None]
    rel = q + P - k
    band = (rel >= 0) & (rel < P)
    band = np.stack([band & ((k >= P) | (n > 0)) for n in range(NB)], 1)
    return {
        "alpha_w": i["gla_alpha_w_2"][0], "level_mask": level_masks(),
        "causal": np.where(np.arange(P)[None] <= np.arange(P)[:, None], 0.0, NEG).astype(np.float32),
        "buckets": bucket_rows(), "rel_bias": i["rel_bias_2"], "pT": i["p_2"][0, 0].T,
        "keysT": i["peer_sub_keys"][0].reshape(2 * PH, NKEY, P).transpose(2, 0, 1),
        "xT": i["x"][0].T, "stream": stream,
        "cols": np.concatenate([cols[n] for n, _ in COLS], 1).astype(np.float32),
        "squares": squares, "band_mask": np.where(band, 0.0, NEG).astype(np.float32),
        "positions": i["positions"][0], "sinks": i["attn_sinks"][0], "b_v": b[3200:3328],
    }


def kernel(**inputs):
    import concourse.bacc as bacc
    from concourse.bass_utils import run_bass_kernel_spmd
    arrays = {k: np.ascontiguousarray(v) for k, v in
              lay_out({k: np.asarray(v) for k, v in inputs.items()}).items()}
    nc = bacc.Bacc("TRN2", target_bir_lowering=False, num_devices=1)
    a = {n: nc.dram_tensor("in_" + n, v.shape, mybir.dt.from_np(v.dtype), kind="ExternalInput").ap()
         for n, v in arrays.items()}
    out = nc.dram_tensor("out", (D, S), F32, kind="ExternalOutput").ap()
    build(nc, a, out)
    r = run_bass_kernel_spmd(nc, [{"in_" + n: v for n, v in arrays.items()}], core_ids=[0])
    return np.ascontiguousarray(r.results[0]["out"].T)[None]
```
